# Optimizing a Trainium2 kernel written in Bass

```python
import math
import jax, jax.numpy as jnp
from jax import lax
import numpy as np

D_MODEL = 1024
BATCH = 1
SEQ = 512
DEPTH = 2

CHUNK = 64
N_EVEN = (DEPTH + 1) // 2
N_ODD = DEPTH // 2
RMS_EPS = 1e-6
NEG_INF = -1e30
MIX_WIDTH = D_MODEL

A_HEADS = 8
A_HEAD_DIM = 64
A_WIDTH = A_HEADS * A_HEAD_DIM
A_LEFT_CHUNKS = 8
A_BAND = (A_LEFT_CHUNKS + 1) * CHUNK
A_REL_CLIP = 256

B_HEADS = 8
B_HEAD_DIM = 64
B_WIDTH = B_HEADS * B_HEAD_DIM
B_GROUPS = 2
B_HEADS_PER_GROUP = B_HEADS // B_GROUPS
B_STATE = 128
B_CONV = 4
B_CONV_CH = B_WIDTH + 2 * B_GROUPS * B_STATE
B_NORM_EPS = 1e-5

C_HEADS = 8
C_HEAD_DIM = 64
C_WIDTH = C_HEADS * C_HEAD_DIM
C_DECAY_RANK = 64
C_AAA_RANK = 64
C_GATE_RANK = 128
C_IN = 3 * C_WIDTH + C_DECAY_RANK + C_AAA_RANK + C_GATE_RANK
C_GN_EPS = 64e-5

D_HEADS = 8
D_NOPE = 64
D_ROPE = 32
D_VDIM = 64
D_WIDTH = D_HEADS * D_VDIM
D_Q_RANK = 384
D_KV_RANK = 256
ROPE_THETA = 10000.0
Q_BLOCK = 128

IN_EVEN = 3 * A_WIDTH + B_WIDTH + B_CONV_CH + B_HEADS
IN_ODD = C_IN + D_Q_RANK + D_KV_RANK + D_ROPE

FF_DENSE = 2816
N_EXPERTS = 8
TOP_K = 2
FF_EXPERT = 3584
MOE_BLOCK = 128
MAX_START_CHUNK = 256

kernel_name = "hybrid_chunked_attn_ssd_rwkv7_mla_moe"

F32 = jnp.float32

def rmsnorm(x, w, eps=RMS_EPS):
    xf = x.astype(F32)
    y = xf * lax.rsqrt(jnp.mean(xf * xf, axis=-1, keepdims=True) + eps)
    return (y * w.astype(F32)).astype(x.dtype)

def split_cols(p, sizes):
    idx = [int(i) for i in np.cumsum(sizes)[:-1]]
    return jnp.split(p, idx, axis=-1)

def swiglu(h, w_gate, w_up, w_down):
    return (jax.nn.silu(h @ w_gate) * (h @ w_up)) @ w_down

def causal_depthwise_conv(u, w, bias):
    width, ch = w.shape
    y = lax.conv_general_dilated(u, w[:, None, :], window_strides=(1,),
                                 padding=[(width - 1, 0)],
                                 dimension_numbers=("NWC", "WIO", "NWC"),
                                 feature_group_count=ch)
    return y + bias

def rope(u, positions):
    half = u.shape[-1] // 2
    inv = ROPE_THETA ** (-jnp.arange(half, dtype=F32) / half)
    ang = positions.astype(F32)[:, :, None] * inv
    cos, sin = jnp.cos(ang)[:, :, None, :], jnp.sin(ang)[:, :, None, :]
    u1, u2 = u[..., :half].astype(F32), u[..., half:].astype(F32)
    return jnp.concatenate([u1 * cos - u2 * sin, u1 * sin + u2 * cos], axis=-1).astype(u.dtype)

def chunk_band_attention(q, k, v, rel_table):
    b, L, H, dh = q.shape
    nc = L // CHUNK
    qc = q.reshape(b, nc, CHUNK, H, dh)
    pad = ((0, 0), (A_LEFT_CHUNKS, 0), (0, 0), (0, 0), (0, 0))
    kc = jnp.pad(k.reshape(b, nc, CHUNK, H, dh), pad)
    vc = jnp.pad(v.reshape(b, nc, CHUNK, H, dh), pad)
    band_idx = jnp.arange(nc)[:, None] + jnp.arange(A_LEFT_CHUNKS + 1)[None, :]
    kb = kc[:, band_idx].reshape(b, nc, A_BAND, H, dh)
    vb = vc[:, band_idx].reshape(b, nc, A_BAND, H, dh)
    rel = jnp.arange(CHUNK)[:, None] + A_LEFT_CHUNKS * CHUNK - jnp.arange(A_BAND)[None, :]
    bias = rel_table[:, jnp.clip(rel, -A_REL_CLIP, A_REL_CLIP) + A_REL_CLIP]
    valid = jnp.repeat(band_idx >= A_LEFT_CHUNKS, CHUNK, axis=1)
    s = jnp.einsum("bcqhd,bckhd->bchqk", qc, kb).astype(F32) * (dh ** -0.5) + bias.astype(F32)
    s = jnp.where(valid[None, :, None, None, :], s, NEG_INF)
    p = jax.nn.softmax(s, axis=-1).astype(v.dtype)
    o = jnp.einsum("bchqk,bckhd->bcqhd", p, vb)
    return o.reshape(b, L, H * dh)

def mamba2_ssd(z, xbc, dt_raw, conv_w, conv_b, dt_bias, a_log, d_skip, norm_w):
    b, L, _ = z.shape
    nc = L // CHUNK
    G, R, P, N = B_GROUPS, B_HEADS_PER_GROUP, B_HEAD_DIM, B_STATE
    xbc = jax.nn.silu(causal_depthwise_conv(xbc, conv_w, conv_b)).astype(F32)
    xs, bm, cm = split_cols(xbc, [B_WIDTH, G * N, G * N])
    x = xs.reshape(b, nc, CHUNK, G, R, P)
    bm = bm.reshape(b, nc, CHUNK, G, N)
    cm = cm.reshape(b, nc, CHUNK, G, N)
    dt = jax.nn.softplus(dt_raw.astype(F32) + dt_bias.astype(F32)).reshape(b, nc, CHUNK, G, R)
    a = dt * (-jnp.exp(a_log.astype(F32))).reshape(G, R)
    a_cum = jnp.cumsum(jnp.moveaxis(a, 2, -1), axis=-1)
    xdt = x * dt[..., None]
    causal = jnp.tril(jnp.ones((CHUNK, CHUNK), bool))
    seg = a_cum[..., :, None] - a_cum[..., None, :]
    l_mat = jnp.exp(jnp.where(causal, seg, -jnp.inf))
    cb = jnp.einsum("bclgn,bcsgn->bcgls", cm, bm)
    y_diag = jnp.einsum("bcgls,bcgrls,bcsgrp->bclgrp", cb, l_mat, xdt)
    decay_to_end = jnp.exp(a_cum[..., -1:] - a_cum)
    states = jnp.einsum("bclgn,bcgrl,bclgrp->bcgrpn", bm, decay_to_end, xdt)
    chunk_decay = jnp.exp(a_cum[..., -1])

    def carry_state(h, inp):
        st, dec = inp
        return h * dec[..., None, None] + st, h

    h0 = jnp.zeros((b, G, R, P, N), F32)
    _, h_prev = lax.scan(carry_state, h0, (jnp.moveaxis(states, 1, 0), jnp.moveaxis(chunk_decay, 1, 0)))
    h_prev = jnp.moveaxis(h_prev, 0, 1)
    y_off = jnp.einsum("bclgn,bcgrpn,bcgrl->bclgrp", cm, h_prev, jnp.exp(a_cum))
    y = y_diag + y_off + x * d_skip.astype(F32).reshape(G, R, 1)
    y = y.reshape(b, L, B_WIDTH) * jax.nn.silu(z.astype(F32))
    yg = y.reshape(b, L, G, B_WIDTH // G)
    yg = yg * lax.rsqrt(jnp.mean(yg * yg, axis=-1, keepdims=True) + B_NORM_EPS)
    return (yg.reshape(b, L, B_WIDTH) * norm_w.astype(F32)).astype(z.dtype)

def rwkv7_time_mix(pc, mu, w0, w2, a0, a2, g2, k_k, k_a, r_k, ln_w, ln_b):
    b, L, _ = pc.shape
    H, N = C_HEADS, C_HEAD_DIM
    prev = jnp.pad(pc, ((0, 0), (1, 0), (0, 0)))[:, :-1]
    mixed = pc + (prev - pc) * mu
    r, k, v, wd, ad, gd = split_cols(mixed, [C_WIDTH] * 3 + [C_DECAY_RANK, C_AAA_RANK, C_GATE_RANK])
    w_log = -jax.nn.softplus(-(w0 + jnp.tanh(wd) @ w2).astype(F32)) - 0.5
    decay = jnp.exp(-jnp.exp(w_log))
    a = jax.nn.sigmoid((a0 + ad @ a2).astype(F32))
    g = (jax.nn.sigmoid(gd) @ g2).astype(F32)
    heads = lambda u: u.astype(F32).reshape(b, L, H, N)
    r, k, v, decay, a = heads(r), heads(k), heads(v), heads(decay), heads(a)
    kk = k * k_k.astype(F32).reshape(H, N)
    kk = kk / jnp.maximum(jnp.sqrt(jnp.sum(kk * kk, axis=-1, keepdims=True)), 1e-12)
    k = k * (1.0 + (a - 1.0) * k_a.astype(F32).reshape(H, N))

    def step(S, inp):
        r_t, w_t, k_t, v_t, kk_t, a_t = inp
        sa = jnp.einsum("bhvk,bhk->bhv", S, -kk_t)
        S = S * w_t[:, :, None, :] + sa[..., None] * (kk_t * a_t)[:, :, None, :] + v_t[..., None] * k_t[:, :, None, :]
        return S, jnp.einsum("bhvk,bhk->bhv", S, r_t)

    tm = lambda u: jnp.swapaxes(u, 0, 1)
    S0 = jnp.zeros((b, H, N, N), F32)
    _, y = lax.scan(step, S0, (tm(r), tm(decay), tm(k), tm(v), tm(kk), tm(a)))
    y = tm(y)
    mean = jnp.mean(y, axis=-1, keepdims=True)
    var = jnp.mean((y - mean) ** 2, axis=-1, keepdims=True)
    y = ((y - mean) * lax.rsqrt(var + C_GN_EPS)).reshape(b, L, C_WIDTH)
    y = y * ln_w.astype(F32) + ln_b.astype(F32)
    bonus = jnp.sum(r * k * r_k.astype(F32), axis=-1, keepdims=True) * v
    y = (y + bonus.reshape(b, L, C_WIDTH)) * g
    return y.astype(pc.dtype)

def latent_attention(q_down, kv_down, k_rope, positions, q_norm, w_uq, kv_norm, w_ukv):
    b, L, _ = q_down.shape
    q = (rmsnorm(q_down, q_norm) @ w_uq).reshape(b, L, D_HEADS, D_NOPE + D_ROPE)
    kv = (rmsnorm(kv_down, kv_norm) @ w_ukv).reshape(b, L, D_HEADS, D_NOPE + D_VDIM)
    q_nope, q_pe = q[..., :D_NOPE], rope(q[..., D_NOPE:], positions)
    k_nope, v = kv[..., :D_NOPE], kv[..., D_NOPE:]
    k_pe = rope(k_rope[:, :, None, :], positions)[:, :, 0]
    scale = (D_NOPE + D_ROPE) ** -0.5
    nqb = L // Q_BLOCK
    to_blocks = lambda u: jnp.swapaxes(u.reshape(b, nqb, Q_BLOCK, *u.shape[2:]), 0, 1)
    key_chunk = jnp.arange(L) // CHUNK

    def attend(args):
        qn, qp, blk = args
        s = jnp.einsum("bqhd,bkhd->bhqk", qn, k_nope) + jnp.einsum("bqhd,bkd->bhqk", qp, k_pe)
        s = s.astype(F32) * scale
        q_chunk = (blk * Q_BLOCK + jnp.arange(Q_BLOCK)) // CHUNK
        s = jnp.where(key_chunk[None, :] <= q_chunk[:, None], s, NEG_INF)
        p = jax.nn.softmax(s, axis=-1).astype(v.dtype)
        return jnp.einsum("bhqk,bkhd->bqhd", p, v)

    o = lax.map(attend, (to_blocks(q_nope), to_blocks(q_pe), jnp.arange(nqb)))
    return jnp.swapaxes(o, 0, 1).reshape(b, L, D_WIDTH)

def moe_swiglu(h, router, w_gate, w_up, w_down):
    b, L, d = h.shape
    t = h.reshape(-1, d)
    n = t.shape[0]
    n_assign = n * TOP_K
    logits = (t @ router).astype(F32)
    top_v, top_i = lax.top_k(logits, TOP_K)
    gates = jax.nn.softmax(top_v, axis=-1)
    e_flat = top_i.reshape(-1)
    g_flat = gates.reshape(-1)
    tok_flat = jnp.arange(n_assign, dtype=jnp.int32) // TOP_K
    order = jnp.argsort(e_flat)
    e_s, tok_s, g_s = e_flat[order], tok_flat[order], g_flat[order]
    counts = jnp.bincount(e_flat, length=N_EXPERTS)
    start = jnp.cumsum(counts) - counts
    padded = (counts + MOE_BLOCK - 1) // MOE_BLOCK * MOE_BLOCK
    pad_end = jnp.cumsum(padded)
    pad_start = pad_end - padded
    dest = pad_start[e_s] + (jnp.arange(n_assign) - start[e_s])
    n_slots = n_assign + N_EXPERTS * MOE_BLOCK
    n_blocks = n_slots // MOE_BLOCK
    slot_tok = jnp.zeros((n_slots,), jnp.int32).at[dest].set(tok_s)
    slot_g = jnp.zeros((n_slots,), F32).at[dest].set(g_s)
    block_e = jnp.minimum(jnp.searchsorted(pad_end, jnp.arange(n_blocks) * MOE_BLOCK, side="right"), N_EXPERTS - 1)

    def run_block(args):
        tok, e = args
        return swiglu(t[tok], w_gate[e], w_up[e], w_down[e])

    out = lax.map(run_block, (slot_tok.reshape(n_blocks, MOE_BLOCK), block_e))
    out = out.reshape(n_slots, d) * slot_g[:, None].astype(t.dtype)
    y = jnp.zeros_like(t).at[slot_tok].add(out)
    return y.reshape(b, L, d)

def even_layer(x, norm_mix, w_in, rel_bias, conv_w, conv_b, dt_bias, a_log, d_skip, ssm_norm,
               w_out, norm_ffn, w_gate, w_up, w_down):
    b, L, _ = x.shape
    h = rmsnorm(x, norm_mix)
    q, k, v, z, xbc, dt = split_cols(h @ w_in, [A_WIDTH] * 3 + [B_WIDTH, B_CONV_CH, B_HEADS])
    shp = (b, L, A_HEADS, A_HEAD_DIM)
    y_a = chunk_band_attention(q.reshape(shp), k.reshape(shp), v.reshape(shp), rel_bias)
    y_b = mamba2_ssd(z, xbc, dt, conv_w, conv_b, dt_bias, a_log, d_skip, ssm_norm)
    x = x + jnp.concatenate([y_a, y_b], axis=-1) @ w_out
    return x + swiglu(rmsnorm(x, norm_ffn), w_gate, w_up, w_down)

def odd_layer(x, positions, norm_mix, w_in, mu, w0, w2, a0, a2, g2, k_k, k_a, r_k, ln_w, ln_b,
              q_norm, w_uq, kv_norm, w_ukv, w_out, norm_ffn, router, e_gate, e_up, e_down):
    h = rmsnorm(x, norm_mix)
    pc, q_down, kv_down, k_rope = split_cols(h @ w_in, [C_IN, D_Q_RANK, D_KV_RANK, D_ROPE])
    y_c = rwkv7_time_mix(pc, mu, w0, w2, a0, a2, g2, k_k, k_a, r_k, ln_w, ln_b)
    y_d = latent_attention(q_down, kv_down, k_rope, positions, q_norm, w_uq, kv_norm, w_ukv)
    x = x + jnp.concatenate([y_c, y_d], axis=-1) @ w_out
    return x + moe_swiglu(rmsnorm(x, norm_ffn), router, e_gate, e_up, e_down)

def setup_inputs(seed: int = 0) -> dict:
    key = jax.random.key(seed)
    ks = iter(jax.random.split(key, 64))

    def nrm(shape, scale):
        return jax.random.normal(next(ks), shape, F32) * scale

    def gain(shape):
        return 1.0 + nrm(shape, 0.02)

    def unif(shape, lo, hi):
        return jax.random.uniform(next(ks), shape, F32, lo, hi)

    PE, PO, D = N_EVEN, N_ODD, D_MODEL
    x = nrm((BATCH, SEQ, D), 1.0)
    offsets = jax.random.randint(next(ks), (BATCH, 1), 0, MAX_START_CHUNK) * CHUNK
    positions = (offsets + jnp.arange(SEQ, dtype=jnp.int32)[None, :]).astype(jnp.int32)
    dt_init = jnp.exp(unif((PE, B_HEADS), math.log(1e-3), math.log(1e-1)))
    return {
        "x": x,
        "positions": positions,
        "e_norm_mix": gain((PE, D)),
        "e_w_in": nrm((PE, D, IN_EVEN), D ** -0.5),
        "a_rel_bias": nrm((PE, A_HEADS, 2 * A_REL_CLIP + 1), 0.5),
        "b_conv_w": nrm((PE, B_CONV, B_CONV_CH), B_CONV ** -0.5),
        "b_conv_b": nrm((PE, B_CONV_CH), 0.02),
        "b_dt_bias": dt_init + jnp.log(-jnp.expm1(-dt_init)),
        "b_a_log": jnp.log(unif((PE, B_HEADS), 1.0, 16.0)),
        "b_d_skip": 1.0 + nrm((PE, B_HEADS), 0.1),
        "b_norm_w": gain((PE, B_WIDTH)),
        "e_w_out": nrm((PE, MIX_WIDTH, D), MIX_WIDTH ** -0.5),
        "e_norm_ffn": gain((PE, D)),
        "ff_w_gate": nrm((PE, D, FF_DENSE), D ** -0.5),
        "ff_w_up": nrm((PE, D, FF_DENSE), D ** -0.5),
        "ff_w_down": nrm((PE, FF_DENSE, D), FF_DENSE ** -0.5),
        "o_norm_mix": gain((PO, D)),
        "o_w_in": nrm((PO, D, IN_ODD), D ** -0.5),
        "c_mu": unif((PO, C_IN), 0.0, 1.0),
        "c_w0": unif((PO, C_WIDTH), -6.0, -1.0),
        "c_w2": nrm((PO, C_DECAY_RANK, C_WIDTH), 0.1),
        "c_a0": nrm((PO, C_WIDTH), 0.1),
        "c_a2": nrm((PO, C_AAA_RANK, C_WIDTH), 0.1),
        "c_g2": nrm((PO, C_GATE_RANK, C_WIDTH), C_GATE_RANK ** -0.5),
        "c_k_k": 0.85 + nrm((PO, C_WIDTH), 0.05),
        "c_k_a": 1.0 + nrm((PO, C_WIDTH), 0.05),
        "c_r_k": nrm((PO, C_HEADS, C_HEAD_DIM), 0.1),
        "c_ln_w": gain((PO, C_WIDTH)),
        "c_ln_b": nrm((PO, C_WIDTH), 0.02),
        "d_q_norm": gain((PO, D_Q_RANK)),
        "d_w_uq": nrm((PO, D_Q_RANK, D_HEADS * (D_NOPE + D_ROPE)), D_Q_RANK ** -0.5),
        "d_kv_norm": gain((PO, D_KV_RANK)),
        "d_w_ukv": nrm((PO, D_KV_RANK, D_HEADS * (D_NOPE + D_VDIM)), D_KV_RANK ** -0.5),
        "o_w_out": nrm((PO, MIX_WIDTH, D), MIX_WIDTH ** -0.5),
        "o_norm_ffn": gain((PO, D)),
        "moe_router": nrm((PO, D, N_EXPERTS), D ** -0.5),
        "moe_w_gate": nrm((PO, N_EXPERTS, D, FF_EXPERT), D ** -0.5),
        "moe_w_up": nrm((PO, N_EXPERTS, D, FF_EXPERT), D ** -0.5),
        "moe_w_down": nrm((PO, N_EXPERTS, FF_EXPERT, D), FF_EXPERT ** -0.5),
        "final_norm": gain((D,)),
    }

def reference(x, positions, e_norm_mix, e_w_in, a_rel_bias, b_conv_w, b_conv_b, b_dt_bias, b_a_log,
              b_d_skip, b_norm_w, e_w_out, e_norm_ffn, ff_w_gate, ff_w_up, ff_w_down,
              o_norm_mix, o_w_in, c_mu, c_w0, c_w2, c_a0, c_a2, c_g2, c_k_k, c_k_a, c_r_k,
              c_ln_w, c_ln_b, d_q_norm, d_w_uq, d_kv_norm, d_w_ukv, o_w_out, o_norm_ffn,
              moe_router, moe_w_gate, moe_w_up, moe_w_down, final_norm):
    for layer in range(DEPTH):
        i = layer // 2
        if layer % 2 == 0:
            x = even_layer(x, e_norm_mix[i], e_w_in[i], a_rel_bias[i], b_conv_w[i], b_conv_b[i],
                           b_dt_bias[i], b_a_log[i], b_d_skip[i], b_norm_w[i], e_w_out[i],
                           e_norm_ffn[i], ff_w_gate[i], ff_w_up[i], ff_w_down[i])
        else:
            x = odd_layer(x, positions, o_norm_mix[i], o_w_in[i], c_mu[i], c_w0[i], c_w2[i], c_a0[i],
                          c_a2[i], c_g2[i], c_k_k[i], c_k_a[i], c_r_k[i], c_ln_w[i], c_ln_b[i],
                          d_q_norm[i], d_w_uq[i], d_kv_norm[i], d_w_ukv[i], o_w_out[i],
                          o_norm_ffn[i], moe_router[i], moe_w_gate[i], moe_w_up[i], moe_w_down[i])
    return rmsnorm(x, final_norm)


_drawn_inputs = setup_inputs


def setup_inputs(seed=0):
    import zlib

    import numpy as np

    out = dict(_drawn_inputs(seed))
    spreads = {}
    factors = {'c_ln_w': 28.119,
     'c_ln_b': 29.508,
     'd_q_norm': 8.0,
     'd_kv_norm': 6.466,
     'final_norm': 7.441,
     'c_w2': 4.171,
     'c_a0': 4.283,
     'c_k_k': 3.691,
     'c_k_a': 3.372,
     'c_r_k': 2.889,
     'o_norm_ffn': 6.375}
    for name, (base, spread) in spreads.items():
        noise = np.random.default_rng([zlib.crc32(name.encode()), seed]).standard_normal(out[name].shape)
        drawn = base * np.exp(spread * noise) if base else spread * noise
        out[name] = __import__('jax').numpy.asarray(drawn.astype(out[name].dtype))
    for name, factor in factors.items():
        out[name] = (out[name] * factor).astype(out[name].dtype)
    return out
```

```python
import math
from contextlib import ExitStack

import concourse.bass as bass
from concourse import mybir

F32 = mybir.dt.float32
I32 = mybir.dt.int32
ALU = mybir.AluOpType
ACT = mybir.ActivationFunctionType
AX = mybir.AxisListType.X

P = 128
SEQ, D = 512, 1024
NT = SEQ // P
KT = D // P
CHUNK = 64
RMS_EPS = 1e-6
HEADS, HD = 8, 64
REL_CLIP = 256
A_COLS = 3 * HEADS * HD
B_WIDTH, B_STATE, B_GROUPS, B_CONV = 512, 128, 2, 4
B_CONV_CH = B_WIDTH + 2 * B_GROUPS * B_STATE
CONV_TILES = B_CONV_CH // P
DT_COL = A_COLS + B_WIDTH + B_CONV_CH
B_NORM_EPS = 1e-5
FF = 2816
FF_TILES = FF // P
C_WIDTH = 512
C_IN = 3 * C_WIDTH + 64 + 64 + 128
C_TILES = C_IN // P
C_GN_EPS = 64e-5
Q_RANK, KV_RANK, ROPE = 384, 256, 32
QKVR = Q_RANK + KV_RANK + ROPE
QD = HD + ROPE
MLA_SCALE = QD ** -0.5
ROPE_THETA = 10000.0
N_EXPERTS, TOP_K, FF_E = 8, 2, 3584
FE_TILES = FF_E // P
GROUPS_E = FE_TILES // 2
CAP = 168
CAP2 = CAP - P
MAX_ROUNDS = -(-SEQ // CAP)
MASKED = -1e30
DECAY_RATE = -math.exp(-0.5)
SLOTS = 7
SLOT = 2048
MAGIC = 1.5 * 2.0 ** 23
TWO_PI = (6.28125, 0.00193500518798828125, 3.0199159819e-07)


class Banks:

    def __init__(self, banks, start):
        self.banks, self.n, self.read = banks, 0, [start] * len(banks)

    def open(self, signal, count):
        i = self.n % len(self.banks)
        former, self.read[i] = self.read[i], (signal, count)
        self.n += 1
        return self.banks[i], former


class Steps:

    def __init__(self, eng, sem):
        self.eng, self.sem, self.n, self.turn, self.size = eng, sem, 0, None, 0

    def __call__(self, instruction):
        self.n += 1
        instruction.then_inc(self.sem, 1)
        value = self.n if self.turn is None else self.turn * self.size + self.n
        self.eng.wait_ge(self.sem, value)


COUNTS_ON = {
    "pc_full": ("conv_full", 8), "pc_stored": ("conv_stored", 8), "qkvr_full": ("v_full", 8), "qkvr_stored": ("v_stored", 8),
    "ycT_full": ("ynT_full", 4), "rkv_full": ("x_tok_full", 4), "lora_full": ("cb_full", 8), "cum_full": ("row_full", 16),
    "end_full": ("dt_col_full", 1), "ft_full": ("ssd_full", 8), "uq_full": ("z_full", 8), "ukv_full": ("qk_full", 8),
    "kpe_full": ("dt_full", 1), "rkv_ready": ("x_tok_ready", 4), "wa_sum": ("cb_ready", 8),
}


def total(name, count):
    return count + COUNTS_ON.get(name, (name, 0))[1]


def weight_order():
    w = [("e_in", c) for c in range(12)] + [("e_out", c) for c in range(4)]
    for c in range(FF_TILES // 2):
        w += [("ff_g", c), ("ff_u", c)]
    w += [("ff_d", half, c) for half in range(2) for c in range(6)]
    w += [("o_in", c) for c in range(10)]
    w += [("uq", 0), ("uq", 1), ("ukv", 0)]
    w += [("o_out", c) for c in range(4)]
    return w


def expert_order():
    w = [("g", 0), ("u", 0)]
    for j in range(1, GROUPS_E):
        w += [("g", j), ("u", j), ("d", j - 1)]
    return w + [("d", GROUPS_E - 1)]


def last_use(item):
    kind, c = item[0], item[-1]
    if kind == "e_in":
        name, per, first = [("qk_full", 2, 0), ("v_full", 4, 4), ("z_full", 4, 6), ("conv_full", 2, 8)][
            0 if c < 4 else 1 if c < 6 else 2 if c < 8 else 3]
        return name, per * (c - first + 1)
    if kind == "o_in":
        return ("pc_full", 2 * (c + 1)) if c < 7 else ("qkvr_full", 4 * (c - 6))
    if kind in ("e_out", "o_out"):
        return "mix_full", 4 * (c + 1) + (16 if kind == "o_out" else 0)
    if kind in ("ff_g", "ff_u"):
        return ("gate_full" if kind == "ff_g" else "up_full"), 2 * (c + 1)
    if kind == "ff_d":
        return ("down_used", 5 * item[1] + c + 1) if c < 5 else ("down_full", 4 * (item[1] + 1))
    return {"uq": ("uq_full", 4 * (c + 1)), "ukv": ("ukv_full", 12)}[kind]


class Ring:

    def __init__(self, slots, landed):
        self.slots, self.landed = slots, landed
        self.n, self.turn, self.size = 0, None, 0

    def start_loop(self, n, turn, size):
        assert size % SLOTS == 0
        self.n, self.turn, self.size = n, turn, size

    def load(self, eng, view, source):
        slot = self.n % SLOTS
        eng.dma_start(view(self.slots[slot]), source).then_inc(self.landed[slot], 16)
        self.n += 1

    def take(self):
        slot, value = self.n % SLOTS, 16 * (self.n // SLOTS + 1)
        if self.turn is not None:
            value = self.turn * (16 * self.size // SLOTS) + value
        self.n += 1
        return self.slots[slot], (self.landed[slot], value)


def hybrid_trunk(nc, x, positions, e_norm_mix, e_w_in, a_rel_bias, b_conv_w, b_conv_b, b_dt_bias,
                 b_a_log, b_d_skip, b_norm_w, e_w_out, e_norm_ffn, ff_w_gate, ff_w_up, ff_w_down,
                 o_norm_mix, o_w_in, c_mu, c_w0, c_w2, c_a0, c_a2, c_g2, c_k_k, c_k_a, c_r_k,
                 c_ln_w, c_ln_b, d_q_norm, d_w_uq, d_kv_norm, d_w_ukv, o_w_out, o_norm_ffn,
                 moe_router, moe_w_gate, moe_w_up, moe_w_down, final_norm, out, dbg=None, upto=99):
    ctx = ExitStack()
    with ctx:
        def sb(name, shape, dt=F32):
            return ctx.enter_context(nc.sbuf_tensor(name, shape, dt))

        sems, bank = {}, {}

        def sem(name):
            name = COUNTS_ON.get(name, (name,))[0]
            if name not in sems:
                sems[name] = ctx.enter_context(nc.semaphore(name))
            return sems[name]

        slots = [sb(f"slot{i}", [P, SLOT]) for i in range(SLOTS)]
        xs = sb("xs", [P, NT, D])
        ident = sb("ident", [P, P])
        flip = sb("flip", [P, P])
        chunk_mask = sb("chunk_mask", [P, P])
        causal_mask = sb("causal_mask", [P, P])
        cum_incl = sb("cum_incl", [P, P])
        cum_excl = sb("cum_excl", [P, P])
        cum_rev = sb("cum_rev", [P, P])
        chunk_sum = sb("chunk_sum", [P, 2])
        before = sb("before", [P, P])
        ones = sb("ones", [P, P])
        pair_mask = sb("pair_mask", [P, 2, CHUNK])
        level_mask = sb("level_mask", [P, 6, CHUNK])
        level_one = sb("level_one", [P, CHUNK])
        eye64 = sb("eye64", [P, CHUNK])
        slot_no = sb("slot_no", [P, CAP])
        vec_rows = sb("vec_rows", [P, P])
        vc = sb("vc", [P, 95])
        w_dt = sb("w_dt", [P, KT, HEADS])
        w_router = sb("w_router", [P, KT, N_EXPERTS])
        lora = sb("lora", [P, 2, C_WIDTH])
        small = sb("small", [P, 256])
        small_i = sb("small_i", [P, 16], I32)
        expert_lt = sb("expert_lt", [P, N_EXPERTS, N_EXPERTS])

        ARENA = 30600
        arena = sb("arena", [P, ARENA])

        def region(at, *shape, rows=P):
            n = math.prod(shape)
            assert at + n <= ARENA, (at, shape)
            v = arena[0:rows, at:at + n]
            if len(shape) == 2:
                v = v.rearrange("p (a b) -> p a b", b=shape[1])
            if len(shape) == 3:
                v = v.rearrange("p (a b c) -> p a b c", b=shape[1], c=shape[2])
            return v

        head_row = lora[0:HEADS, :, :].rearrange("p a b -> p (a b)").rearrange("p (a b) -> p a b", b=P)
        hT = region(0, KT, SEQ)
        xn = region(4096, NT, D)
        yT = region(4096, KT, SEQ)
        qT, kT = region(8192, 4, SEQ), region(10240, 4, SEQ)
        v_a, zs = region(12288, NT, C_WIDTH), region(14336, NT, B_WIDTH)
        bias_w = region(16384, HEADS, SEQ)
        conv_in = region(20480, CONV_TILES, SEQ + B_CONV - 1)
        conv_out = region(24600, CONV_TILES, SEQ)
        probs = region(28696, 3, SEQ)
        probsT = [region(2048 * i, NT, SEQ) for i in range(2)]
        bias_ext = region(24600, 640, rows=HEADS)
        x_tok, xdt = region(8192, NT, B_WIDTH), region(10240, NT, B_WIDTH)
        y_tok, cbT = region(12288, NT, B_WIDTH), region(16384, B_GROUPS, NT, SEQ)
        decay = [region(20480 + 2048 * i, NT, SEQ) for i in range(2)]
        wT = [region(24600 + 2048 * i, NT, SEQ) for i in range(2)]
        dt_row = [region(28696 + 512 * i, SEQ, rows=HEADS) for i in range(3)]
        sqd = region(0, D)
        hid = region(8192, FF_TILES, SEQ)
        sil = region(19456, 2, SEQ)
        BC = 27000
        bc = {n: region(BC + 512 * i, C_WIDTH) for i, n in enumerate(["w0", "a0", "k_k", "k_a", "r_k", "ln_w", "ln_b"])}
        pcT = region(8192, C_TILES, SEQ + 1)
        qkvr = region(15376, NT, QKVR)
        rw = 18064
        mixdiff = region(rw, 2, SEQ)
        free_rows = list(range(0, 4096, 512)) + list(range(6144, 8192, 512)) + list(range(rw, BC - 511, 512))
        R, F = {}, {}
        F["ar"] = arena[:, 0:1024].rearrange("p (a b c) -> p a b c", b=2, c=P)
        F["ab"] = arena[:, 1024:2048].rearrange("p (a b) -> p a b", b=P)
        F["ak"] = arena[:, 2048:3072].rearrange("p (a b) -> p a b", b=P)
        names = ["r", "k", "v", "sig", "a", "g", "kk", "b", "Eex", "Ein", "Eni", "Erev", "al", "rt", "bt", "kt", "bh", "kh", "tmp",
                 "btT", "ktT", "state"]
        for i, name in enumerate(names):
            R[name] = region(free_rows[6 + i], C_WIDTH)
        for name, former in (("X", "Eex"), ("XT", "Ein"), ("Y1", "Eni"), ("ot0", "Erev"), ("ot1", "r"), ("Z1", "rt"), ("U", "bt"),
                             ("SA", "kt"), ("y", "k"), ("A", "a")):
            R[name] = R[former]
        for name in ("btT", "ktT"):
            F[name] = R[name].rearrange("p (a b) -> p a b", b=P)
        F["wt"] = R["sig"].rearrange("p (a b) -> p a b", b=P)
        state = [R["state"][:, 256 * i:256 * (i + 1)].rearrange("p (a b) -> p a b", b=HD) for i in range(2)]

        q_tok = region(8192, NT, HEADS, QD)
        qT_d = region(18064, HEADS, SEQ, rows=QD)
        kT_d = region(22160, HEADS, SEQ, rows=QD)
        v_d = region(11264, NT, C_WIDTH)
        qnT, kvnT = region(26256, 3, SEQ), region(13312, 2, SEQ)
        rope_cs = region(14336, 16, 16)
        E0 = 8192
        pick = region(E0, NT, CAP)
        pick_g = region(E0 + 672, NT, CAP)
        pickT = region(E0 + 1344, 2, SEQ)
        xgT = region(E0 + 2368, KT, CAP)
        sil_e = region(E0 + 3712, 2, 2 * CAP)
        hid_e = region(E0 + 4384, 2, 2 * CAP)
        outT = region(E0 + 5056, KT, CAP)
        out_tok = region(E0 + 6400, 2, D)
        final_w = region(E0 + 8448, D)
        y_out = region(E0 + 9472, NT, D)
        M0 = E0 + 13568
        logit, ex, gate, place, rank, sel = [region(M0 + 32 * i, NT, N_EXPERTS) for i in range(6)]
        same, more = [region(M0 + 256 * (1 + i), NT, N_EXPERTS * N_EXPERTS).rearrange("p t (e j) -> p t e j", j=N_EXPERTS)
                      for i in range(2)]
        top = region(M0 + 1024, NT)
        ones_row, dt_keep = region(6144, SEQ, rows=HEADS), region(6656, SEQ, rows=HEADS)

        banks = [ctx.enter_context(nc.psum_tensor(f"bank{i}", [P, 512], F32)) for i in range(8)]
        turn_banks, acc = banks[0:4], banks[4:8]

        ext_d = nc.dram_tensor("bias_ext_d", [HEADS, 640], F32)

        def cols8(dram, lo, n):
            return dram[:, lo:lo + n].rearrange("(k p) n -> p k n", p=P)

        landed = [sem(f"landed{i}") for i in range(SLOTS)]

        block = ctx.enter_context(nc.Block())

        @block.sync
        def _(sp):
            w = Ring(slots, landed)
            xv = x[0].rearrange("(t p) d -> p t d", p=P)
            for t in range(NT):
                sp.dma_start(xs[:, t, :], xv[:, t, :]).then_inc(sem("x_loaded"), 16)
            row = 0
            for dram, n in ((e_norm_mix, 8), (e_norm_ffn, 8), (o_norm_mix, 8), (o_norm_ffn, 8), (b_conv_b, 8)):
                sp.dma_start(vec_rows[row:row + n, :], dram[0].rearrange("(k p) -> k p", p=P)).then_inc(sem("vec_loaded"), 16)
                row += n
            for tap in range(B_CONV):
                sp.dma_start(vec_rows[row:row + 8, :], b_conv_w[0, tap].rearrange("(k p) -> k p", p=P)).then_inc(sem("vec_loaded"), 16)
                row += 8
            for dram, n in ((c_mu, 14), (d_q_norm, 3), (d_kv_norm, 2), (b_norm_w, 4)):
                sp.dma_start(vec_rows[row:row + n, :], dram[0].rearrange("(k p) -> k p", p=P)).then_inc(sem("vec_loaded"), 16)
                row += n
            assert row == 95

            def load(kind, *c):
                if kind in ("e_in", "o_in", "e_out", "o_out", "ff_g", "ff_u"):
                    dram = {"e_in": e_w_in, "o_in": o_w_in, "e_out": e_w_out, "o_out": o_w_out,
                            "ff_g": ff_w_gate, "ff_u": ff_w_up}[kind]
                    n = min(256, dram.shape[2] - 256 * c[0])
                    w.load(sp, lambda s: s[:, 0:KT * n].rearrange("p (k n) -> p k n", n=n),
                           cols8(dram[0], 256 * c[0], n))
                elif kind == "ff_d":
                    half, j = c
                    n = min(4, FF_TILES - 4 * j)
                    w.load(sp, lambda s: s[:, 0:n * 512].rearrange("p (k n) -> p k n", n=512),
                           ff_w_down[0, 4 * j * P:(4 * j + n) * P, 512 * half:512 * half + 512]
                           .rearrange("(k p) n -> p k n", p=P))
                elif kind == "uq":
                    w.load(sp, lambda s: s[:, 0:3 * 384].rearrange("p (k n) -> p k n", n=384),
                           cols8(d_w_uq[0], 384 * c[0], 384))
                elif kind == "ukv":
                    w.load(sp, lambda s: s[:, :].rearrange("p (k n) -> p k n", n=1024),
                           cols8(d_w_ukv[0], 0, 1024))

            order = weight_order()
            last_item = {1: ("e_in", 11), 2: ("e_out", 3), 3: ("ff_d", 1, 5), 4: ("o_in", 9)}.get(upto)
            for n, item in enumerate(order):
                if item == ("ff_d", 0, 0):
                    sp.wait_ge(sem("mix_full"), 16)
                    sp.dma_start(lora[0:64, 0, :], c_w2[0]).then_inc(sem("lora_loaded"), 16)
                    sp.dma_start(lora[64:128, 0, :], c_a2[0]).then_inc(sem("lora_loaded"), 16)
                    sp.dma_start(lora[:, 1, :], c_g2[0]).then_inc(sem("lora_loaded"), 16)
                    for i, dram in enumerate((c_w0, c_a0, c_k_k, c_k_a, None, c_ln_w, c_ln_b)):
                        src = dram[0:1, :] if dram is not None else c_r_k[0:1].rearrange("a h d -> a (h d)")
                        sp.dma_start(region(BC + 512 * i, C_WIDTH), src.to_broadcast([P, C_WIDTH])).then_inc(sem("bc_loaded"), 16)
                if n >= SLOTS:
                    name, count = last_use(order[n - SLOTS])
                    sp.wait_ge(sem(name), total(name, count))
                load(*item)
                if item == last_item:
                    break
            w_n = w.n
            if upto >= 6:
                sp.wait_ge(sem("mix_full"), 32)
                sp.dma_start(final_w, final_norm.rearrange("(a n) -> a n", a=1).to_broadcast([P, D])).then_inc(sem("final_loaded"), 16)
                sp.wait_ge(sem("rounds_ready"), 1)
                rounds = sp.value_load(small_i[0:1, 8:9], min_val=1, max_val=MAX_ROUNDS)
                with sp.Fori(0, rounds) as r:
                    with sp.Fori(0, N_EXPERTS) as e:
                        turn = r * N_EXPERTS + e
                        w.start_loop(w_n, turn, 3 * GROUPS_E)
                        tiles = expert_order()
                        for n, (kind, j) in enumerate(tiles):
                            former, fj = tiles[n - SLOTS]
                            name, done = {"g": ("gate_full", 2 * FF_TILES // 2), "u": ("up_full", FF_TILES),
                                          "d": ("down_used", 10)}[former]
                            before_turn = 0 if n >= SLOTS else GROUPS_E
                            sp.wait_ge(sem(name), turn * GROUPS_E + (done + fj + 1 - before_turn))
                            if kind in ("g", "u"):
                                dram = moe_w_gate if kind == "g" else moe_w_up
                                w.load(sp, lambda s: s[:, :].rearrange("p (k n) -> p k n", n=256),
                                       dram[0, bass.ds(e, 1), :, 256 * j:256 * j + 256].rearrange("a (k p) n -> p (a k) n", p=P))
                            else:
                                w.load(sp, lambda s: s[:, :].rearrange("p (k n) -> p k n", n=D),
                                       moe_w_down[0, bass.ds(e, 1), 256 * j:256 * j + 256, :].rearrange("a (k p) n -> p (a k) n", p=P))
                sp.wait_ge(sem("y_ready"), NT)
                sp.dma_start(out[0].rearrange("(t p) d -> p t d", p=P), y_out).then_inc(sem("stored"), 16)
                sp.wait_ge(sem("stored"), 16)

        @block.gpsimd
        def _(pool):
            link = Steps(pool, sem("pool_step"))
            for k in range(KT):
                pool.dma_start(w_dt[:, k, :], e_w_in[0, k * P:(k + 1) * P, DT_COL:DT_COL + HEADS]).then_inc(sem("w_dt_loaded"), 16)
            pool.dma_start(w_router[:, :, :], moe_router[0].rearrange("(k p) e -> p k e", p=P)).then_inc(sem("router_loaded"), 16)
            pool.dma_start(small[0:HEADS, 0:1], b_dt_bias[0].rearrange("(h a) -> h a", a=1)).then_inc(sem("small_loaded"), 16)
            pool.dma_start(small[0:HEADS, 1:2], b_a_log[0].rearrange("(h a) -> h a", a=1)).then_inc(sem("small_loaded"), 16)
            pool.dma_start(small[:, 8:16], b_d_skip[0:1, :].to_broadcast([P, HEADS])).then_inc(sem("small_loaded"), 16)
            pool.dma_start(small_i[:, 0:NT], positions[0].rearrange("(t p) -> p t", p=P),
                           allow_slow_non_contiguous=True).then_inc(sem("small_loaded"), 16)

            pool.dma_start(bias_ext[:, 0:384], a_rel_bias[0, :, 129:513]).then_inc(sem("rel_loaded"), 16)
            pool.wait_ge(sem("rel_loaded"), 16)
            link(pool.tensor_copy(bias_ext[:, 384:640], bias_ext[:, 383:384].to_broadcast([HEADS, 256])))
            pool.dma_start(ext_d[:, :], bias_ext).then_inc(sem("rel_stored"), 16)
            pool.wait_ge(sem("rel_stored"), 16)
            for h in range(HEADS):
                src = bass.AP(ext_d, 640 * h, [[1, P], [1, SEQ]])
                pool.dma_start(bias_w[:, h, :], src).then_inc(sem("bias_loaded"), 16)

            def select(view, op, fill, base, pattern, mult):
                link(pool.affine_select(out=view, in_=view, compare_op=op, fill=fill, base=base,
                                        pattern=pattern, channel_multiplier=mult))

            link(pool.memset(ident[:, :], 0.0))
            select(ident[:, :], ALU.not_equal, 1.0, 0, [[-1, P]], 1)
            link(pool.memset(flip[:, :], 0.0))
            select(flip[:, :], ALU.not_equal, 1.0, -(P - 1), [[1, P]], 1)
            link(pool.memset(chunk_mask[:, :], 0.0))
            link(pool.memset(chunk_mask[0:CHUNK, CHUNK:P], MASKED))
            link(pool.memset(causal_mask[:, :], 0.0))
            select(causal_mask[:, :], ALU.is_ge, MASKED, 0, [[1, P]], -1)
            link(pool.memset(ones[:, :], 1.0))
            link(pool.memset(before[:, :], 1.0))
            select(before[:, :], ALU.is_gt, 0.0, 0, [[1, P]], -1)
            for m, op, sign in ((cum_incl, ALU.is_ge, 1), (cum_excl, ALU.is_gt, 1), (cum_rev, ALU.is_gt, -1)):
                link(pool.memset(m[:, :], DECAY_RATE))
                select(m[:, :], op, 0.0, 0, [[sign, P]], -sign)
                if sign > 0:
                    link(pool.memset(m[0:CHUNK, CHUNK:P], 0.0))
                else:
                    link(pool.memset(m[CHUNK:P, 0:CHUNK], 0.0))
            link(pool.memset(chunk_sum[:, :], 0.0))
            for c in range(2):
                link(pool.memset(chunk_sum[CHUNK * c:CHUNK * (c + 1), c:c + 1], DECAY_RATE))
            link(pool.memset(pair_mask[:, :, :], 1.0))
            link(pool.memset(level_mask[:, :, :], 1.0))
            link(pool.memset(level_one[:, :], 1.0))
            link(pool.memset(eye64[:, :], 0.0))
            for c in range(2):
                rows = slice(CHUNK * c, CHUNK * (c + 1))
                select(pair_mask[rows, 0, :], ALU.is_gt, 0.0, 0, [[1, CHUNK]], -1)
                select(pair_mask[rows, 1, :], ALU.is_ge, 0.0, 0, [[1, CHUNK]], -1)
                select(eye64[rows, :], ALU.not_equal, 1.0, 0, [[-1, CHUNK]], 1)
                v = level_one[rows, :].rearrange("p (b c) -> p b c", c=2)
                select(v, ALU.is_equal, 0.0, 0, [[-2, CHUNK // 2], [0, 2]], 1)
                link(pool.memset(v[:, :, 0:1], 0.0))
                for n in range(6):
                    s = 1 << n
                    v = level_mask[rows, n, :].rearrange("p (b c) -> p b c", c=2 * s)
                    link(pool.memset(v[:, :, s:2 * s], 0.0))
                    select(v, ALU.is_ge, 0.0, -s, [[-2 * s, CHUNK // (2 * s)], [0, 2 * s]], 1)
                    select(v, ALU.is_ge, 0.0, 2 * s - 1, [[2 * s, CHUNK // (2 * s)], [0, 2 * s]], -1)
            link(pool.iota(slot_no[:, :], [[1, CAP]], base=0, channel_multiplier=0, allow_small_or_imprecise_dtypes=True))
            link(pool.memset(expert_lt[:, :, :], 1.0))
            select(expert_lt[:, :, :], ALU.is_gt, 0.0, 0, [[1, N_EXPERTS], [-1, N_EXPERTS]], 0)
            link(pool.memset(head_row[:, :, :], 0.0))
            select(head_row[:, :, :], ALU.not_equal, 1.0, 0, [[-1, HEADS], [0, P]], 1)
            pool.memset(conv_in[:, :, 0:B_CONV - 1], 0.0).then_inc(sem("const_ready"), 1)


        @block.tensor
        def _(pe):
            w = Ring(slots, landed)
            turn_bank = Banks(turn_banks, (sem("const_ready"), 1))

            def tile(name, count):
                bank[name, count], former = turn_bank.open(sem(name), total(name, count))
                return bank[name, count], former

            def mm(o, lhsT, rhs, start):
                return pe.matmul(o, lhsT, rhs, start=start, stop=True, skip_group_check=True)

            def tp(o, i, rows=P):
                return pe.transpose(o, i, ident[0:rows, 0:rows])

            def norm(j):
                for t in range(NT):
                    pe.wait_ge(sem("xn_ready"), NT * j + t + 1)
                    for half in range(2):
                        b, former = tile("hT_ready", 8 * j + 2 * t + half + 1)
                        pe.wait_ge(*former)
                        for k in range(4):
                            m = tp(b[:, P * k:P * (k + 1)], xn[:, t, P * (4 * half + k):P * (4 * half + k + 1)])
                        m.then_inc(sem("xnT_full"), 1)
                pe.wait_ge(sem("hT_ready"), 8 * (j + 1))

            def by_feature(slab, cols, rhs, o, kt=KT, fresh=True):
                for k in range(kt):
                    m = mm(o, slab[:, k, cols], rhs[:, k, :], fresh and k == 0)
                return m

            def by_token(lhs, t, slab, o, kt=KT):
                for k in range(kt):
                    m = mm(o, lhs[:, k, P * t:P * (t + 1)], slab[:, k, :], k == 0)
                return m

            def slab_of(n=256, kt=KT):
                slot, here = w.take()
                return slot[:, 0:kt * n].rearrange("p (k n) -> p k n", n=n), here

            def attention(first, score, value, done):
                for i in range(HEADS * NT + 2):
                    if i < HEADS * NT:
                        b, former = tile("probs_ready", first + i + 1)
                        pe.wait_ge(*former)
                        score(b, i // NT, i % NT).then_inc(sem("scores_full"), 1)
                    u = i - 2
                    if u < 0:
                        continue
                    h, t = divmod(u, NT)
                    pe.wait_ge(sem("probs_scaled"), first + u + 1)
                    b, former = tile("probsT_ready", first + u + 1)
                    pe.wait_ge(*former)
                    for k in range(t + 1):
                        m = tp(b[:, P * k:P * (k + 1)], probs[:, u % 3, P * k:P * (k + 1)])
                    m.then_inc(sem("probsT_full"), 1)
                    if t == NT - 1:
                        pe.wait_ge(sem("probsT_ready"), first + u + 1)
                        pair = h // 2
                        if h % 2 == 0 and pair >= 2:
                            pe.wait_ge(sem("yT_ready"), done + pair - 1)
                        rows = slice(64 * (h % 2), 64 * (h % 2) + 64)
                        for k in range(NT):
                            m = mm(acc[pair % 2][rows, P * k:], value(h, k), probsT[h % 2][:, k, P * k:], k == 0)
                        m.then_inc(sem("pv_done"), 1)

            def out_proj(base):
                for c in range(4):
                    slab, here = slab_of()
                    pe.wait_ge(*here)
                    for t in range(NT):
                        b, former = tile("x_added", base + 4 * c + t + 1)
                        pe.wait_ge(*former)
                        by_token(yT, t, slab, b[:, 0:256]).then_inc(sem("mix_full"), 1)

            pe.wait_ge(sem("const_ready"), 1)
            pe.wait_ge(sem("vec_loaded"), 16 * 13)
            b, former = tile("vc_ready", 1)
            pe.wait_ge(*former)
            tp(b[:, 0:95], vec_rows[0:95, :], 95).then_inc(sem("vec_full"), 1)

            norm(0)
            for c in range(12):
                slab, here = slab_of()
                pe.wait_ge(*here)
                if c < 4 or c >= 8:
                    full, stored = ("qk_full", "qk_stored") if c < 4 else ("conv_full", "conv_stored")
                    for m in range(2):
                        b, former = tile(stored, 2 * (c % 8) + m + 1)
                        pe.wait_ge(*former)
                        by_feature(slab, slice(P * m, P * (m + 1)), hT, b[:, :]).then_inc(sem(full), 1)
                else:
                    full, stored = ("v_full", "v_stored") if c < 6 else ("z_full", "z_stored")
                    for t in range(NT):
                        b, former = tile(stored, 4 * (c % 2) + t + 1)
                        pe.wait_ge(*former)
                        by_token(hT, t, slab, b[:, 0:256]).then_inc(sem(full), 1)
            pe.wait_ge(sem("w_dt_loaded"), 16 * KT)
            b, former = tile("u_ready", 1)
            pe.wait_ge(*former)
            by_feature(w_dt, slice(0, HEADS), hT, b[0:HEADS, :]).then_inc(sem("dt_full"), 1)

            if upto >= 2:
                pe.wait_ge(sem("bias_loaded"), 16 * HEADS)
                pe.wait_ge(sem("qk_stored"), 8)
                pe.wait_ge(sem("v_stored"), 8)

                def score_a(b, h, t):
                    rows = slice(64 * (h % 2), 64 * (h % 2) + 64)
                    mm(b[:, 0:P * (t + 1)], qT[rows, h // 2, P * t:P * (t + 1)], kT[rows, h // 2, 0:P * (t + 1)], True)
                    for k in range(t + 1):
                        mm(b[:, P * k:P * (k + 1)], bias_w[:, h, P * (t - k):P * (t - k + 1)], flip[:, :], False)
                    return mm(b[:, P * t:P * (t + 1)], ident[:, :], chunk_mask[:, :], False)

                attention(0, score_a, lambda h, k: v_a[:, k, HD * h:HD * (h + 1)], 0)

                pe.wait_ge(sem("conv_ready"), CONV_TILES)
                for t in range(NT):
                    b, former = tile("x_tok_ready", t + 1)
                    pe.wait_ge(*former)
                    for c in range(4):
                        m = tp(b[:, P * c:P * (c + 1)], conv_out[:, c, P * t:P * (t + 1)])
                    m.then_inc(sem("x_tok_full"), 1)
                for g in range(B_GROUPS):
                    for j in range(NT):
                        b, former = tile("cb_ready", NT * g + j + 1)
                        pe.wait_ge(*former)
                        mm(b[:, P * j:], conv_out[:, 4 + g, P * j:P * (j + 1)], conv_out[:, 6 + g, P * j:], True)\
                            .then_inc(sem("cb_full"), 1)
                pe.wait_ge(sem("cum_ready"), 1)
                b, former = tile("dt_col_ready", 1)
                pe.wait_ge(*former)
                for j in range(NT):
                    tp(b[:, HEADS * j:HEADS * (j + 1)], dt_row[2][:, P * j:P * (j + 1)], HEADS)
                    m = tp(b[:, 32 + HEADS * j:32 + HEADS * (j + 1)], dt_row[0][:, P * j:P * (j + 1)], HEADS)
                m.then_inc(sem("dt_col_full"), 1)
                for h in range(HEADS + 1):
                    if h < HEADS:
                        for masked in range(2):
                            b, former = tile("decay_ready", 7 * h + (7 if masked else 5))
                            pe.wait_ge(*former)
                            m = mm(b[:, :], head_row[:, h, :], dt_row[1], True)
                            if masked:
                                for j in range(NT):
                                    m = mm(b[:, P * j:P * (j + 1)], ident[:, :], causal_mask[:, :], False)
                            m.then_inc(sem("row_full"), 1)
                    if h >= 1:
                        g = h - 1
                        pe.wait_ge(sem("w_ready"), NT * (g + 1))
                        b, former = tile("y_tok_ready", g + 1)
                        pe.wait_ge(*former)
                        for l in range(NT):
                            for j in range(l + 1):
                                m = mm(b[:, HD * l:HD * (l + 1)], wT[g % 2][:, j, P * l:P * (l + 1)],
                                       xdt[:, j, HD * g:HD * (g + 1)], l == 0)
                        m.then_inc(sem("ssd_full"), 1)
                for t in range(NT):
                    pe.wait_ge(sem("yn_ready"), 1)
                    b, former = tile("yT_b_ready", t + 1)
                    pe.wait_ge(*former)
                    for c in range(4):
                        m = tp(b[:, P * c:P * (c + 1)], y_tok[:, t, P * c:P * (c + 1)])
                    m.then_inc(sem("ynT_full"), 1)
                pe.wait_ge(sem("yT_ready"), 4)
                pe.wait_ge(sem("yT_b_ready"), 4)
                out_proj(0)

            if upto >= 3:
                norm(1)
                for c in range(FF_TILES // 2):
                    for full, stored in (("gate_full", "sil_ready"), ("up_full", "hid_ready")):
                        slab, here = slab_of()
                        pe.wait_ge(*here)
                        for m in range(2):
                            b, former = tile(stored, 2 * c + m + 1)
                            pe.wait_ge(*former)
                            by_feature(slab, slice(P * m, P * (m + 1)), hT, b[:, :]).then_inc(sem(full), 1)
                pe.wait_ge(sem("hid_ready"), FF_TILES)
                for half in range(2):
                    for c in range(6):
                        n = min(4, FF_TILES - 4 * c)
                        slab, here = slab_of(512, n)
                        pe.wait_ge(*here)
                        for k in range(n):
                            f = 4 * c + k
                            for t in range(NT):
                                if half and f == 0:
                                    pe.wait_ge(sem("x_added"), 16 + t + 1)
                                m = mm(acc[t][:, :], hid[:, f, P * t:P * (t + 1)], slab[:, k, :], f == 0)
                                if f == FF_TILES - 1:
                                    m.then_inc(sem("down_full"), 1)
                        if c < 5:
                            m.then_inc(sem("down_used"), 1)

            if upto >= 4:
                norm(2)
                for c in range(7):
                    slab, here = slab_of()
                    pe.wait_ge(*here)
                    for m in range(2):
                        b, former = tile("pc_stored", 2 * c + m + 1)
                        pe.wait_ge(*former)
                        by_feature(slab, slice(P * m, P * (m + 1)), hT, b[:, :]).then_inc(sem("pc_full"), 1)
                for c in range(3):
                    n = 256 if c < 2 else QKVR - 512
                    slab, here = slab_of(n)
                    pe.wait_ge(*here)
                    for t in range(NT):
                        b, former = tile("qkvr_stored", 4 * c + t + 1)
                        pe.wait_ge(*former)
                        by_token(hT, t, slab, b[:, 0:n]).then_inc(sem("qkvr_full"), 1)

                pe.wait_ge(sem("lora_loaded"), 48)
                quad = lambda c: slice(64 * c, 64 * c + 64)
                for t in range(NT):
                    now = slice(1 + P * t, 1 + P * (t + 1))
                    pe.wait_ge(sem("mixed"), C_TILES)
                    for a in range(3):
                        b, former = tile("rkv_ready", 3 * t + a + 1)
                        pe.wait_ge(*former)
                        for k in range(4):
                            m = tp(b[:, P * k:P * (k + 1)], pcT[:, 4 * a + k, now])
                        m.then_inc(sem("rkv_full"), 1)
                    pe.wait_ge(sem("lora_in_ready"), 2)
                    for a in range(2):
                        b, former = tile("wa_sum", 2 * t + a + 1)
                        pe.wait_ge(*former)
                        mm(b[:, :], pcT[quad(a), 12, now], lora[quad(a), 0, :], True).then_inc(sem("lora_full"), 1)
                    b, former = tile("g_ready", t + 1)
                    pe.wait_ge(*former)
                    mm(b[:, :], pcT[:, 13, now], lora[:, 1, :], True).then_inc(sem("lora_full"), 1)
                    pe.wait_ge(sem("sig_ready"), 2 * t + 1)
                    for i, tri in enumerate((cum_excl, cum_incl, cum_rev)):
                        b, former = tile("exp_ready", 4 * t + (1, 3, 4)[i])
                        pe.wait_ge(*former)
                        mm(b[:, :], tri[:, :], R["sig"], True).then_inc(sem("cum_full"), 1)
                    b, former = tile("end_ready", t + 1)
                    pe.wait_ge(*former)
                    for k in range(4):
                        m = mm(b[:, 2 * k:2 * k + 2], R["sig"][:, P * k:P * (k + 1)], chunk_sum[:, :], k == 0)
                    m.then_inc(sem("end_full"), 1)
                    for i, name in enumerate(("al", "rt", "bt", "kt")):
                        pe.wait_ge(sem("scaled_ready"), 6 * t + i + 1)
                        b, former = tile("ft_ready", 4 * t + i + 1)
                        pe.wait_ge(*former)
                        for k in range(4):
                            m = tp(b[:, P * k:P * (k + 1)], R[name][:, P * k:P * (k + 1)])
                        m.then_inc(sem("ft_full"), 1)
                    pe.wait_ge(sem("ft_ready"), 4 * (t + 1))
                    for i, lhs in enumerate(("btT", "ktT")):
                        for par in range(2):
                            b, former = tile("pm_ready", 6 * t + 2 * i + par + 1)
                            pe.wait_ge(*former)
                            for pair in range(4):
                                for c in range(2):
                                    m = mm(b[quad(c), P * pair:P * (pair + 1)], F[lhs][quad(par), pair, quad(c)],
                                           F["ar"][quad(par), pair, c, :], pair == 0)
                            m.then_inc(sem("pm_full"), 1)
                    for par in range(2):
                        b, former = tile("pm_ready", 6 * t + 5 + par)
                        pe.wait_ge(*former)
                        for pair in range(4):
                            for c in range(2):
                                m = mm(b[quad(c), HD * pair:HD * (pair + 1)], F["ar"][quad(par), pair, c, 0:CHUNK],
                                       F["btT"][quad(par), pair, quad(c)], pair == 0)
                        m.then_inc(sem("pm_full"), 1)

                    def each(b, lhs, rhs):
                        for h in range(HEADS):
                            for c in range(2):
                                m = mm(b[quad(c), HD * h:HD * (h + 1)], lhs(h, c), rhs(h, c), h == 0)
                        return m

                    def at(name):
                        return lambda h, c: R[name][quad(c), HD * h:HD * (h + 1)]

                    for n in range(5):
                        if n == 0:
                            pe.wait_ge(sem("inv_ready"), t + 1)
                        else:
                            pe.wait_ge(sem("dx_used"), 9 * t + 2 * n)
                        b, former = tile("y1_ready", 5 * t + n + 1)
                        pe.wait_ge(*former)
                        each(b, at(f"ot{n % 2}"), at("X")).then_inc(sem("y1_full"), 1)
                        pe.wait_ge(sem("y1_ready"), 5 * t + n + 1)
                        b, former = tile("dx_used", 9 * t + 2 * n + 1)
                        pe.wait_ge(*former)
                        each(b, at("XT"), at("Y1")).then_inc(sem("dx_full"), 1)
                        if n < 4:
                            b, former = tile("dx_used", 9 * t + 2 * n + 2)
                            pe.wait_ge(*former)
                            each(b, at("Y1"), at("XT")).then_inc(sem("dx_full"), 1)
                    b, former = tile("z_ready", 4 * t + 1)
                    pe.wait_ge(*former)
                    each(b, lambda h, c: F["ak"][quad(c), h, 0:CHUNK], at("v")).then_inc(sem("zu_full"), 1)
                    pe.wait_ge(sem("dx_used"), 9 * t + 9)
                    pe.wait_ge(sem("z_ready"), 4 * t + 1)
                    b, former = tile("z_ready", 4 * t + 2)
                    pe.wait_ge(*former)
                    each(b, at("X"), at("Z1")).then_inc(sem("zu_full"), 1)
                    for c in range(2):
                        b, former = tile("z_ready", 4 * t + 3 + c)
                        pe.wait_ge(*former)
                        for h in range(HEADS):
                            m = mm(b[quad(h % 2), CHUNK * (h // 2):CHUNK * (h // 2 + 1)], at("al")(h, c), at("X")(h, c), h < 2)
                        m.then_inc(sem("zu_full"), 1)
                    pe.wait_ge(sem("z_ready"), 4 * t + 4)
                    pe.wait_ge(sem("scaled_ready"), 6 * t + 6)
                    for c in range(2):
                        n = 2 * t + c
                        S = state[n % 2]
                        pe.wait_ge(sem("state_ready"), n + 1)
                        for par in range(2):
                            b, former = tile("y_stored", 2 * n + par + 1)
                            pe.wait_ge(*former)
                            for pair in range(4):
                                mm(b[quad(c), HD * pair:HD * (pair + 1)], F["wt"][quad(par), pair, quad(c)],
                                   S[quad(par), pair, :], pair == 0)
                            for pair in range(4):
                                m = mm(b[quad(c), 256 + HD * pair:256 + HD * (pair + 1)], F["ar"][quad(par), pair, c, CHUNK:],
                                       S[quad(par), pair, :], False)
                            m.then_inc(sem("sa_full"), 1)
                        by, former = tile("y_added", n + 1)
                        pe.wait_ge(*former)
                        bs, former = tile("state_ready", n + 2)
                        pe.wait_ge(*former)
                        for h in range(HEADS):
                            mm(bs[quad(h % 2), HD * (h // 2):HD * (h // 2 + 1)], at("kh")(h, c), at("v")(h, c), h < 2)
                        for h in range(HEADS):
                            mm(by[quad(c), HD * h:HD * (h + 1)], F["ak"][quad(c), h, CHUNK:], at("v")(h, c), h == 0)
                        pe.wait_ge(sem("sa_ready"), 2 * n + 2)
                        for h in range(HEADS):
                            m = mm(bs[quad(h % 2), HD * (h // 2):HD * (h // 2 + 1)], at("bh")(h, c), at("SA")(h, c), False)
                        m.then_inc(sem("state_full"), 1)
                        for h in range(HEADS):
                            m = mm(by[quad(c), HD * h:HD * (h + 1)], F["ab"][quad(c), h, CHUNK:], at("SA")(h, c), False)
                        m.then_inc(sem("yc_full"), 1)
                    pe.wait_ge(sem("yc_ready"), t + 1)
                    b, former = tile("ycT_ready", t + 1)
                    pe.wait_ge(*former)
                    for k in range(4):
                        m = tp(b[:, P * k:P * (k + 1)], R["y"][:, P * k:P * (k + 1)])
                    m.then_inc(sem("ycT_full"), 1)

            if upto >= 5:
                for t in range(NT):
                    pe.wait_ge(sem("qkvn_ready"), t + 1)
                    for i, (lo, n) in enumerate(((0, 3), (Q_RANK, 2))):
                        b, former = tile("qnT_ready", 2 * t + i + 1)
                        pe.wait_ge(*former)
                        for k in range(n):
                            m = tp(b[:, P * k:P * (k + 1)], qkvr[:, t, lo + P * k:lo + P * (k + 1)])
                        m.then_inc(sem("qnT_full"), 1)
                pe.wait_ge(sem("qnT_ready"), 8)
                for half in range(2):
                    slab, here = slab_of(384, 3)
                    pe.wait_ge(*here)
                    for t in range(NT):
                        b, former = tile("q_stored", 4 * half + t + 1)
                        pe.wait_ge(*former)
                        by_token(qnT, t, slab, b[:, 0:384], 3).then_inc(sem("uq_full"), 1)
                slab, here = slab_of(1024, 2)
                pe.wait_ge(*here)
                for h in range(HEADS):
                    b, former = tile("kn_stored", h + 1)
                    pe.wait_ge(*former)
                    by_feature(slab, slice(P * h, P * h + HD), kvnT, b[0:HD, :], 2).then_inc(sem("ukv_full"), 1)
                vals = slab.rearrange("p k (h n) -> p k h n", n=P)[:, :, :, HD:P]
                for t in range(NT):
                    b, former = tile("v_d_stored", t + 1)
                    pe.wait_ge(*former)
                    by_token(kvnT, t, vals, b[:, :].rearrange("p (h n) -> p h n", n=HD), 2).then_inc(sem("ukv_full"), 1)
                pe.wait_ge(sem("rope_ready"), 2)
                b, former = tile("kpe_ready", 1)
                pe.wait_ge(*former)
                for t in range(NT):
                    m = tp(b[0:QD, P * t:P * (t + 1)], qkvr[:, t, QKVR - QD:QKVR])
                m.then_inc(sem("kpe_full"), 1)
                for h in range(HEADS):
                    b, former = tile("qT_ready", h + 1)
                    pe.wait_ge(*former)
                    for t in range(NT):
                        m = tp(b[0:QD, P * t:P * (t + 1)], q_tok[:, t, h, :])
                    m.then_inc(sem("qT_full"), 1)
                pe.wait_ge(sem("qT_ready"), HEADS)
                pe.wait_ge(sem("kpe_ready"), 1)
                pe.wait_ge(sem("kn_stored"), HEADS)
                pe.wait_ge(sem("v_d_stored"), NT)

                def score_d(b, h, t):
                    mm(b[:, 0:P * (t + 1)], qT_d[:, h, P * t:P * (t + 1)], kT_d[:, h, 0:P * (t + 1)], True)
                    return mm(b[:, P * t:P * (t + 1)], ident[:, :], chunk_mask[:, :], False)

                attention(HEADS * NT, score_d, lambda h, k: v_d[:, k, HD * h:HD * (h + 1)], 4)
                pe.wait_ge(sem("yT_ready"), 8)
                pe.wait_ge(sem("ycT_ready"), NT)
                out_proj(24)

            if upto >= 6:
                norm(3)
                pe.wait_ge(sem("router_loaded"), 16)
                b, former = tile("logit_ready", 1)
                pe.wait_ge(*former)
                for t in range(NT):
                    for k in range(KT):
                        m = mm(b[:, 8 * t:8 * t + 8], hT[:, k, P * t:P * (t + 1)], w_router[:, k, :], t == 0 and k == 0)
                m.then_inc(sem("logit_full"), 1)
                pe.wait_ge(sem("sel_ready"), 1)
                b, former = tile("place_ready", 1)
                pe.wait_ge(*former)
                for t in range(NT + 1):
                    for s in range(min(t + 1, NT)):
                        m = mm(b[:, 8 * t:8 * t + 8], (before if s == t else ones)[:, :], sel[:, s, :], t == 0)
                m.then_inc(sem("place_full"), 1)
                pe.wait_ge(sem("place_ready"), 1)
                pe.wait_ge(sem("rounds_ready"), 1)
                w_n = w.n
                rounds = pe.value_load(small_i[0:1, 8:9], min_val=1, max_val=MAX_ROUNDS)
                with pe.Fori(0, rounds) as r:
                    with pe.Fori(0, N_EXPERTS) as e:
                        turn = r * N_EXPERTS + e
                        w.start_loop(w_n, turn, 3 * GROUPS_E)
                        ebank = Banks(turn_banks, (sem("place_ready"), 1))

                        def etile(name, per, first, count):
                            return ebank.open(sem(name), turn * per + (first + count))

                        pe.wait_ge(sem("pick_ready"), turn * 2 + 1)
                        for i in range(3):
                            b, former = etile("xg_ready", 3, 0, i + 1)
                            pe.wait_ge(*former)
                            for d in range(3 * i, min(3 * i + 3, KT)):
                                for t in range(NT):
                                    m = mm(b[:, CAP * (d % 3):CAP * (d % 3 + 1)], xn[:, t, P * d:P * (d + 1)], pick[:, t, :],
                                           d % 3 == 0 and t == 0)
                            m.then_inc(sem("xg_full"), 1)
                        pe.wait_ge(sem("pick_ready"), turn * 2 + 2)
                        b, former = etile("pickT_ready", 2, 0, 1)
                        pe.wait_ge(*former)
                        for t in range(NT):
                            m = tp(b[:, P * t:P * (t + 1)], pick_g[:, t, 0:P])
                        m.then_inc(sem("pickT_full"), 1)
                        for t in range(NT):
                            m = tp(acc[3][0:CAP2, P * t:P * (t + 1)], pick_g[:, t, P:CAP])
                        m.then_inc(sem("pickT_full"), 1)
                        pe.wait_ge(sem("xg_ready"), turn * 3 + 3)

                        def up(j):
                            for full, stored, first in (("gate_full", "sil_ready", FF_TILES), ("up_full", "hid_ready", FF_TILES)):
                                slab, here = slab_of()
                                pe.wait_ge(*here)
                                b, former = etile(stored, GROUPS_E, first, j + 1)
                                pe.wait_ge(*former)
                                for m in range(2):
                                    last = by_feature(slab, slice(P * m, P * (m + 1)), xgT, b[:, CAP * m:CAP * (m + 1)],
                                                      fresh=m == 0)
                                last.then_inc(sem(full), 1)

                        def down(j):
                            slab, here = slab_of(D, 2)
                            pe.wait_ge(*here)
                            pe.wait_ge(sem("hid_ready"), turn * GROUPS_E + (FF_TILES + j + 1))
                            for k in range(2):
                                for d in range(KT):
                                    m = mm(acc[d // 3][:, CAP * (d % 3):CAP * (d % 3 + 1)], slab[:, k, P * d:P * (d + 1)],
                                           hid_e[:, j % 2, CAP * k:CAP * (k + 1)], j == 0 and k == 0 and d % 3 == 0)
                            m.then_inc(sem("down_used"), 1)

                        up(0)
                        for j in range(1, GROUPS_E):
                            up(j)
                            down(j - 1)
                        down(GROUPS_E - 1)
                        pe.wait_ge(sem("outT_ready"), turn * 3 + 3)
                        halves = []
                        for i in range(4):
                            b, former = etile("out_tok_ready", 4, 0, i + 1)
                            pe.wait_ge(*former)
                            halves.append(b)
                        for rows, lo in ((P, 0), (CAP2, P)):
                            for half in range(2):
                                b = halves[half + (0 if rows == P else 2)]
                                for d in range(4 * half, 4 * half + 4):
                                    m = tp(b[0:rows, P * (d % 4):P * (d % 4 + 1)], outT[:, d, lo:lo + rows])
                                m.then_inc(sem("out_tok_full"), 1)
                        pe.wait_ge(sem("pickT_ready"), turn * 2 + 2)
                        pe.wait_ge(sem("out_tok_ready"), turn * 4 + 4)
                        for t in range(NT):
                            for half in range(2):
                                b, former = etile("moe_added", 8, 0, 2 * t + half + 1)
                                pe.wait_ge(*former)
                                cols = slice(512 * half, 512 * half + 512)
                                mm(b[:, :], pickT[:, 0, P * t:P * (t + 1)], out_tok[:, 0, cols], True)
                                mm(b[:, :], pickT[0:CAP2, 1, P * t:P * (t + 1)], out_tok[0:CAP2, 1, cols], False)\
                                    .then_inc(sem("scatter_full"), 1)
                        pe.wait_ge(sem("moe_added"), turn * 8 + 8)
                        assert ebank.n % 4 == 0

        @block.scalar
        def _(act):
            step = Steps(act, sem("act_step"))

            def norm(j):
                for t in range(NT):
                    if j == 0:
                        act.wait_ge(sem("x_loaded"), 16 * NT)
                    elif j < 4:
                        act.wait_ge(sem("x_added"), (None, 12, 20, 36)[j] + t + 1)
                    step(act.activation(sqd, xs[:, t, :], ACT.Square, accum_out=small[:, 32 + t:33 + t]))
                act.activation(small[:, 32:36], small[:, 32:36], ACT.Copy, scale=1.0 / D).then_inc(sem("ss_ready"), 1)
                act.wait_ge(sem("ms_ready"), j + 1)
                act.activation(small[:, 40:44], small[:, 36:40], ACT.Sqrt).then_inc(sem("rstd_ready"), 1)

            def attention(first, done):
                def outputs(pair):
                    act.wait_ge(sem("pv_done"), 2 * done + 2 * (pair + 1))
                    act.activation(yT[:, done + pair, :], acc[pair % 2][:, :], ACT.Copy).then_inc(sem("yT_ready"), 1)

                for u in range(HEADS * NT):
                    if u >= 10 and (u - 10) % 8 == 0:
                        outputs((u - 10) // 8)
                    t = u % NT
                    n = P * (t + 1)
                    act.wait_ge(sem("max_ready"), first + u + 1)
                    if first or u >= 3:
                        act.wait_ge(sem("probsT_full"), first + u - 2)
                    b = bank["probs_ready", first + u + 1]
                    act.activation(probs[:, u % 3, 0:n], b[:, 0:n], ACT.Exp, bias=small[:, 48 + u % 4:49 + u % 4],
                                   accum_out=small[:, 52 + u % 4:53 + u % 4]).then_inc(sem("probs_ready"), 1)
                outputs(3)

            norm(0)
            for c in range(8):
                act.wait_ge(sem("qk_full"), c + 1)
                act.activation((qT if c < 4 else kT)[:, c % 4, :], bank["qk_stored", c + 1][:, :], ACT.Copy,
                               scale=HD ** -0.5 if c < 4 else 1.0).then_inc(sem("qk_stored"), 1)
            for i in range(8):
                act.wait_ge(sem("z_full"), i + 1)
                act.activation(zs[:, i % 4, 256 * (i // 4):256 * (i // 4) + 256], bank["z_stored", i + 1][:, 0:256], ACT.Silu)\
                    .then_inc(sem("z_stored"), 1)
            act.wait_ge(sem("const_ready"), 1)
            for c in range(CONV_TILES):
                act.wait_ge(sem("conv_full"), c + 1)
                act.activation(conv_in[:, c, B_CONV - 1:], bank["conv_stored", c + 1][:, :], ACT.Copy).then_inc(sem("conv_stored"), 1)
            act.wait_ge(sem("small_loaded"), 64)
            act.wait_ge(sem("dt_full"), 1)
            act.activation(dt_row[0], bank["u_ready", 1][0:HEADS, :], ACT.Identity, bias=small[0:HEADS, 0:1]).then_inc(sem("u_ready"), 1)
            act.activation(small[0:HEADS, 2:3], small[0:HEADS, 1:2], ACT.Exp)
            act.wait_ge(sem("abs_ready"), 1)
            step(act.activation(dt_row[1], dt_row[1], ACT.Exp, scale=-1.0))
            act.activation(dt_row[1], dt_row[1], ACT.Ln, bias=1.0).then_inc(sem("ln_ready"), 1)
            for c in range(CONV_TILES):
                act.wait_ge(sem("conv_sum"), c + 1)
                act.activation(conv_out[:, c, :], conv_out[:, c, :], ACT.Silu).then_inc(sem("conv_ready"), 1)
            if upto >= 2:
                attention(0, 0)
                act.wait_ge(sem("dt_col_ready"), 1)
                for h in range(HEADS):
                    plain, masked = bank["decay_ready", 7 * h + 5], bank["decay_ready", 7 * h + 7]
                    if h >= 2:
                        act.wait_ge(sem("w_ready"), NT * (h - 1))
                    act.wait_ge(sem("row_full"), 2 * h + 2)
                    for j in range(NT):
                        bias = small[:, 64 + HEADS * j + h:65 + HEADS * j + h]
                        if j < NT - 1:
                            act.activation(decay[h % 2][:, j, P * (j + 1):], plain[:, P * (j + 1):], ACT.Exp, bias=bias)\
                                .then_inc(sem("decay_ready"), 1)
                        act.activation(decay[h % 2][:, j, P * j:P * (j + 1)], masked[:, P * j:P * (j + 1)], ACT.Exp, bias=bias)\
                            .then_inc(sem("decay_ready"), 1)
                act.wait_ge(sem("ssd_ms_ready"), 1)
                act.activation(small[:, 144:152], small[:, 136:144], ACT.Sqrt).then_inc(sem("ssd_rstd"), 1)

            if upto >= 3:
                norm(1)
                for f in range(FF_TILES):
                    act.wait_ge(sem("gate_full"), f + 1)
                    if f >= 2:
                        act.wait_ge(sem("hid_ready"), f - 1)
                    act.activation(sil[:, f % 2, :], bank["sil_ready", f + 1][:, :], ACT.Silu).then_inc(sem("sil_ready"), 1)

            if upto >= 4:
                norm(2)
                for c in range(C_TILES):
                    act.wait_ge(sem("pc_full"), total("pc_full", c + 1))
                    act.activation(pcT[:, c, 1:], bank["pc_stored", c + 1][:, :], ACT.Copy).then_inc(sem("pc_stored"), 1)
                act.wait_ge(sem("mixed"), 13)
                act.activation(pcT[0:64, 12, 1:], pcT[0:64, 12, 1:], ACT.Tanh).then_inc(sem("lora_in_ready"), 1)
                act.wait_ge(sem("mixed"), 14)
                act.activation(pcT[:, 13, 1:], pcT[:, 13, 1:], ACT.Sigmoid).then_inc(sem("lora_in_ready"), 1)
                for t in range(NT):
                    for i, name in enumerate(("sig", "a")):
                        act.wait_ge(sem("wa_sum"), total("wa_sum", 2 * t + i + 1))
                        act.activation(R[name], R[name], ACT.Sigmoid).then_inc(sem("sig_ready"), 1)
                    act.wait_ge(sem("lora_full"), total("lora_full", 3 * t + 3))
                    act.activation(R["g"], bank["g_ready", t + 1][:, :], ACT.Copy).then_inc(sem("g_ready"), 1)
                    act.wait_ge(sem("kk_ss"), t + 1)
                    act.activation(small[:, 176:184], small[:, 176:184], ACT.Sqrt).then_inc(sem("kk_norm"), 1)
                    for i, (name, row, sign) in enumerate((("Eex", 0, 1.0), ("Ein", 1, 1.0), ("Eni", 1, -1.0), ("Erev", 2, 1.0))):
                        act.wait_ge(sem("cum_full"), total("cum_full", 3 * t + row + 1))
                        act.activation(R[name], bank["exp_ready", 4 * t + (1, 3, 4)[row]][:, :], ACT.Exp, scale=sign).then_inc(sem("exp_ready"), 1)
                    act.wait_ge(sem("end_full"), total("end_full", t + 1))
                    act.activation(small[:, 224 + 8 * (t % 2):232 + 8 * (t % 2)], bank["end_ready", t + 1][:, 0:8], ACT.Exp)\
                        .then_inc(sem("end_ready"), 1)
                    for i in range(4):
                        act.wait_ge(sem("ft_full"), total("ft_full", 4 * t + i + 1))
                        b = bank["ft_ready", 4 * t + i + 1]
                        if i in (0, 1):
                            o = F["ar"][:, :, :, CHUNK * i:CHUNK * (i + 1)]
                            v = b[:, :].rearrange("p (a b c) -> p a b c", b=2, c=CHUNK)
                        else:
                            o, v = F["btT" if i == 2 else "ktT"], b[:, :].rearrange("p (a b) -> p a b", b=P)
                        act.activation(o, v, ACT.Copy).then_inc(sem("ft_ready"), 1)
                    for n in range(5):
                        act.wait_ge(sem("y1_full"), 5 * t + n + 1)
                        act.activation(R["Y1"], bank["y1_ready", 5 * t + n + 1][:, :], ACT.Copy).then_inc(sem("y1_ready"), 1)
                    for i, o in enumerate((R["Z1"], R["U"], F["wt"][:, :, 0:CHUNK], F["wt"][:, :, CHUNK:])):
                        act.wait_ge(sem("zu_full"), 4 * t + i + 1)
                        b = bank["z_ready", 4 * t + i + 1]
                        v = b[:, 0:256].rearrange("p (a b) -> p a b", b=CHUNK) if i >= 2 else b[:, :]
                        act.activation(o, v, ACT.Copy).then_inc(sem("z_ready"), 1)
                    for c in range(2):
                        n = 2 * t + c
                        rows = slice(CHUNK * c, CHUNK * (c + 1))
                        act.wait_ge(sem("sa_ready"), 2 * n + 2)
                        for par in range(2):
                            act.activation(R["y"][rows, :].rearrange("p (a b n) -> p a b n", b=2, n=HD)[:, :, par, :],
                                           bank["y_stored", 2 * n + par + 1][rows, 256:].rearrange("p (a n) -> p a n", n=HD), ACT.Copy)\
                                .then_inc(sem("y_stored"), 1)
                    act.wait_ge(sem("gn_ms"), t + 1)
                    act.activation(small[:, 216:224], small[:, 216:224], ACT.Sqrt).then_inc(sem("gn_rstd"), 1)
                    act.wait_ge(sem("ycT_full"), total("ycT_full", t + 1))
                    act.activation(yT[:, 0:4, P * t:P * (t + 1)], bank["ycT_ready", t + 1][:, :].rearrange("p (a b) -> p a b", b=P), ACT.Copy)\
                        .then_inc(sem("ycT_ready"), 1)

            if upto >= 5:
                for t in range(NT):
                    act.wait_ge(sem("qkvr_stored"), total("qkvr_stored", 12))
                    step(act.activation(sqd[:, 0:Q_RANK], qkvr[:, t, 0:Q_RANK], ACT.Square, accum_out=small[:, 152 + t:153 + t]))
                    step(act.activation(sqd[:, 0:KV_RANK], qkvr[:, t, Q_RANK:Q_RANK + KV_RANK], ACT.Square, accum_out=small[:, 156 + t:157 + t]))
                act.activation(small[:, 160:168], small[:, 152:160], ACT.Copy).then_inc(sem("mla_ss"), 1)
                act.wait_ge(sem("mla_ms"), 1)
                act.activation(small[:, 168:176], small[:, 160:168], ACT.Sqrt).then_inc(sem("mla_rstd"), 1)
                act.wait_ge(sem("angle_ready"), 1)
                for i in range(2):
                    act.activation(rope_cs[:, 4 * i:4 * i + 4, :], rope_cs[:, 4 * i:4 * i + 4, :], ACT.Sin).then_inc(sem("sin_ready"), 1)
                for i in range(8):
                    half, t = divmod(i, NT)
                    act.wait_ge(sem("uq_full"), total("uq_full", i + 1))
                    act.activation(q_tok[:, t, 4 * half:4 * half + 4, :], bank["q_stored", i + 1][:, 0:384].rearrange("p (h n) -> p h n", n=QD),
                                   ACT.Copy, scale=MLA_SCALE).then_inc(sem("q_stored"), 1)
                for h in range(HEADS):
                    act.wait_ge(sem("ukv_full"), total("ukv_full", h + 1))
                    act.activation(kT_d[0:HD, h, :], bank["kn_stored", h + 1][0:HD, :], ACT.Copy).then_inc(sem("kn_stored"), 1)
                for h in range(HEADS):
                    act.wait_ge(sem("qT_full"), h + 1)
                    act.activation(qT_d[:, h, :], bank["qT_ready", h + 1][0:QD, :], ACT.Copy).then_inc(sem("qT_ready"), 1)
                attention(HEADS * NT, 4)

            if upto >= 6:
                norm(3)
                act.wait_ge(sem("top_ready"), 1)
                act.activation(ex, ex, ACT.Exp).then_inc(sem("ex_ready"), 1)
                act.wait_ge(sem("rounds_ready"), 1)
                rounds = act.value_load(small_i[0:1, 8:9], min_val=1, max_val=MAX_ROUNDS)
                with act.Fori(0, rounds) as r:
                    with act.Fori(0, N_EXPERTS) as e:
                        turn = r * N_EXPERTS + e
                        act.wait_ge(sem("pickT_full"), turn * 2 + 1)
                        act.activation(pickT[:, 0, :], turn_banks[3][:, :], ACT.Copy).then_inc(sem("pickT_ready"), 1)
                        act.wait_ge(sem("pickT_full"), turn * 2 + 2)
                        act.activation(pickT[0:CAP2, 1, :], acc[3][0:CAP2, :], ACT.Copy).then_inc(sem("pickT_ready"), 1)
                        for j in range(GROUPS_E):
                            act.wait_ge(sem("gate_full"), turn * GROUPS_E + (FF_TILES + j + 1))
                            act.wait_ge(sem("hid_ready"), turn * GROUPS_E + (FF_TILES + j - 1))
                            act.activation(sil_e[:, j % 2, :], turn_banks[(4 + 2 * j) % 4][:, 0:2 * CAP], ACT.Silu)\
                                .then_inc(sem("sil_ready"), 1)
                        act.wait_ge(sem("down_used"), turn * GROUPS_E + (10 + GROUPS_E))
                        for i in range(3):
                            n = min(3, KT - 3 * i)
                            act.activation(outT[:, 3 * i:3 * i + n, :], acc[i][:, 0:CAP * n].rearrange("p (a b) -> p a b", b=CAP), ACT.Copy)\
                                .then_inc(sem("outT_ready"), 1)
                        for i in range(4):
                            act.wait_ge(sem("out_tok_full"), turn * 4 + i + 1)
                            rows = P if i < 2 else CAP2
                            act.activation(out_tok[0:rows, i // 2, 512 * (i % 2):512 * (i % 2) + 512],
                                           turn_banks[(4 + 2 * GROUPS_E + i) % 4][0:rows, :], ACT.Copy).then_inc(sem("out_tok_ready"), 1)
                act.wait_ge(sem("moe_done"), 1)
                norm(4)

        @block.vector
        def _(dve):
            step = Steps(dve, sem("dve_step"))

            def tt(o, a, b, op):
                return dve.tensor_tensor(o, a, b, op)

            def scale_by(view, shape):
                return view.to_broadcast(shape)

            def inv_mean(o, i, n, eps):
                step(dve.tensor_scalar(o, i, n, eps, ALU.mult, ALU.add))
                return dve.reciprocal(o, o)

            def norm(j):
                dve.wait_ge(sem("ss_ready"), j + 1)
                inv_mean(small[:, 36:40], small[:, 32:36], 1.0, RMS_EPS).then_inc(sem("ms_ready"), 1)
                dve.wait_ge(sem("rstd_ready"), j + 1)
                if j == 4:
                    return
                for t in range(NT):
                    dve.tensor_scalar(xn[:, t, :], xs[:, t, :], small[:, 40 + t:41 + t], None, ALU.mult).then_inc(sem("xn_ready"), 1)
                for t in range(NT):
                    for half in range(2):
                        dve.wait_ge(sem("xnT_full"), 8 * j + 2 * t + half + 1)
                        b = bank["hT_ready", 8 * j + 2 * t + half + 1][:, :].rearrange("p (a b) -> p a b", b=P)
                        wv = vc[:, 8 * j + 4 * half:8 * j + 4 * half + 4].unsqueeze(2).to_broadcast([P, 4, P])
                        tt(hT[:, 4 * half:4 * half + 4, P * t:P * (t + 1)], b, wv, ALU.mult).then_inc(sem("hT_ready"), 1)

            def attention(first, done):
                for i in range(HEADS * NT + 2):
                    if i < HEADS * NT:
                        n = P * (i % NT + 1)
                        dve.wait_ge(sem("scores_full"), first + i + 1)
                        step(dve.tensor_reduce(small[:, 60 + i % 4:61 + i % 4], bank["probs_ready", first + i + 1][:, 0:n], AX, ALU.max))
                        dve.tensor_scalar(small[:, 48 + i % 4:49 + i % 4], small[:, 60 + i % 4:61 + i % 4], -1.0, None, ALU.mult).then_inc(sem("max_ready"), 1)
                    u = i - 1
                    if 0 <= u < HEADS * NT:
                        n = P * (u % NT + 1)
                        dve.wait_ge(sem("probs_ready"), first + u + 1)
                        step(dve.reciprocal(small[:, 56 + u % 4:57 + u % 4], small[:, 52 + u % 4:53 + u % 4]))
                        dve.tensor_scalar(probs[:, u % 3, 0:n], probs[:, u % 3, 0:n], small[:, 56 + u % 4:57 + u % 4], None, ALU.mult).then_inc(sem("probs_scaled"), 1)
                    u = i - 2
                    if u >= 0:
                        h, t = divmod(u, NT)
                        dve.wait_ge(sem("probsT_full"), first + u + 1)
                        if t == 0 and h >= 2:
                            dve.wait_ge(sem("pv_done"), 2 * done + h - 1)
                        dve.tensor_copy(probsT[h % 2][:, 0:t + 1, P * t:P * (t + 1)],
                                            bank["probsT_ready", first + u + 1][:, 0:P * (t + 1)].rearrange("p (a b) -> p a b", b=P)).then_inc(sem("probsT_ready"), 1)

            def add_x(full, count, t, cols, b):
                dve.wait_ge(sem(full), count)
                tt(xs[:, t, cols], xs[:, t, cols], b, ALU.add).then_inc(sem("x_added"), 1)

            def out_proj(base, full0):
                for c in range(4):
                    for t in range(NT):
                        n = 4 * c + t
                        add_x("mix_full", full0 + n + 1, t, slice(256 * c, 256 * c + 256), bank["x_added", base + n + 1][:, 0:256])

            dve.wait_ge(sem("vec_full"), 1)
            dve.wait_ge(sem("small_loaded"), 64)
            dve.tensor_copy(vc[:, :], bank["vc_ready", 1][:, 0:95]).then_inc(sem("vc_ready"), 1)
            dve.wait_ge(sem("vc_ready"), 1)
            norm(0)
            for i in range(8):
                dve.wait_ge(sem("v_full"), i + 1)
                dve.tensor_copy(v_a[:, i % 4, 256 * (i // 4):256 * (i // 4) + 256], bank["v_stored", i + 1][:, 0:256]).then_inc(sem("v_stored"), 1)
            dve.wait_ge(sem("const_ready"), 1)
            for c in range(CONV_TILES):
                dve.wait_ge(sem("conv_stored"), c + 1)
                tap = lambda k: vc[:, 40 + 8 * k + c:41 + 8 * k + c]
                step(dve.tensor_scalar(conv_out[:, c, :], conv_in[:, c, 0:SEQ], tap(0), vc[:, 32 + c:33 + c], ALU.mult, ALU.add))
                for k in range(1, B_CONV):
                    i = dve.scalar_tensor_tensor(out=conv_out[:, c, :], in0=conv_in[:, c, k:k + SEQ], scalar=tap(k),
                                                 in1=conv_out[:, c, :], op0=ALU.mult, op1=ALU.add)
                    if k < B_CONV - 1:
                        step(i)
                i.then_inc(sem("conv_sum"), 1)
            dve.wait_ge(sem("u_ready"), 1)
            dve.scalar_tensor_tensor(out=dt_row[1], in0=dt_row[0], scalar=-1.0, in1=dt_row[0], op0=ALU.mult, op1=ALU.max).then_inc(sem("abs_ready"), 1)
            dve.wait_ge(sem("ln_ready"), 1)
            step(dve.scalar_tensor_tensor(out=dt_keep, in0=dt_row[0], scalar=0.0, in1=dt_row[1], op0=ALU.max, op1=ALU.add))
            if upto >= 2:
                attention(0, 0)
                step(dve.memset(ones_row, 1.0))
                dve.wait_ge(sem("pv_done"), HEADS)
                step(dve.tensor_copy(dt_row[0], dt_keep))
                step(dve.tensor_scalar(dt_row[2], dt_row[0], small[0:HEADS, 2:3], -1.0, ALU.mult, ALU.mult))
                step(dve.tensor_tensor_scan(dt_row[1], ones_row, dt_row[2], 0.0, ALU.mult, ALU.add))
                dve.tensor_scalar(dt_row[2], dt_row[1], -1.0, None, ALU.mult).then_inc(sem("cum_ready"), 1)
                for t in range(NT):
                    dve.wait_ge(sem("x_tok_full"), t + 1)
                    dve.tensor_copy(x_tok[:, t, :], bank["x_tok_ready", t + 1][:, :]).then_inc(sem("x_tok_ready"), 1)
                for i in range(8):
                    g, j = divmod(i, NT)
                    dve.wait_ge(sem("cb_full"), i + 1)
                    dve.tensor_copy(cbT[:, g, j, P * j:], bank["cb_ready", i + 1][:, P * j:]).then_inc(sem("cb_ready"), 1)
                dve.wait_ge(sem("dt_col_full"), 1)
                step(dve.tensor_copy(small[:, 64:128], bank["dt_col_ready", 1][:, 0:64]))
                dve.tensor_copy(small[:, 3:4], small[:, 64:65]).then_inc(sem("dt_col_ready"), 1)
                dtc = small[:, 96:128].rearrange("p (t h) -> p t h", h=HEADS).unsqueeze(3).to_broadcast([P, NT, HEADS, HD])
                step(tt(xdt.rearrange("p t (h n) -> p t h n", n=HD), x_tok.rearrange("p t (h n) -> p t h n", n=HD), dtc, ALU.mult))
                for h in range(HEADS + 1):
                    if h < HEADS:
                        if h >= 2:
                            dve.wait_ge(sem("ssd_full"), h - 1)
                        for j in range(NT):
                            dve.wait_ge(sem("decay_ready"), 7 * h + min(2 * j + 2, 7))
                            tt(wT[h % 2][:, j, P * j:], decay[h % 2][:, j, P * j:], cbT[:, h // 4, j, P * j:], ALU.mult).then_inc(sem("w_ready"), 1)
                    if h >= 1:
                        g = h - 1
                        dve.wait_ge(sem("ssd_full"), g + 1)
                        cols = slice(HD * g, HD * (g + 1))
                        dve.scalar_tensor_tensor(out=y_tok[:, :, cols], in0=x_tok[:, :, cols], scalar=small[:, 8 + g:9 + g],
                                                     in1=bank["y_tok_ready", g + 1][:, 0:256].rearrange("p (a b) -> p a b", b=HD),
                                                     op0=ALU.mult, op1=ALU.add).then_inc(sem("y_tok_ready"), 1)
                dve.wait_ge(sem("y_tok_ready"), HEADS)
                dve.wait_ge(sem("z_stored"), 8)
                step(tt(y_tok, y_tok, zs, ALU.mult))
                step(tt(decay[0], y_tok, y_tok, ALU.mult))
                step(dve.tensor_reduce(small[:, 128:136], decay[0].rearrange("p t (g n) -> p (t g) n", n=256), AX, ALU.add))
                inv_mean(small[:, 136:144], small[:, 128:136], 1.0 / 256, B_NORM_EPS).then_inc(sem("ssd_ms_ready"), 1)
                dve.wait_ge(sem("ssd_rstd"), 1)
                rs = small[:, 144:152].unsqueeze(2).to_broadcast([P, 8, 256])
                yv = y_tok.rearrange("p t (g n) -> p (t g) n", n=256)
                tt(yv, yv, rs, ALU.mult).then_inc(sem("yn_ready"), 1)
                for t in range(NT):
                    dve.wait_ge(sem("ynT_full"), t + 1)
                    tt(yT[:, 4:8, P * t:P * (t + 1)], bank["yT_b_ready", t + 1][:, :].rearrange("p (a b) -> p a b", b=P),
                           vc[:, 91:95].unsqueeze(2).to_broadcast([P, 4, P]), ALU.mult).then_inc(sem("yT_b_ready"), 1)
                out_proj(0, 0)

            if upto >= 3:
                norm(1)
                for f in range(FF_TILES):
                    dve.wait_ge(sem("up_full"), f + 1)
                    dve.wait_ge(sem("sil_ready"), f + 1)
                    tt(hid[:, f, :], sil[:, f % 2, :], bank["hid_ready", f + 1][:, :], ALU.mult).then_inc(sem("hid_ready"), 1)
                for half in range(2):
                    for t in range(NT):
                        add_x("down_full", 4 * half + t + 1, t, slice(512 * half, 512 * half + 512), acc[t][:, :])

            if upto >= 4:
                norm(2)
                step(dve.memset(pcT[:, :, 0:1], 0.0))
                for j in range(C_TILES):
                    dve.wait_ge(sem("pc_stored"), total("pc_stored", j + 1))
                    step(tt(mixdiff[:, j % 2, :], pcT[:, j, 0:SEQ], pcT[:, j, 1:], ALU.subtract))
                    dve.scalar_tensor_tensor(out=pcT[:, j, 1:], in0=mixdiff[:, j % 2, :], scalar=vc[:, 72 + j:73 + j],
                                                 in1=pcT[:, j, 1:], op0=ALU.mult, op1=ALU.add).then_inc(sem("mixed"), 1)
                for i in range(12):
                    c, t = divmod(i, NT)
                    n = 256 if c < 2 else QKVR - 512
                    dve.wait_ge(sem("qkvr_full"), total("qkvr_full", i + 1))
                    dve.tensor_copy(qkvr[:, t, 256 * c:256 * c + n], bank["qkvr_stored", i + 1][:, 0:n]).then_inc(sem("qkvr_stored"), 1)
                dve.wait_ge(sem("bc_loaded"), 16 * 7)
                by_head = lambda v: v.rearrange("p (h n) -> p h n", n=HD)
                spread = lambda v: v.unsqueeze(2).to_broadcast([P, HEADS, HD])
                dve.wait_ge(sem("mixed"), C_TILES)
                dve.memset(state[0], 0.0).then_inc(sem("state_ready"), 1)
                for t in range(NT):
                    for a, name in enumerate("rkv"):
                        dve.wait_ge(sem("rkv_full"), total("rkv_full", 3 * t + a + 1))
                        dve.tensor_copy(R[name], bank["rkv_ready", 3 * t + a + 1][:, :]).then_inc(sem("rkv_ready"), 1)
                    for i, (name, bias) in enumerate((("sig", "w0"), ("a", "a0"))):
                        dve.wait_ge(sem("lora_full"), total("lora_full", 3 * t + i + 1))
                        tt(R[name], bank["wa_sum", 2 * t + i + 1][:, :], bc[bias], ALU.add).then_inc(sem("wa_sum"), 1)
                    dve.wait_ge(sem("rkv_ready"), total("rkv_ready", 3 * t + 3))
                    step(tt(R["kk"], R["k"], bc["k_k"], ALU.mult))
                    step(tt(R["tmp"], R["kk"], R["kk"], ALU.mult))
                    dve.tensor_reduce(small[:, 176:184], by_head(R["tmp"]), AX, ALU.add).then_inc(sem("kk_ss"), 1)
                    dve.wait_ge(sem("kk_ss"), t + 1)
                    dve.wait_ge(sem("sig_ready"), 2 * t + 2)
                    step(dve.scalar_tensor_tensor(out=R["tmp"], in0=R["a"], scalar=-1.0, in1=bc["k_a"], op0=ALU.add, op1=ALU.mult))
                    step(dve.scalar_tensor_tensor(out=R["k"], in0=R["tmp"], scalar=1.0, in1=R["k"], op0=ALU.add, op1=ALU.mult))
                    step(tt(R["tmp"], R["r"], R["k"], ALU.mult))
                    step(tt(R["tmp"], R["tmp"], bc["r_k"], ALU.mult))
                    step(dve.tensor_reduce(small[:, 192:200], by_head(R["tmp"]), AX, ALU.add))
                    dve.wait_ge(sem("kk_norm"), t + 1)
                    step(dve.tensor_scalar(small[:, 184:192], small[:, 176:184], 1e-12, None, ALU.max))
                    step(dve.reciprocal(small[:, 184:192], small[:, 184:192]))
                    step(tt(by_head(R["kk"]), by_head(R["kk"]), spread(small[:, 184:192]), ALU.mult))
                    step(tt(R["b"], R["kk"], R["a"], ALU.mult))
                    dve.wait_ge(sem("exp_ready"), 4 * t + 4)
                    dve.scalar_tensor_tensor(out=R["al"], in0=R["kk"], scalar=-1.0, in1=R["Eex"], op0=ALU.mult, op1=ALU.mult).then_inc(sem("scaled_ready"), 1)
                    for o, i, e in (("rt", "r", "Ein"), ("bt", "b", "Eni"), ("kt", "k", "Eni"), ("bh", "b", "Erev"), ("kh", "k", "Erev")):
                        tt(R[o], R[i], R[e], ALU.mult).then_inc(sem("scaled_ready"), 1)
                    dve.wait_ge(sem("scaled_ready"), 6 * t + 6)
                    for i in range(6):
                        dve.wait_ge(sem("pm_full"), 6 * t + i + 1)
                        b = bank["pm_ready", 6 * t + i + 1]
                        par = i % 2
                        if i < 4:
                            mask = pair_mask[:, :, :].rearrange("p a b -> p (a b)")
                            o = F["ab" if i < 2 else "ak"][:, par::2, :]
                            tt(o, b[:, :].rearrange("p (h n) -> p h n", n=P), mask.unsqueeze(1).to_broadcast([P, 4, P]), ALU.mult).then_inc(sem("pm_ready"), 1)
                        else:
                            dve.tensor_copy(by_head(R["A"])[:, par::2, :], b[:, 0:256].rearrange("p (h n) -> p h n", n=HD)).then_inc(sem("pm_ready"), 1)
                    dve.wait_ge(sem("pm_ready"), 6 * t + 6)
                    over_heads = lambda m: m.unsqueeze(1).to_broadcast([P, HEADS, CHUNK])
                    step(tt(by_head(R["X"]), F["ab"][:, :, 0:CHUNK], over_heads(level_one[:, :]), ALU.mult))
                    step(tt(by_head(R["X"]), by_head(R["X"]), over_heads(eye64[:, :]), ALU.add))
                    step(tt(by_head(R["XT"]), by_head(R["A"]), over_heads(level_mask[:, 0, :]), ALU.mult))
                    step(tt(by_head(R["XT"]), by_head(R["XT"]), over_heads(eye64[:, :]), ALU.add))
                    tt(by_head(R["ot0"]), by_head(R["A"]), over_heads(level_mask[:, 1, :]), ALU.mult).then_inc(sem("inv_ready"), 1)
                    for n in range(5):
                        if n < 4:
                            step(tt(by_head(R[f"ot{(n + 1) % 2}"]), by_head(R["A"]), over_heads(level_mask[:, n + 2, :]), ALU.mult))
                        dve.wait_ge(sem("dx_full"), 9 * t + 2 * n + 1)
                        if n < 4:
                            dve.wait_ge(sem("dx_full"), 9 * t + 2 * n + 2)
                        tt(R["X"], R["X"], bank["dx_used", 9 * t + 2 * n + 1][:, :], ALU.add).then_inc(sem("dx_used"), 1)
                        if n < 4:
                            tt(R["XT"], R["XT"], bank["dx_used", 9 * t + 2 * n + 2][:, :], ALU.add).then_inc(sem("dx_used"), 1)
                        dve.wait_ge(sem("dx_used"), 9 * t + (2 * n + 2 if n < 4 else 9))
                    for c in range(2):
                        n = 2 * t + c
                        rows = slice(CHUNK * c, CHUNK * (c + 1))
                        dve.wait_ge(sem("end_ready"), t + 1)
                        decays = small[:, 224 + 8 * (t % 2):232 + 8 * (t % 2)].rearrange("p (a b) -> p a b", b=2)[:, :, c:c + 1].to_broadcast([P, 4, HD])
                        dve.wait_ge(sem("state_ready"), n + 1)
                        if n >= 1:
                            dve.wait_ge(sem("yc_full"), n)
                        step(tt(state[(n + 1) % 2], state[n % 2], decays, ALU.mult))
                        dve.wait_ge(sem("z_ready"), 4 * t + 2)
                        for par in range(2):
                            dve.wait_ge(sem("sa_full"), 2 * n + par + 1)
                            tt(by_head(R["SA"])[rows, par::2, :], bank["y_stored", 2 * n + par + 1][rows, 0:256]
                                   .rearrange("p (h n) -> p h n", n=HD), by_head(R["U"])[rows, par::2, :], ALU.add).then_inc(sem("sa_ready"), 1)
                        dve.wait_ge(sem("state_full"), n + 1)
                        tt(state[(n + 1) % 2], state[(n + 1) % 2],
                               bank["state_ready", n + 2][:, 0:256].rearrange("p (a b) -> p a b", b=HD), ALU.add).then_inc(sem("state_ready"), 1)
                        dve.wait_ge(sem("yc_full"), n + 1)
                        dve.wait_ge(sem("y_stored"), 2 * n + 2)
                        tt(R["y"][rows, :], R["y"][rows, :], bank["y_added", n + 1][rows, :], ALU.add).then_inc(sem("y_added"), 1)
                    dve.wait_ge(sem("y_added"), 2 * t + 2)
                    y = by_head(R["y"])
                    step(dve.tensor_reduce(small[:, 200:208], y, AX, ALU.add))
                    step(dve.tensor_scalar(small[:, 200:208], small[:, 200:208], -1.0 / HD, None, ALU.mult))
                    step(tt(y, y, spread(small[:, 200:208]), ALU.add))
                    step(tt(R["tmp"], R["y"], R["y"], ALU.mult))
                    step(dve.tensor_reduce(small[:, 208:216], by_head(R["tmp"]), AX, ALU.add))
                    inv_mean(small[:, 216:224], small[:, 208:216], 1.0 / HD, C_GN_EPS).then_inc(sem("gn_ms"), 1)
                    dve.wait_ge(sem("gn_rstd"), t + 1)
                    step(tt(y, y, spread(small[:, 216:224]), ALU.mult))
                    step(tt(R["y"], R["y"], bc["ln_w"], ALU.mult))
                    step(tt(R["y"], R["y"], bc["ln_b"], ALU.add))
                    step(tt(by_head(R["tmp"]), by_head(R["v"]), spread(small[:, 192:200]), ALU.mult))
                    step(tt(R["y"], R["y"], R["tmp"], ALU.add))
                    dve.wait_ge(sem("g_ready"), t + 1)
                    tt(R["y"], R["y"], R["g"], ALU.mult).then_inc(sem("yc_ready"), 1)

            if upto >= 5:
                dve.wait_ge(sem("mla_ss"), 1)
                step(dve.tensor_scalar(small[:, 160:164], small[:, 160:164], 1.0 / Q_RANK, RMS_EPS, ALU.mult, ALU.add))
                step(dve.tensor_scalar(small[:, 164:168], small[:, 164:168], 1.0 / KV_RANK, RMS_EPS, ALU.mult, ALU.add))
                dve.reciprocal(small[:, 160:168], small[:, 160:168]).then_inc(sem("mla_ms"), 1)
                dve.wait_ge(sem("mla_rstd"), 1)
                dve.wait_ge(sem("ycT_ready"), NT)
                for t in range(NT):
                    step(dve.tensor_scalar(qkvr[:, t, 0:Q_RANK], qkvr[:, t, 0:Q_RANK], small[:, 168 + t:169 + t], None, ALU.mult))
                    kv = qkvr[:, t, Q_RANK:Q_RANK + KV_RANK]
                    dve.tensor_scalar(kv, kv, small[:, 172 + t:173 + t], None, ALU.mult).then_inc(sem("qkvn_ready"), 1)
                for i in range(16):
                    step(dve.memset(small[:, 16 + i:17 + i], ROPE_THETA ** (-i / 16)))
                step(dve.tensor_copy(small[:, 240:244], small_i[:, 0:NT]))
                ang, turns = rope_cs[:, 0:4, :], rope_cs[:, 4:8, :]
                step(dve.tensor_copy(ang, small[:, 16:32].unsqueeze(1).to_broadcast([P, NT, 16])))
                step(tt(ang, ang, small[:, 240:244].unsqueeze(2).to_broadcast([P, NT, 16]), ALU.mult))
                step(dve.tensor_scalar(turns, ang, 1.0 / (2 * math.pi), MAGIC, ALU.mult, ALU.add))
                step(dve.tensor_scalar(turns, turns, -MAGIC, None, ALU.add))
                for part in TWO_PI:
                    step(dve.scalar_tensor_tensor(out=ang, in0=turns, scalar=-part, in1=ang, op0=ALU.mult, op1=ALU.add))
                step(dve.tensor_scalar(ang, ang, 3.1415925, -3.1415925, ALU.min, ALU.max))
                step(dve.scalar_tensor_tensor(out=turns, in0=ang, scalar=-1.0, in1=ang, op0=ALU.mult, op1=ALU.max))
                dve.tensor_scalar(turns, turns, -1.0, math.pi / 2, ALU.mult, ALU.add).then_inc(sem("angle_ready"), 1)
                for t in range(NT):
                    for i, (n, col) in enumerate(((3, 86), (2, 89))):
                        dve.wait_ge(sem("qnT_full"), 2 * t + i + 1)
                        o = (qnT if i == 0 else kvnT)[:, :, P * t:P * (t + 1)]
                        tt(o, bank["qnT_ready", 2 * t + i + 1][:, 0:P * n].rearrange("p (a b) -> p a b", b=P),
                               vc[:, col:col + n].unsqueeze(2).to_broadcast([P, n, P]), ALU.mult).then_inc(sem("qnT_ready"), 1)
                dve.wait_ge(sem("sin_ready"), 2)

                def rope(lo, hi, sin, cos, tmp):
                    step(tt(tmp[0], lo, sin, ALU.mult))
                    step(tt(tmp[1], hi, sin, ALU.mult))
                    step(tt(lo, lo, cos, ALU.mult))
                    step(tt(hi, hi, cos, ALU.mult))
                    step(tt(lo, lo, tmp[1], ALU.subtract))
                    tt(hi, hi, tmp[0], ALU.add).then_inc(sem("rope_ready"), 1)

                sin, cos = rope_cs[:, 0:4, :], rope_cs[:, 4:8, :]
                kr = qkvr[:, :, QKVR - ROPE:]
                rope(kr[:, :, 0:16], kr[:, :, 16:32], sin, cos, [rope_cs[:, 8:12, :], rope_cs[:, 12:16, :]])
                for t in range(NT):
                    dve.wait_ge(sem("ukv_full"), total("ukv_full", HEADS + t + 1))
                    dve.tensor_copy(v_d[:, t, :], bank["v_d_stored", t + 1][:, :]).then_inc(sem("v_d_stored"), 1)
                dve.wait_ge(sem("q_stored"), 8)
                tmp = [region(512 * i, NT, HEADS, 16) for i in range(2)]
                wide = [v.unsqueeze(2).to_broadcast([P, NT, HEADS, 16]) for v in (sin, cos)]
                rope(q_tok[:, :, :, HD:HD + 16], q_tok[:, :, :, HD + 16:], wide[0], wide[1], tmp)
                dve.wait_ge(sem("kpe_full"), total("kpe_full", 1))
                dve.tensor_copy(kT_d[HD:QD, :, :], bank["kpe_ready", 1][HD:QD, :].unsqueeze(1).to_broadcast([ROPE, HEADS, SEQ])).then_inc(sem("kpe_ready"), 1)
                attention(HEADS * NT, 4)
                out_proj(24, 16)

            if upto >= 6:
                norm(3)
                L, E2 = NT * N_EXPERTS, [P, NT, N_EXPERTS, N_EXPERTS]
                dve.wait_ge(sem("logit_full"), 1)
                dve.tensor_copy(logit, bank["logit_ready", 1][:, 0:L].rearrange("p (t e) -> p t e", e=N_EXPERTS)).then_inc(sem("logit_ready"), 1)
                dve.wait_ge(sem("logit_ready"), 1)
                step(dve.tensor_reduce(top, logit, AX, ALU.max))
                tt(ex, logit, top.unsqueeze(2).to_broadcast([P, NT, N_EXPERTS]), ALU.subtract).then_inc(sem("top_ready"), 1)
                other, own = logit.unsqueeze(2).to_broadcast(E2), logit.unsqueeze(3).to_broadcast(E2)
                step(tt(same, other, own, ALU.is_equal))
                step(tt(same, same, expert_lt[:, :, :].unsqueeze(1).to_broadcast(E2), ALU.mult))
                step(tt(more, other, own, ALU.is_gt))
                step(tt(more, more, same, ALU.add))
                step(dve.tensor_reduce(rank, more, AX, ALU.add))
                dve.tensor_scalar(sel, rank, TOP_K - 0.5, None, ALU.is_lt).then_inc(sem("sel_ready"), 1)
                dve.wait_ge(sem("sel_ready"), 1)
                dve.wait_ge(sem("ex_ready"), 1)
                step(tt(ex, ex, sel, ALU.mult))
                step(dve.tensor_reduce(top, ex, AX, ALU.add))
                step(dve.reciprocal(top, top))
                step(tt(gate, ex, top.unsqueeze(2).to_broadcast([P, NT, N_EXPERTS]), ALU.mult))
                dve.wait_ge(sem("place_full"), 1)
                b = bank["place_ready", 1]
                step(dve.scalar_tensor_tensor(out=place, in0=b[:, 0:L].rearrange("p (t e) -> p t e", e=N_EXPERTS), scalar=4096.0,
                                              in1=sel, op0=ALU.add, op1=ALU.mult))
                step(dve.tensor_scalar(place, place, -4096.0, None, ALU.add))
                dve.tensor_reduce(small[:, 5:6], b[:, L:L + N_EXPERTS], AX, ALU.max).then_inc(sem("place_ready"), 1)
                dve.wait_ge(sem("place_ready"), 1)
                step(dve.tensor_scalar(small[:, 6:7], small[:, 5:6], CAP + 0.5, 1.0, ALU.is_gt, ALU.add))
                for i in range(2, MAX_ROUNDS):
                    step(dve.scalar_tensor_tensor(out=small[:, 6:7], in0=small[:, 5:6], scalar=i * CAP + 0.5, in1=small[:, 6:7],
                                                  op0=ALU.is_gt, op1=ALU.add))
                dve.tensor_copy(small_i[:, 8:9], small[:, 6:7]).then_inc(sem("rounds_ready"), 1)
                dve.wait_ge(sem("rounds_ready"), 1)
                rounds = dve.value_load(small_i[0:1, 8:9], min_val=1, max_val=MAX_ROUNDS)
                with dve.Fori(0, rounds) as r:
                    with dve.Fori(0, N_EXPERTS) as e:
                        turn = r * N_EXPERTS + e
                        at = lambda v, t: v[:, t, bass.ds(e, 1)]
                        for g in range(2):
                            for t in range(NT):
                                if g == 0:
                                    i = dve.tensor_scalar(pick[:, t, :], slot_no[:, :], at(place, t), None, ALU.is_equal)
                                else:
                                    i = dve.tensor_scalar(pick_g[:, t, :], slot_no[:, :], at(place, t), at(gate, t), ALU.is_equal, ALU.mult)
                            i.then_inc(sem("pick_ready"), 1)
                        for i in range(3):
                            n = min(3, KT - 3 * i)
                            dve.wait_ge(sem("xg_full"), turn * 3 + i + 1)
                            tt(xgT[:, 3 * i:3 * i + n, :], turn_banks[i][:, 0:CAP * n].rearrange("p (a b) -> p a b", b=CAP),
                                   vc[:, 24 + 3 * i:24 + 3 * i + n].unsqueeze(2).to_broadcast([P, n, CAP]), ALU.mult).then_inc(sem("xg_ready"), 1)
                        for j in range(GROUPS_E):
                            dve.wait_ge(sem("up_full"), turn * GROUPS_E + (FF_TILES + j + 1))
                            dve.wait_ge(sem("sil_ready"), turn * GROUPS_E + (FF_TILES + j + 1))
                            dve.wait_ge(sem("down_used"), turn * GROUPS_E + (10 + j - 1))
                            tt(hid_e[:, j % 2, :], sil_e[:, j % 2, :], turn_banks[(5 + 2 * j) % 4][:, 0:2 * CAP], ALU.mult).then_inc(sem("hid_ready"), 1)
                        for i in range(8):
                            t, half = divmod(i, 2)
                            dve.wait_ge(sem("scatter_full"), turn * 8 + i + 1)
                            cols = slice(512 * half, 512 * half + 512)
                            tt(xs[:, t, cols], xs[:, t, cols], turn_banks[i % 4][:, :], ALU.add).then_inc(sem("moe_added"), 1)
                        dve.wait_ge(sem("moe_added"), turn * 8 + 8)
                    dve.tensor_scalar(place, place, -float(CAP), None, ALU.add).then_inc(sem("round_step"), 1)
                    dve.wait_ge(sem("round_step"), r + 1)
                dve.tensor_copy(small[:, 7:8], small[:, 6:7]).then_inc(sem("moe_done"), 1)
                norm(4)
                dve.wait_ge(sem("final_loaded"), 16)
                for t in range(NT):
                    dve.scalar_tensor_tensor(out=y_out[:, t, :], in0=xs[:, t, :], scalar=small[:, 40 + t:41 + t], in1=final_w,
                                                 op0=ALU.mult, op1=ALU.mult).then_inc(sem("y_ready"), 1)


_OUT = (1, SEQ, D)


def kernel(**inputs):
    import numpy as np
    import concourse.bacc as bacc
    from concourse.bass_utils import run_bass_kernel_spmd

    nc = bacc.Bacc("TRN2", target_bir_lowering=False, num_devices=1)
    arrays, args = {}, {}
    for name, value in inputs.items():
        a = np.ascontiguousarray(value)
        arrays[f"in_{name}_dram"] = a
        args[name] = nc.dram_tensor(f"in_{name}_dram", a.shape, mybir.dt.from_np(a.dtype), kind="ExternalInput").ap()
    args["out"] = nc.dram_tensor("out_0_dram", _OUT, F32, kind="ExternalOutput").ap()
    hybrid_trunk(nc, **args)
    r = run_bass_kernel_spmd(nc, [arrays], core_ids=[0])
    return r.results[0]["out_0_dram"]
```

```python
import math
from contextlib import ExitStack

import concourse.bass as bass
from concourse import mybir

F32 = mybir.dt.float32
F32R = mybir.dt.float32r
I32 = mybir.dt.int32
ALU = mybir.AluOpType
ACT = mybir.ActivationFunctionType
AX = mybir.AxisListType.X

P = 128
SEQ, D = 512, 1024
NT = SEQ // P
KT = D // P
CHUNK = 64
RMS_EPS = 1e-6
HEADS, HD = 8, 64
REL_CLIP = 256
A_COLS = 3 * HEADS * HD
B_WIDTH, B_STATE, B_GROUPS, B_CONV = 512, 128, 2, 4
B_CONV_CH = B_WIDTH + 2 * B_GROUPS * B_STATE
CONV_TILES = B_CONV_CH // P
DT_COL = A_COLS + B_WIDTH + B_CONV_CH
B_NORM_EPS = 1e-5
FF = 2816
FF_TILES = FF // P
C_WIDTH = 512
C_IN = 3 * C_WIDTH + 64 + 64 + 128
C_TILES = C_IN // P
C_GN_EPS = 64e-5
Q_RANK, KV_RANK, ROPE = 384, 256, 32
QKVR = Q_RANK + KV_RANK + ROPE
QD = HD + ROPE
MLA_SCALE = QD ** -0.5
ROPE_THETA = 10000.0
N_EXPERTS, TOP_K, FF_E = 8, 2, 3584
FE_TILES = FF_E // P
GROUPS_E = FE_TILES // 2
CAPS = (P, 144, 168)
CAP = CAPS[-1]
CAP2 = CAP - P
MAX_ROUNDS = -(-SEQ // CAP)
CANDIDATES = MAX_ROUNDS * N_EXPERTS
MAX_TURNS = (TOP_K * SEQ + N_EXPERTS * (CAP - 1)) // CAP + len(CAPS) - 1
IDLE = 8192.0
TILES_E = 3 * GROUPS_E
MASKED = -1e30
DECAY_RATE = -math.exp(-0.5)
SLOTS = 7
DENSE_RAW, DENSE_SPLIT = 3, 2
RAW, SPLIT = 6, 3
SPLIT_PHASES = (("e_in",), ("ff_g", "ff_u"), ("o_in",))
SLOT = 2048
MAGIC = 1.5 * 2.0 ** 23
TWO_PI = (6.28125, 0.00193500518798828125, 3.0199159819e-07)


class Banks:

    def __init__(self, banks, start):
        self.banks, self.n, self.read = banks, 0, [start] * len(banks)

    def open(self, signal, count):
        i = self.n % len(self.banks)
        former, self.read[i] = self.read[i], (signal, count)
        self.n += 1
        return self.banks[i], former


class Steps:

    def __init__(self, eng, sem):
        self.eng, self.sem, self.n, self.turn, self.size = eng, sem, 0, None, 0

    def __call__(self, instruction):
        self.n += 1
        instruction.then_inc(self.sem, 1)
        value = self.n if self.turn is None else self.turn * self.size + self.n
        self.eng.wait_ge(self.sem, value)


COUNTS_ON = {
    "pc_full": ("conv_full", 8), "pc_stored": ("conv_stored", 8), "qkvr_full": ("v_full", 8), "qkvr_stored": ("v_stored", 8),
    "ycT_full": ("ynT_full", 4), "rkv_full": ("x_tok_full", 4), "lora_full": ("cb_full", 8), "cum_full": ("row_full", 16),
    "end_full": ("dt_col_full", 1), "ft_full": ("ssd_full", 8), "uq_full": ("z_full", 8), "ukv_full": ("qk_full", 8),
    "w_high_ready": ("dense_high_ready", 44), "w_low_ready": ("dense_low_ready", 44), "xg_high_ready": ("h_high_ready", 24),
    "xg_split": ("h_low_ready", 24), "hid_high_ready": ("w_dt_high", 1), "hid_split": ("w_dt_split", 1),
    "kpe_full": ("dt_full", 1), "rkv_ready": ("x_tok_ready", 4), "wa_sum": ("cb_ready", 8),
}


def total(name, count):
    return count + COUNTS_ON.get(name, (name, 0))[1]


def weight_order():
    w = [("e_in", c) for c in range(12)] + [("e_out", c) for c in range(4)]
    for c in range(FF_TILES // 2):
        w += [("ff_g", c), ("ff_u", c)]
    w += [("ff_d", half, c) for half in range(2) for c in range(6)]
    w += [("o_in", c) for c in range(10)]
    w += [("uq", 0), ("uq", 1), ("ukv", 0)]
    w += [("o_out", c) for c in range(4)]
    return w


def split_tiles():
    return [[n for n, item in enumerate(weight_order()) if item[0] in kinds] for kinds in SPLIT_PHASES]


def splits_before(n):
    return sum(m < n for phase in split_tiles() for m in phase)


def phase_splits(phase):
    first = sum(len(tiles) for tiles in split_tiles()[:phase])
    return first, first + len(split_tiles()[phase]) - 1


def expert_order():
    w = [("g", 0), ("u", 0)]
    for j in range(1, GROUPS_E):
        w += [("g", j), ("u", j), ("d", j - 1)]
    return w + [("d", GROUPS_E - 1)]


def last_use(item):
    kind, c = item[0], item[-1]
    if kind == "e_in":
        name, per, first = [("qk_full", 2, 0), ("v_full", 4, 4), ("z_full", 4, 6), ("conv_full", 2, 8)][
            0 if c < 4 else 1 if c < 6 else 2 if c < 8 else 3]
        return name, per * (c - first + 1)
    if kind == "o_in":
        return ("pc_full", 2 * (c + 1)) if c < 7 else ("qkvr_full", 4 * (c - 6))
    if kind in ("e_out", "o_out"):
        return "mix_full", 4 * (c + 1) + (16 if kind == "o_out" else 0)
    if kind in ("ff_g", "ff_u"):
        return ("gate_full" if kind == "ff_g" else "up_full"), 2 * (c + 1)
    if kind == "ff_d":
        return ("down_used", 5 * item[1] + c + 1) if c < 5 else ("down_full", 4 * (item[1] + 1))
    return {"uq": ("uq_full", 4 * (c + 1)), "ukv": ("ukv_full", 12)}[kind]


def expert_tile_used(n):
    kind, j = expert_order()[n]
    name, done = {"g": ("gate_full", FF_TILES), "u": ("up_full", FF_TILES), "d": ("down_used", 10)}[kind]
    return name, done + j + 1 - (0 if n >= 0 else GROUPS_E)


class Ring:

    def __init__(self, slots, landed, before=None, turn=None, size=0):
        self.slots, self.landed, self.before = slots, landed, before or [0] * len(slots)
        self.n, self.turn, self.size = 0, turn, size
        assert size % len(slots) == 0

    def load(self, eng, view, source):
        slot = self.n % len(self.slots)
        eng.dma_start(view(self.slots[slot]), source).then_inc(self.landed[slot], 16)
        self.n += 1

    def take(self):
        slot = self.n % len(self.slots)
        value = 16 * (self.before[slot] + self.n // len(self.slots) + 1)
        if self.turn is not None:
            value = self.turn * (16 * self.size // len(self.slots)) + value
        self.n += 1
        return self.slots[slot], (self.landed[slot], value)


def expert_ring(slots, landed, turn):
    n = len(weight_order())
    return Ring(slots, landed[:RAW], [len(range(i, n, DENSE_RAW)) if i < DENSE_RAW else 0 for i in range(RAW)], turn, TILES_E)


def hybrid_trunk(nc, x, positions, e_norm_mix, e_w_in, a_rel_bias, b_conv_w, b_conv_b, b_dt_bias,
                 b_a_log, b_d_skip, b_norm_w, e_w_out, e_norm_ffn, ff_w_gate, ff_w_up, ff_w_down,
                 o_norm_mix, o_w_in, c_mu, c_w0, c_w2, c_a0, c_a2, c_g2, c_k_k, c_k_a, c_r_k,
                 c_ln_w, c_ln_b, d_q_norm, d_w_uq, d_kv_norm, d_w_ukv, o_w_out, o_norm_ffn,
                 moe_router, moe_w_gate, moe_w_up, moe_w_down, final_norm, out, dbg=None, upto=99):
    ctx = ExitStack()
    with ctx:
        def sb(name, shape, dt=F32):
            return ctx.enter_context(nc.sbuf_tensor(name, shape, dt))

        sems, bank = {}, {}

        def sem(name):
            name = COUNTS_ON.get(name, (name,))[0]
            if name not in sems:
                sems[name] = ctx.enter_context(nc.semaphore(name))
            return sems[name]

        slots, slot_at = [], []
        for i in range(SLOTS):
            slots.append(sb(f"slot{i}", [P, SLOT]))
            slot_at.append(nc.sbuf_base - 4 * SLOT)
        xs = sb("xs", [P, NT, D])
        ident = sb("ident", [P, P])
        flip = sb("flip", [P, P])
        chunk_mask = sb("chunk_mask", [P, P])
        causal_mask = sb("causal_mask", [P, P])
        cum_incl = sb("cum_incl", [P, P])
        cum_excl = sb("cum_excl", [P, P])
        cum_rev = sb("cum_rev", [P, P])
        chunk_sum = sb("chunk_sum", [P, 2])
        before = sb("before", [P, P])
        ones = sb("ones", [P, P])
        pair_mask = sb("pair_mask", [P, 2, CHUNK])
        level_mask = sb("level_mask", [P, 6, CHUNK])
        level_one = sb("level_one", [P, CHUNK])
        eye64 = sb("eye64", [P, CHUNK])
        slot_no = sb("slot_no", [P, CAP])
        vec_rows = sb("vec_rows", [P, P])
        vc = sb("vc", [P, 95])
        w_dt = sb("w_dt", [P, KT, HEADS])
        w_dt_high, w_dt_low = sb("w_dt_high", [P, KT, HEADS], F32R), sb("w_dt_low", [P, KT, HEADS], F32R)
        w_router = sb("w_router", [P, KT, N_EXPERTS])
        lora = sb("lora", [P, 2, C_WIDTH])
        small = sb("small", [P, 256])
        small_i = sb("small_i", [P, 16], I32)
        expert_lt = sb("expert_lt", [P, N_EXPERTS, N_EXPERTS])
        cand = sb("cand", [P, 3, CANDIDATES])
        turn_off = sb("turn_off", [P, MAX_TURNS + 1])
        turn_ends = sb("turn_ends", [P, 3])
        idle = sb("idle", [P, 3])
        turn_expert_i = sb("turn_expert_i", [P, MAX_TURNS + 1], I32)
        turn_ends_i = sb("turn_ends_i", [P, 3], I32)

        ARENA = 30600
        arena = sb("arena", [P, ARENA])
        arena_at = nc.sbuf_base - 4 * ARENA

        def rounded(name, at, *shape):
            return nc.alloc_sbuf_tensor_at(name, [P, *shape], F32R, offset=at)

        def region(at, *shape, rows=P):
            n = math.prod(shape)
            assert at + n <= ARENA, (at, shape)
            v = arena[0:rows, at:at + n]
            if len(shape) == 2:
                v = v.rearrange("p (a b) -> p a b", b=shape[1])
            if len(shape) == 3:
                v = v.rearrange("p (a b c) -> p a b c", b=shape[1], c=shape[2])
            return v

        head_row = lora[0:HEADS, :, :].rearrange("p a b -> p (a b)").rearrange("p (a b) -> p a b", b=P)
        hT = region(0, KT, SEQ)
        xn = region(4096, NT, D)
        yT = region(4096, KT, SEQ)
        qT, kT = region(8192, 4, SEQ), region(10240, 4, SEQ)
        v_a, zs = region(12288, NT, C_WIDTH), region(14336, NT, B_WIDTH)
        bias_w = region(16384, HEADS, SEQ)
        conv_in = region(20480, CONV_TILES, SEQ + B_CONV - 1)
        conv_out = region(24600, CONV_TILES, SEQ)
        probs = region(28696, 3, SEQ)
        probsT = [region(2048 * i, NT, SEQ) for i in range(2)]
        bias_ext = region(24600, 640, rows=HEADS)
        x_tok, xdt = region(8192, NT, B_WIDTH), region(10240, NT, B_WIDTH)
        y_tok, cbT = region(12288, NT, B_WIDTH), region(16384, B_GROUPS, NT, SEQ)
        decay = [region(20480 + 2048 * i, NT, SEQ) for i in range(2)]
        wT = [region(24600 + 2048 * i, NT, SEQ) for i in range(2)]
        dt_row = [region(28696 + 512 * i, SEQ, rows=HEADS) for i in range(3)]
        sqd = region(0, D)
        hid = region(8192, FF_TILES, SEQ)
        sil = region(19456, 2, SEQ)
        BC = 27000
        bc = {n: region(BC + 512 * i, C_WIDTH) for i, n in enumerate(["w0", "a0", "k_k", "k_a", "r_k", "ln_w", "ln_b"])}
        pcT = region(8192, C_TILES, SEQ + 1)
        qkvr = region(15376, NT, QKVR)
        rw = 18064
        mixdiff = region(rw, 2, SEQ)
        free_rows = list(range(0, 4096, 512)) + list(range(6144, 8192, 512)) + list(range(rw, BC - 511, 512))
        R, F = {}, {}
        F["ar"] = arena[:, 0:1024].rearrange("p (a b c) -> p a b c", b=2, c=P)
        F["ab"] = arena[:, 1024:2048].rearrange("p (a b) -> p a b", b=P)
        F["ak"] = arena[:, 2048:3072].rearrange("p (a b) -> p a b", b=P)
        names = ["r", "k", "v", "sig", "a", "g", "kk", "b", "Eex", "Ein", "Eni", "Erev", "al", "rt", "bt", "kt", "bh", "kh", "tmp",
                 "btT", "ktT", "state"]
        for i, name in enumerate(names):
            R[name] = region(free_rows[6 + i], C_WIDTH)
        for name, former in (("X", "Eex"), ("XT", "Ein"), ("Y1", "Eni"), ("ot0", "Erev"), ("ot1", "r"), ("Z1", "rt"), ("U", "bt"),
                             ("SA", "kt"), ("y", "k"), ("A", "a")):
            R[name] = R[former]
        for name in ("btT", "ktT"):
            F[name] = R[name].rearrange("p (a b) -> p a b", b=P)
        F["wt"] = R["sig"].rearrange("p (a b) -> p a b", b=P)
        state = [R["state"][:, 256 * i:256 * (i + 1)].rearrange("p (a b) -> p a b", b=HD) for i in range(2)]

        q_tok = region(8192, NT, HEADS, QD)
        qT_d = region(18064, HEADS, SEQ, rows=QD)
        kT_d = region(22160, HEADS, SEQ, rows=QD)
        v_d = region(11264, NT, C_WIDTH)
        qnT, kvnT = region(26256, 3, SEQ), region(13312, 2, SEQ)
        rope_cs = region(14336, 16, 16)
        E0 = 8192
        pick = region(E0, NT, CAP)
        pick_g = region(E0 + 672, NT, CAP)
        pickT = region(E0 + 1344, 2, SEQ)
        xgT = region(E0 + 2368, KT, CAP)
        sil_e = region(E0 + 3712, 2, 2 * CAP)
        hid_e = region(E0 + 4384, 2, 2 * CAP)
        outT = region(E0 + 5056, KT, CAP)
        out_tok = region(E0 + 6400, 2, D)
        final_w = region(E0 + 8448, D)
        y_out = region(E0 + 9472, NT, D)
        M0 = E0 + 13568
        logit, ex, gate, place, rank, sel = [region(M0 + 32 * i, NT, N_EXPERTS) for i in range(6)]
        same, more = [region(M0 + 256 * (1 + i), NT, N_EXPERTS * N_EXPERTS).rearrange("p t (e j) -> p t e j", j=N_EXPERTS)
                      for i in range(2)]
        top = region(M0 + 1024, NT)
        own_place = region(M0 + 1028, NT)
        key, pos, key_tmp = [region(M0 + 1040 + 32 * i, CANDIDATES) for i in range(3)]
        rivals = region(M0 + 1200, CANDIDATES, CANDIDATES)
        at_turn = [region(M0 + 2300 + 544 * i, MAX_TURNS + 1, CANDIDATES) for i in range(3)]
        w_high = [rounded(f"w_high{i}", at, SLOT) for i, at in enumerate((slot_at[3], slot_at[4], arena_at))]
        w_low = [rounded(f"w_low{i}", at, SLOT) for i, at in enumerate((slot_at[5], slot_at[6], arena_at + 4 * SLOT))]
        raw_slots = slots[:3] + [region(E0 + 9472 + SLOT * i, SLOT) for i in range(2)] + [region(M0 + 1200, SLOT)]
        S0 = 25600
        assert M0 + 1200 + SLOT <= S0 and len(raw_slots) == RAW
        xg_high, xg_low = rounded("xg_high", arena_at + 4 * S0, KT, P), rounded("xg_low", arena_at + 4 * (S0 + 1024), KT, P)
        hid_tok = region(S0 + 2048, 2, 2 * P)
        hid_high = rounded("hid_high", arena_at + 4 * (S0 + 2560), 2, 2, P)
        hid_low = rounded("hid_low", arena_at + 4 * (S0 + 3072), 2, 2, P)
        h_high, h_low = rounded("h_high", arena_at + 4 * 4096, KT, SEQ), rounded("h_low", arena_at, KT, SEQ)
        ones_row, dt_keep = region(6144, SEQ, rows=HEADS), region(6656, SEQ, rows=HEADS)

        banks = [ctx.enter_context(nc.psum_tensor(f"bank{i}", [P, 512], F32)) for i in range(8)]
        turn_banks, acc = banks[0:4], banks[4:8]

        ext_d = nc.dram_tensor("bias_ext_d", [HEADS, 640], F32)

        def cols8(dram, lo, n):
            return dram[:, lo:lo + n].rearrange("(k p) n -> p k n", p=P)

        def pair_of(view, cap):
            return view.rearrange("p (a b) -> p a b", b=CAP)[:, :, 0:cap]

        landed = [sem(f"landed{i}") for i in range(SLOTS)]

        block = ctx.enter_context(nc.Block())

        @block.sync
        def _(sp):
            w = Ring(slots[:DENSE_RAW], landed[:DENSE_RAW])
            xv = x[0].rearrange("(t p) d -> p t d", p=P)
            for t in range(NT):
                sp.dma_start(xs[:, t, :], xv[:, t, :]).then_inc(sem("x_loaded"), 16)
            row = 0
            for dram, n in ((e_norm_mix, 8), (e_norm_ffn, 8), (o_norm_mix, 8), (o_norm_ffn, 8), (b_conv_b, 8)):
                sp.dma_start(vec_rows[row:row + n, :], dram[0].rearrange("(k p) -> k p", p=P)).then_inc(sem("vec_loaded"), 16)
                row += n
            for tap in range(B_CONV):
                sp.dma_start(vec_rows[row:row + 8, :], b_conv_w[0, tap].rearrange("(k p) -> k p", p=P)).then_inc(sem("vec_loaded"), 16)
                row += 8
            for dram, n in ((c_mu, 14), (d_q_norm, 3), (d_kv_norm, 2), (b_norm_w, 4)):
                sp.dma_start(vec_rows[row:row + n, :], dram[0].rearrange("(k p) -> k p", p=P)).then_inc(sem("vec_loaded"), 16)
                row += n
            assert row == 95

            def load(kind, *c):
                if kind in ("e_in", "o_in", "e_out", "o_out", "ff_g", "ff_u"):
                    dram = {"e_in": e_w_in, "o_in": o_w_in, "e_out": e_w_out, "o_out": o_w_out,
                            "ff_g": ff_w_gate, "ff_u": ff_w_up}[kind]
                    n = min(256, dram.shape[2] - 256 * c[0])
                    w.load(sp, lambda s: s[:, 0:KT * n].rearrange("p (k n) -> p k n", n=n),
                           cols8(dram[0], 256 * c[0], n))
                elif kind == "ff_d":
                    half, j = c
                    n = min(4, FF_TILES - 4 * j)
                    w.load(sp, lambda s: s[:, 0:n * 512].rearrange("p (k n) -> p k n", n=512),
                           ff_w_down[0, 4 * j * P:(4 * j + n) * P, 512 * half:512 * half + 512]
                           .rearrange("(k p) n -> p k n", p=P))
                elif kind == "uq":
                    w.load(sp, lambda s: s[:, 0:3 * 384].rearrange("p (k n) -> p k n", n=384),
                           cols8(d_w_uq[0], 384 * c[0], 384))
                elif kind == "ukv":
                    w.load(sp, lambda s: s[:, :].rearrange("p (k n) -> p k n", n=1024),
                           cols8(d_w_ukv[0], 0, 1024))

            order = weight_order()
            last_item = {1: ("e_in", 11), 2: ("e_out", 3), 3: ("ff_d", 1, 5), 4: ("o_in", 9)}.get(upto)
            for n, item in enumerate(order):
                if item == ("ff_d", 0, 0):
                    sp.wait_ge(sem("mix_full"), 16)
                    sp.dma_start(lora[0:64, 0, :], c_w2[0]).then_inc(sem("lora_loaded"), 16)
                    sp.dma_start(lora[64:128, 0, :], c_a2[0]).then_inc(sem("lora_loaded"), 16)
                    sp.dma_start(lora[:, 1, :], c_g2[0]).then_inc(sem("lora_loaded"), 16)
                    for i, dram in enumerate((c_w0, c_a0, c_k_k, c_k_a, None, c_ln_w, c_ln_b)):
                        src = dram[0:1, :] if dram is not None else c_r_k[0:1].rearrange("a h d -> a (h d)")
                        sp.dma_start(region(BC + 512 * i, C_WIDTH), src.to_broadcast([P, C_WIDTH])).then_inc(sem("bc_loaded"), 16)
                if n >= DENSE_RAW:
                    former = n - DENSE_RAW
                    if splits_before(former + 1) > splits_before(former):
                        sp.wait_ge(sem("dense_low_ready"), splits_before(former + 1))
                    else:
                        name, count = last_use(order[former])
                        sp.wait_ge(sem(name), total(name, count))
                load(*item)
                if item == last_item:
                    break
            if upto >= 6:
                sp.wait_ge(sem("mix_full"), 32)
                sp.dma_start(final_w, final_norm.rearrange("(a n) -> a n", a=1).to_broadcast([P, D])).then_inc(sem("final_loaded"), 16)
                sp.wait_ge(sem("turns_ready"), 1)
                ends = [sp.value_load(turn_ends_i[0:1, i:i + 1], min_val=i + 1, max_val=MAX_TURNS) for i in range(len(CAPS))]

                def expert(turn, split):
                    e = sp.value_load(turn_expert_i[0:1, bass.ds(turn, 1)], min_val=0, max_val=N_EXPERTS - 1)
                    ring = expert_ring(raw_slots, landed, turn)
                    for n, (kind, j) in enumerate(expert_order()):
                        if split:
                            sp.wait_ge(sem("w_low_ready"), turn * TILES_E + total("w_low_ready", n + 1))
                        else:
                            if n == RAW:
                                sp.wait_ge(sem("splits_over"), 1)
                            name, count = expert_tile_used(n - RAW)
                            sp.wait_ge(sem(name), turn * GROUPS_E + count)
                        if kind in ("g", "u"):
                            dram = moe_w_gate if kind == "g" else moe_w_up
                            ring.load(sp, lambda s: s[:, :].rearrange("p (k n) -> p k n", n=256),
                                      dram[0, bass.ds(e, 1), :, 256 * j:256 * j + 256].rearrange("a (k p) n -> p (a k) n", p=P))
                        else:
                            ring.load(sp, lambda s: s[:, :].rearrange("p (k n) -> p k n", n=D),
                                      moe_w_down[0, bass.ds(e, 1), 256 * j:256 * j + 256, :].rearrange("a (k p) n -> p (a k) n", p=P))

                with sp.Fori(0, ends[0]) as turn:
                    expert(turn, True)
                with sp.Fori(ends[0], ends[2]) as turn:
                    expert(turn, False)
                sp.wait_ge(sem("y_ready"), NT)
                sp.dma_start(out[0].rearrange("(t p) d -> p t d", p=P), y_out).then_inc(sem("stored"), 16)
                sp.wait_ge(sem("stored"), 16)

        @block.gpsimd
        def _(pool):
            link = Steps(pool, sem("pool_step"))

            def select(view, op, fill, base, pattern, mult):
                link(pool.affine_select(out=view, in_=view, compare_op=op, fill=fill, base=base,
                                        pattern=pattern, channel_multiplier=mult))

            link(pool.memset(ident[:, :], 0.0))
            pool.affine_select(out=ident[:, :], in_=ident[:, :], compare_op=ALU.not_equal, fill=1.0, base=0,
                               pattern=[[-1, P]], channel_multiplier=1).then_inc(sem("ident_ready"), 1)
            for k in range(KT):
                pool.dma_start(w_dt[:, k, :], e_w_in[0, k * P:(k + 1) * P, DT_COL:DT_COL + HEADS]).then_inc(sem("w_dt_loaded"), 16)
            pool.dma_start(w_router[:, :, :], moe_router[0].rearrange("(k p) e -> p k e", p=P)).then_inc(sem("router_loaded"), 16)
            pool.dma_start(small[0:HEADS, 0:1], b_dt_bias[0].rearrange("(h a) -> h a", a=1)).then_inc(sem("small_loaded"), 16)
            pool.dma_start(small[0:HEADS, 1:2], b_a_log[0].rearrange("(h a) -> h a", a=1)).then_inc(sem("small_loaded"), 16)
            pool.dma_start(small[:, 8:16], b_d_skip[0:1, :].to_broadcast([P, HEADS])).then_inc(sem("small_loaded"), 16)
            pool.dma_start(small_i[:, 0:NT], positions[0].rearrange("(t p) -> p t", p=P),
                           allow_slow_non_contiguous=True).then_inc(sem("small_loaded"), 16)

            pool.dma_start(bias_ext[:, 0:384], a_rel_bias[0, :, 129:513]).then_inc(sem("rel_loaded"), 16)
            pool.wait_ge(sem("rel_loaded"), 16)
            link(pool.tensor_copy(bias_ext[:, 384:640], bias_ext[:, 383:384].to_broadcast([HEADS, 256])))
            pool.dma_start(ext_d[:, :], bias_ext).then_inc(sem("rel_stored"), 16)
            pool.wait_ge(sem("rel_stored"), 16)
            for h in range(HEADS):
                src = bass.AP(ext_d, 640 * h, [[1, P], [1, SEQ]])
                pool.dma_start(bias_w[:, h, :], src).then_inc(sem("bias_loaded"), 16)

            link(pool.memset(flip[:, :], 0.0))
            select(flip[:, :], ALU.not_equal, 1.0, -(P - 1), [[1, P]], 1)
            link(pool.memset(chunk_mask[:, :], 0.0))
            link(pool.memset(chunk_mask[0:CHUNK, CHUNK:P], MASKED))
            link(pool.memset(causal_mask[:, :], 0.0))
            select(causal_mask[:, :], ALU.is_ge, MASKED, 0, [[1, P]], -1)
            link(pool.memset(ones[:, :], 1.0))
            link(pool.memset(before[:, :], 1.0))
            select(before[:, :], ALU.is_gt, 0.0, 0, [[1, P]], -1)
            for m, op, sign in ((cum_incl, ALU.is_ge, 1), (cum_excl, ALU.is_gt, 1), (cum_rev, ALU.is_gt, -1)):
                link(pool.memset(m[:, :], DECAY_RATE))
                select(m[:, :], op, 0.0, 0, [[sign, P]], -sign)
                if sign > 0:
                    link(pool.memset(m[0:CHUNK, CHUNK:P], 0.0))
                else:
                    link(pool.memset(m[CHUNK:P, 0:CHUNK], 0.0))
            link(pool.memset(chunk_sum[:, :], 0.0))
            for c in range(2):
                link(pool.memset(chunk_sum[CHUNK * c:CHUNK * (c + 1), c:c + 1], DECAY_RATE))
            link(pool.memset(pair_mask[:, :, :], 1.0))
            link(pool.memset(level_mask[:, :, :], 1.0))
            link(pool.memset(level_one[:, :], 1.0))
            link(pool.memset(eye64[:, :], 0.0))
            for c in range(2):
                rows = slice(CHUNK * c, CHUNK * (c + 1))
                select(pair_mask[rows, 0, :], ALU.is_gt, 0.0, 0, [[1, CHUNK]], -1)
                select(pair_mask[rows, 1, :], ALU.is_ge, 0.0, 0, [[1, CHUNK]], -1)
                select(eye64[rows, :], ALU.not_equal, 1.0, 0, [[-1, CHUNK]], 1)
                v = level_one[rows, :].rearrange("p (b c) -> p b c", c=2)
                select(v, ALU.is_equal, 0.0, 0, [[-2, CHUNK // 2], [0, 2]], 1)
                link(pool.memset(v[:, :, 0:1], 0.0))
                for n in range(6):
                    s = 1 << n
                    v = level_mask[rows, n, :].rearrange("p (b c) -> p b c", c=2 * s)
                    link(pool.memset(v[:, :, s:2 * s], 0.0))
                    select(v, ALU.is_ge, 0.0, -s, [[-2 * s, CHUNK // (2 * s)], [0, 2 * s]], 1)
                    select(v, ALU.is_ge, 0.0, 2 * s - 1, [[2 * s, CHUNK // (2 * s)], [0, 2 * s]], -1)
            link(pool.iota(slot_no[:, :], [[1, CAP]], base=0, channel_multiplier=0, allow_small_or_imprecise_dtypes=True))
            iota = dict(base=0, channel_multiplier=0, allow_small_or_imprecise_dtypes=True)
            link(pool.iota(cand[:, 0, :].rearrange("p (r e) -> p r e", e=N_EXPERTS), [[0, MAX_ROUNDS], [1, N_EXPERTS]], **iota))
            link(pool.iota(cand[:, 1, :].rearrange("p (r e) -> p r e", e=N_EXPERTS), [[CAP, MAX_ROUNDS], [0, N_EXPERTS]], **iota))
            link(pool.iota(cand[:, 2, :], [[1, CANDIDATES]], **iota))
            link(pool.memset(expert_lt[:, :, :], 1.0))
            select(expert_lt[:, :, :], ALU.is_gt, 0.0, 0, [[1, N_EXPERTS], [-1, N_EXPERTS]], 0)
            link(pool.memset(head_row[:, :, :], 0.0))
            select(head_row[:, :, :], ALU.not_equal, 1.0, 0, [[-1, HEADS], [0, P]], 1)
            pool.memset(conv_in[:, :, 0:B_CONV - 1], 0.0).then_inc(sem("const_ready"), 1)


        @block.tensor
        def _(pe):
            w = Ring(slots[:DENSE_RAW], landed[:DENSE_RAW])
            turn_bank = Banks(turn_banks, (sem("ident_ready"), 1))

            def tile(name, count):
                bank[name, count], former = turn_bank.open(sem(name), total(name, count))
                return bank[name, count], former

            def mm(o, lhsT, rhs, start):
                return pe.matmul(o, lhsT, rhs, start=start, stop=True, skip_group_check=True)

            def tp(o, i, rows=P):
                return pe.transpose(o, i, ident[0:rows, 0:rows])

            def norm(j):
                for t in range(NT):
                    pe.wait_ge(sem("xn_ready"), NT * j + t + 1)
                    for half in range(2):
                        b, former = tile("hT_ready", 8 * j + 2 * t + half + 1)
                        pe.wait_ge(*former)
                        for k in range(4):
                            m = tp(b[:, P * k:P * (k + 1)], xn[:, t, P * (4 * half + k):P * (4 * half + k + 1)])
                        m.then_inc(sem("xnT_full"), 1)
                pe.wait_ge(sem("hT_ready"), 8 * (j + 1))

            def by_feature(slab, cols, rhs, o, kt=KT, fresh=True):
                for k in range(kt):
                    m = mm(o, slab[:, k, cols], rhs[:, k, :], fresh and k == 0)
                return m

            def by_token(lhs, t, slab, o, kt=KT):
                for k in range(kt):
                    m = mm(o, lhs[:, k, P * t:P * (t + 1)], slab[:, k, :], k == 0)
                return m

            def split_product(o, left, right, start):
                mm(o, left[0], right[0], start)
                mm(o, left[0], right[1], False)
                return mm(o, left[1], right[0], False)

            def split_slab(n=256):
                s = splits_before(w.n)
                w.n += 1
                parts = [v[s % DENSE_SPLIT][:, 0:KT * n].rearrange("p (k n) -> p k n", n=n) for v in (w_high, w_low)]
                return parts, (sem("dense_low_ready"), s + 1)

            def by_feature_split(parts, cols, o, phase=None):
                for k in range(KT):
                    if phase is not None:
                        pe.wait_ge(sem("h_low_ready"), KT * phase + k + 1)
                    m = split_product(o, [v[:, k, cols] for v in parts], (h_high[:, k, :], h_low[:, k, :]), k == 0)
                return m

            def by_token_split(parts, t, o):
                for k in range(KT):
                    m = split_product(o, [v[:, k, P * t:P * (t + 1)] for v in (h_high, h_low)], [v[:, k, :] for v in parts], k == 0)
                return m

            def slab_of(n=256, kt=KT):
                slot, here = w.take()
                return slot[:, 0:kt * n].rearrange("p (k n) -> p k n", n=n), here

            def attention(first, score, value, done):
                for i in range(HEADS * NT + 2):
                    if i < HEADS * NT:
                        b, former = tile("probs_ready", first + i + 1)
                        pe.wait_ge(*former)
                        score(b, i // NT, i % NT).then_inc(sem("scores_full"), 1)
                    u = i - 2
                    if u < 0:
                        continue
                    h, t = divmod(u, NT)
                    pe.wait_ge(sem("probs_scaled"), first + u + 1)
                    b, former = tile("probsT_ready", first + u + 1)
                    pe.wait_ge(*former)
                    for k in range(t + 1):
                        m = tp(b[:, P * k:P * (k + 1)], probs[:, u % 3, P * k:P * (k + 1)])
                    m.then_inc(sem("probsT_full"), 1)
                    if t == NT - 1:
                        pe.wait_ge(sem("probsT_ready"), first + u + 1)
                        pair = h // 2
                        if h % 2 == 0 and pair >= 2:
                            pe.wait_ge(sem("yT_ready"), done + pair - 1)
                        rows = slice(64 * (h % 2), 64 * (h % 2) + 64)
                        for k in range(NT):
                            m = mm(acc[pair % 2][rows, P * k:], value(h, k), probsT[h % 2][:, k, P * k:], k == 0)
                        m.then_inc(sem("pv_done"), 1)

            def out_proj(base):
                for c in range(4):
                    slab, here = slab_of()
                    pe.wait_ge(*here)
                    for t in range(NT):
                        b, former = tile("x_added", base + 4 * c + t + 1)
                        pe.wait_ge(*former)
                        by_token(yT, t, slab, b[:, 0:256]).then_inc(sem("mix_full"), 1)

            pe.wait_ge(sem("ident_ready"), 1)
            pe.wait_ge(sem("vec_loaded"), 16 * 13)
            b, former = tile("vc_ready", 1)
            pe.wait_ge(*former)
            tp(b[:, 0:95], vec_rows[0:95, :], 95).then_inc(sem("vec_full"), 1)

            norm(0)
            for c in range(12):
                parts, here = split_slab()
                pe.wait_ge(*here)
                if c < 4 or c >= 8:
                    full, stored = ("qk_full", "qk_stored") if c < 4 else ("conv_full", "conv_stored")
                    for m in range(2):
                        b, former = tile(stored, 2 * (c % 8) + m + 1)
                        pe.wait_ge(*former)
                        by_feature_split(parts, slice(P * m, P * (m + 1)), b[:, :], 0 if c == m == 0 else None).then_inc(sem(full), 1)
                else:
                    full, stored = ("v_full", "v_stored") if c < 6 else ("z_full", "z_stored")
                    for t in range(NT):
                        b, former = tile(stored, 4 * (c % 2) + t + 1)
                        pe.wait_ge(*former)
                        by_token_split(parts, t, b[:, 0:256]).then_inc(sem(full), 1)
            pe.wait_ge(sem("w_dt_split"), 1)
            b, former = tile("u_ready", 1)
            pe.wait_ge(*former)
            by_feature_split((w_dt_high, w_dt_low), slice(0, HEADS), b[0:HEADS, :]).then_inc(sem("dt_full"), 1)

            if upto >= 2:
                pe.wait_ge(sem("const_ready"), 1)
                pe.wait_ge(sem("bias_loaded"), 16 * HEADS)
                pe.wait_ge(sem("qk_stored"), 8)
                pe.wait_ge(sem("v_stored"), 8)

                def score_a(b, h, t):
                    rows = slice(64 * (h % 2), 64 * (h % 2) + 64)
                    mm(b[:, 0:P * (t + 1)], qT[rows, h // 2, P * t:P * (t + 1)], kT[rows, h // 2, 0:P * (t + 1)], True)
                    for k in range(t + 1):
                        mm(b[:, P * k:P * (k + 1)], bias_w[:, h, P * (t - k):P * (t - k + 1)], flip[:, :], False)
                    return mm(b[:, P * t:P * (t + 1)], ident[:, :], chunk_mask[:, :], False)

                attention(0, score_a, lambda h, k: v_a[:, k, HD * h:HD * (h + 1)], 0)

                pe.wait_ge(sem("conv_ready"), CONV_TILES)
                for t in range(NT):
                    b, former = tile("x_tok_ready", t + 1)
                    pe.wait_ge(*former)
                    for c in range(4):
                        m = tp(b[:, P * c:P * (c + 1)], conv_out[:, c, P * t:P * (t + 1)])
                    m.then_inc(sem("x_tok_full"), 1)
                for g in range(B_GROUPS):
                    for j in range(NT):
                        b, former = tile("cb_ready", NT * g + j + 1)
                        pe.wait_ge(*former)
                        mm(b[:, P * j:], conv_out[:, 4 + g, P * j:P * (j + 1)], conv_out[:, 6 + g, P * j:], True)\
                            .then_inc(sem("cb_full"), 1)
                pe.wait_ge(sem("cum_ready"), 1)
                b, former = tile("dt_col_ready", 1)
                pe.wait_ge(*former)
                for j in range(NT):
                    tp(b[:, HEADS * j:HEADS * (j + 1)], dt_row[2][:, P * j:P * (j + 1)], HEADS)
                    m = tp(b[:, 32 + HEADS * j:32 + HEADS * (j + 1)], dt_row[0][:, P * j:P * (j + 1)], HEADS)
                m.then_inc(sem("dt_col_full"), 1)
                for h in range(HEADS + 1):
                    if h < HEADS:
                        for masked in range(2):
                            b, former = tile("decay_ready", 7 * h + (7 if masked else 5))
                            pe.wait_ge(*former)
                            m = mm(b[:, :], head_row[:, h, :], dt_row[1], True)
                            if masked:
                                for j in range(NT):
                                    m = mm(b[:, P * j:P * (j + 1)], ident[:, :], causal_mask[:, :], False)
                            m.then_inc(sem("row_full"), 1)
                    if h >= 1:
                        g = h - 1
                        pe.wait_ge(sem("w_ready"), NT * (g + 1))
                        b, former = tile("y_tok_ready", g + 1)
                        pe.wait_ge(*former)
                        for l in range(NT):
                            for j in range(l + 1):
                                m = mm(b[:, HD * l:HD * (l + 1)], wT[g % 2][:, j, P * l:P * (l + 1)],
                                       xdt[:, j, HD * g:HD * (g + 1)], l == 0)
                        m.then_inc(sem("ssd_full"), 1)
                for t in range(NT):
                    pe.wait_ge(sem("yn_ready"), 1)
                    b, former = tile("yT_b_ready", t + 1)
                    pe.wait_ge(*former)
                    for c in range(4):
                        m = tp(b[:, P * c:P * (c + 1)], y_tok[:, t, P * c:P * (c + 1)])
                    m.then_inc(sem("ynT_full"), 1)
                pe.wait_ge(sem("yT_ready"), 4)
                pe.wait_ge(sem("yT_b_ready"), 4)
                out_proj(0)

            if upto >= 3:
                norm(1)
                for c in range(FF_TILES // 2):
                    for full, stored in (("gate_full", "sil_ready"), ("up_full", "hid_ready")):
                        parts, here = split_slab()
                        pe.wait_ge(*here)
                        for m in range(2):
                            b, former = tile(stored, 2 * c + m + 1)
                            pe.wait_ge(*former)
                            by_feature_split(parts, slice(P * m, P * (m + 1)), b[:, :],
                                             1 if c == m == 0 and full == "gate_full" else None).then_inc(sem(full), 1)
                pe.wait_ge(sem("hid_ready"), FF_TILES)
                for half in range(2):
                    for c in range(6):
                        n = min(4, FF_TILES - 4 * c)
                        slab, here = slab_of(512, n)
                        pe.wait_ge(*here)
                        for k in range(n):
                            f = 4 * c + k
                            for t in range(NT):
                                if half and f == 0:
                                    pe.wait_ge(sem("x_added"), 16 + t + 1)
                                m = mm(acc[t][:, :], hid[:, f, P * t:P * (t + 1)], slab[:, k, :], f == 0)
                                if f == FF_TILES - 1:
                                    m.then_inc(sem("down_full"), 1)
                        if c < 5:
                            m.then_inc(sem("down_used"), 1)

            if upto >= 4:
                norm(2)
                for c in range(7):
                    parts, here = split_slab()
                    pe.wait_ge(*here)
                    for m in range(2):
                        b, former = tile("pc_stored", 2 * c + m + 1)
                        pe.wait_ge(*former)
                        by_feature_split(parts, slice(P * m, P * (m + 1)), b[:, :], 2 if c == m == 0 else None).then_inc(sem("pc_full"), 1)
                for c in range(3):
                    n = 256 if c < 2 else QKVR - 512
                    parts, here = split_slab(n)
                    pe.wait_ge(*here)
                    for t in range(NT):
                        b, former = tile("qkvr_stored", 4 * c + t + 1)
                        pe.wait_ge(*former)
                        by_token_split(parts, t, b[:, 0:n]).then_inc(sem("qkvr_full"), 1)

                pe.wait_ge(sem("lora_loaded"), 48)
                quad = lambda c: slice(64 * c, 64 * c + 64)
                for t in range(NT):
                    now = slice(1 + P * t, 1 + P * (t + 1))
                    pe.wait_ge(sem("mixed"), C_TILES)
                    for a in range(3):
                        b, former = tile("rkv_ready", 3 * t + a + 1)
                        pe.wait_ge(*former)
                        for k in range(4):
                            m = tp(b[:, P * k:P * (k + 1)], pcT[:, 4 * a + k, now])
                        m.then_inc(sem("rkv_full"), 1)
                    pe.wait_ge(sem("lora_in_ready"), 2)
                    for a in range(2):
                        b, former = tile("wa_sum", 2 * t + a + 1)
                        pe.wait_ge(*former)
                        mm(b[:, :], pcT[quad(a), 12, now], lora[quad(a), 0, :], True).then_inc(sem("lora_full"), 1)
                    b, former = tile("g_ready", t + 1)
                    pe.wait_ge(*former)
                    mm(b[:, :], pcT[:, 13, now], lora[:, 1, :], True).then_inc(sem("lora_full"), 1)
                    pe.wait_ge(sem("sig_ready"), 2 * t + 1)
                    for i, tri in enumerate((cum_excl, cum_incl, cum_rev)):
                        b, former = tile("exp_ready", 4 * t + (1, 3, 4)[i])
                        pe.wait_ge(*former)
                        mm(b[:, :], tri[:, :], R["sig"], True).then_inc(sem("cum_full"), 1)
                    b, former = tile("end_ready", t + 1)
                    pe.wait_ge(*former)
                    for k in range(4):
                        m = mm(b[:, 2 * k:2 * k + 2], R["sig"][:, P * k:P * (k + 1)], chunk_sum[:, :], k == 0)
                    m.then_inc(sem("end_full"), 1)
                    for i, name in enumerate(("al", "rt", "bt", "kt")):
                        pe.wait_ge(sem("scaled_ready"), 6 * t + i + 1)
                        b, former = tile("ft_ready", 4 * t + i + 1)
                        pe.wait_ge(*former)
                        for k in range(4):
                            m = tp(b[:, P * k:P * (k + 1)], R[name][:, P * k:P * (k + 1)])
                        m.then_inc(sem("ft_full"), 1)
                    pe.wait_ge(sem("ft_ready"), 4 * (t + 1))
                    for i, lhs in enumerate(("btT", "ktT")):
                        for par in range(2):
                            b, former = tile("pm_ready", 6 * t + 2 * i + par + 1)
                            pe.wait_ge(*former)
                            for pair in range(4):
                                for c in range(2):
                                    m = mm(b[quad(c), P * pair:P * (pair + 1)], F[lhs][quad(par), pair, quad(c)],
                                           F["ar"][quad(par), pair, c, :], pair == 0)
                            m.then_inc(sem("pm_full"), 1)
                    for par in range(2):
                        b, former = tile("pm_ready", 6 * t + 5 + par)
                        pe.wait_ge(*former)
                        for pair in range(4):
                            for c in range(2):
                                m = mm(b[quad(c), HD * pair:HD * (pair + 1)], F["ar"][quad(par), pair, c, 0:CHUNK],
                                       F["btT"][quad(par), pair, quad(c)], pair == 0)
                        m.then_inc(sem("pm_full"), 1)

                    def each(b, lhs, rhs):
                        for h in range(HEADS):
                            for c in range(2):
                                m = mm(b[quad(c), HD * h:HD * (h + 1)], lhs(h, c), rhs(h, c), h == 0)
                        return m

                    def at(name):
                        return lambda h, c: R[name][quad(c), HD * h:HD * (h + 1)]

                    for n in range(5):
                        if n == 0:
                            pe.wait_ge(sem("inv_ready"), t + 1)
                        else:
                            pe.wait_ge(sem("dx_used"), 9 * t + 2 * n)
                        b, former = tile("y1_ready", 5 * t + n + 1)
                        pe.wait_ge(*former)
                        each(b, at(f"ot{n % 2}"), at("X")).then_inc(sem("y1_full"), 1)
                        pe.wait_ge(sem("y1_ready"), 5 * t + n + 1)
                        b, former = tile("dx_used", 9 * t + 2 * n + 1)
                        pe.wait_ge(*former)
                        each(b, at("XT"), at("Y1")).then_inc(sem("dx_full"), 1)
                        if n < 4:
                            b, former = tile("dx_used", 9 * t + 2 * n + 2)
                            pe.wait_ge(*former)
                            each(b, at("Y1"), at("XT")).then_inc(sem("dx_full"), 1)
                    b, former = tile("z_ready", 4 * t + 1)
                    pe.wait_ge(*former)
                    each(b, lambda h, c: F["ak"][quad(c), h, 0:CHUNK], at("v")).then_inc(sem("zu_full"), 1)
                    pe.wait_ge(sem("dx_used"), 9 * t + 9)
                    pe.wait_ge(sem("z_ready"), 4 * t + 1)
                    b, former = tile("z_ready", 4 * t + 2)
                    pe.wait_ge(*former)
                    each(b, at("X"), at("Z1")).then_inc(sem("zu_full"), 1)
                    for c in range(2):
                        b, former = tile("z_ready", 4 * t + 3 + c)
                        pe.wait_ge(*former)
                        for h in range(HEADS):
                            m = mm(b[quad(h % 2), CHUNK * (h // 2):CHUNK * (h // 2 + 1)], at("al")(h, c), at("X")(h, c), h < 2)
                        m.then_inc(sem("zu_full"), 1)
                    pe.wait_ge(sem("z_ready"), 4 * t + 4)
                    pe.wait_ge(sem("scaled_ready"), 6 * t + 6)
                    for c in range(2):
                        n = 2 * t + c
                        S = state[n % 2]
                        pe.wait_ge(sem("state_ready"), n + 1)
                        for par in range(2):
                            b, former = tile("y_stored", 2 * n + par + 1)
                            pe.wait_ge(*former)
                            for pair in range(4):
                                mm(b[quad(c), HD * pair:HD * (pair + 1)], F["wt"][quad(par), pair, quad(c)],
                                   S[quad(par), pair, :], pair == 0)
                            for pair in range(4):
                                m = mm(b[quad(c), 256 + HD * pair:256 + HD * (pair + 1)], F["ar"][quad(par), pair, c, CHUNK:],
                                       S[quad(par), pair, :], False)
                            m.then_inc(sem("sa_full"), 1)
                        by, former = tile("y_added", n + 1)
                        pe.wait_ge(*former)
                        bs, former = tile("state_ready", n + 2)
                        pe.wait_ge(*former)
                        for h in range(HEADS):
                            mm(bs[quad(h % 2), HD * (h // 2):HD * (h // 2 + 1)], at("kh")(h, c), at("v")(h, c), h < 2)
                        for h in range(HEADS):
                            mm(by[quad(c), HD * h:HD * (h + 1)], F["ak"][quad(c), h, CHUNK:], at("v")(h, c), h == 0)
                        pe.wait_ge(sem("sa_ready"), 2 * n + 2)
                        for h in range(HEADS):
                            m = mm(bs[quad(h % 2), HD * (h // 2):HD * (h // 2 + 1)], at("bh")(h, c), at("SA")(h, c), False)
                        m.then_inc(sem("state_full"), 1)
                        for h in range(HEADS):
                            m = mm(by[quad(c), HD * h:HD * (h + 1)], F["ab"][quad(c), h, CHUNK:], at("SA")(h, c), False)
                        m.then_inc(sem("yc_full"), 1)
                    pe.wait_ge(sem("yc_ready"), t + 1)
                    b, former = tile("ycT_ready", t + 1)
                    pe.wait_ge(*former)
                    for k in range(4):
                        m = tp(b[:, P * k:P * (k + 1)], R["y"][:, P * k:P * (k + 1)])
                    m.then_inc(sem("ycT_full"), 1)

            if upto >= 5:
                for t in range(NT):
                    pe.wait_ge(sem("qkvn_ready"), t + 1)
                    for i, (lo, n) in enumerate(((0, 3), (Q_RANK, 2))):
                        b, former = tile("qnT_ready", 2 * t + i + 1)
                        pe.wait_ge(*former)
                        for k in range(n):
                            m = tp(b[:, P * k:P * (k + 1)], qkvr[:, t, lo + P * k:lo + P * (k + 1)])
                        m.then_inc(sem("qnT_full"), 1)
                pe.wait_ge(sem("qnT_ready"), 8)
                for half in range(2):
                    slab, here = slab_of(384, 3)
                    pe.wait_ge(*here)
                    for t in range(NT):
                        b, former = tile("q_stored", 4 * half + t + 1)
                        pe.wait_ge(*former)
                        by_token(qnT, t, slab, b[:, 0:384], 3).then_inc(sem("uq_full"), 1)
                slab, here = slab_of(1024, 2)
                pe.wait_ge(*here)
                for h in range(HEADS):
                    b, former = tile("kn_stored", h + 1)
                    pe.wait_ge(*former)
                    by_feature(slab, slice(P * h, P * h + HD), kvnT, b[0:HD, :], 2).then_inc(sem("ukv_full"), 1)
                vals = slab.rearrange("p k (h n) -> p k h n", n=P)[:, :, :, HD:P]
                for t in range(NT):
                    b, former = tile("v_d_stored", t + 1)
                    pe.wait_ge(*former)
                    by_token(kvnT, t, vals, b[:, :].rearrange("p (h n) -> p h n", n=HD), 2).then_inc(sem("ukv_full"), 1)
                pe.wait_ge(sem("rope_ready"), 2)
                b, former = tile("kpe_ready", 1)
                pe.wait_ge(*former)
                for t in range(NT):
                    m = tp(b[0:QD, P * t:P * (t + 1)], qkvr[:, t, QKVR - QD:QKVR])
                m.then_inc(sem("kpe_full"), 1)
                for h in range(HEADS):
                    b, former = tile("qT_ready", h + 1)
                    pe.wait_ge(*former)
                    for t in range(NT):
                        m = tp(b[0:QD, P * t:P * (t + 1)], q_tok[:, t, h, :])
                    m.then_inc(sem("qT_full"), 1)
                pe.wait_ge(sem("qT_ready"), HEADS)
                pe.wait_ge(sem("kpe_ready"), 1)
                pe.wait_ge(sem("kn_stored"), HEADS)
                pe.wait_ge(sem("v_d_stored"), NT)

                def score_d(b, h, t):
                    mm(b[:, 0:P * (t + 1)], qT_d[:, h, P * t:P * (t + 1)], kT_d[:, h, 0:P * (t + 1)], True)
                    return mm(b[:, P * t:P * (t + 1)], ident[:, :], chunk_mask[:, :], False)

                attention(HEADS * NT, score_d, lambda h, k: v_d[:, k, HD * h:HD * (h + 1)], 4)
                pe.wait_ge(sem("yT_ready"), 8)
                pe.wait_ge(sem("ycT_ready"), NT)
                out_proj(24)

            if upto >= 6:
                norm(3)
                pe.wait_ge(sem("router_loaded"), 16)
                b, former = tile("logit_ready", 1)
                pe.wait_ge(*former)
                for t in range(NT):
                    for k in range(KT):
                        m = mm(b[:, 8 * t:8 * t + 8], hT[:, k, P * t:P * (t + 1)], w_router[:, k, :], t == 0 and k == 0)
                m.then_inc(sem("logit_full"), 1)
                pe.wait_ge(sem("sel_ready"), 1)
                b, former = tile("place_ready", 1)
                pe.wait_ge(*former)
                for t in range(NT + 1):
                    for s in range(min(t + 1, NT)):
                        m = mm(b[:, 8 * t:8 * t + 8], (before if s == t else ones)[:, :], sel[:, s, :], t == 0)
                m.then_inc(sem("place_full"), 1)
                pe.wait_ge(sem("place_ready"), 1)
                pe.wait_ge(sem("turns_ready"), 1)
                ends = [pe.value_load(turn_ends_i[0:1, i:i + 1], min_val=i + 1, max_val=MAX_TURNS) for i in range(len(CAPS))]

                def gather(turn, ahead, cap):
                        pe.wait_ge(sem("pick_ready"), turn + (ahead + 1))
                        for i in range(3):
                            b = turn_banks[1 + i]
                            for d in range(3 * i, min(3 * i + 3, KT)):
                                for t in range(NT):
                                    m = mm(b[:, CAP * (d % 3):CAP * (d % 3) + cap], xn[:, t, P * d:P * (d + 1)], pick[:, t, 0:cap],
                                           d % 3 == 0 and t == 0)
                            m.then_inc(sem("xg_full"), 1)

                def turn_gates(turn, cap):
                        pe.wait_ge(sem("pick_g_ready"), turn + 1)
                        for t in range(NT):
                            m = tp(turn_banks[0][:, P * t:P * (t + 1)], pick_g[:, t, 0:P])
                        m.then_inc(sem("pickT_full"), 1 if cap > P else 2)
                        if cap > P:
                            for t in range(NT):
                                m = tp(acc[3][0:cap - P, P * t:P * (t + 1)], pick_g[:, t, P:cap])
                            m.then_inc(sem("pickT_full"), 1)

                def scatter(turn, cap):
                        pe.wait_ge(sem("pickT_ready"), turn * 2 + 2)
                        pe.wait_ge(sem("outT_ready"), turn * 3 + 3)
                        pe.wait_ge(sem("out_tok_ready"), turn * 4 + 4)
                        pe.wait_ge(sem("xg_ready"), turn * 3 + 6)
                        for i in range(2 * NT):
                            t, half = divmod(i, 2)
                            if i >= 4:
                                pe.wait_ge(sem("moe_added"), turn * 8 + (8 + i - 3))
                            b = turn_banks[i % 4]
                            cols = slice(512 * half, 512 * half + 512)
                            m = mm(b[:, :], pickT[:, 0, P * t:P * (t + 1)], out_tok[:, 0, cols], True)
                            if cap > P:
                                m = mm(b[:, :], pickT[0:cap - P, 1, P * t:P * (t + 1)], out_tok[0:cap - P, 1, cols], False)
                            m.then_inc(sem("scatter_full"), 1)

                def turn_tokens(turn, cap, next_cap):
                        pe.wait_ge(sem("sil_ready"), turn * GROUPS_E + (FF_TILES + GROUPS_E))
                        pe.wait_ge(sem("hid_ready"), turn * GROUPS_E + (FF_TILES + GROUPS_E))
                        turn_gates(turn, cap)
                        gather(turn, 1, next_cap)

                def open_banks(turn):
                        ebank = Banks(turn_banks, None)
                        ebank.read = [(sem("moe_added"), turn * 8 + (5 + i)) for i in range(4)]

                        def etile(name, count):
                            return ebank.open(sem(name), turn * GROUPS_E + count)

                        return etile

                def expert_split(turn):
                        etile = open_banks(turn)
                        pe.wait_ge(sem("xg_split"), turn * 3 + total("xg_split", 3))

                        def up(n, j, full, stored):
                            b, former = etile(stored, FF_TILES + j + 1)
                            pe.wait_ge(sem("w_low_ready"), turn * TILES_E + total("w_low_ready", RAW + n + 1))
                            pe.wait_ge(*former)
                            wh, wl = [v[n % SPLIT][:, :].rearrange("p (k n) -> p k n", n=256) for v in (w_high, w_low)]
                            for k in range(KT):
                                m = split_product(b[:, 0:256], (xg_high[:, k, :], xg_low[:, k, :]), (wh[:, k, :], wl[:, k, :]), k == 0)
                            m.then_inc(sem(full), 1)

                        def turn_hidden(j):
                            pe.wait_ge(sem("hid_ready"), turn * GROUPS_E + (FF_TILES + j + 1))
                            for k in range(2):
                                m = tp(acc[2 + j % 2][:, P * k:P * (k + 1)], hid_tok[:, j % 2, P * k:P * (k + 1)])
                            m.then_inc(sem("hidT_full"), 1)

                        def down(n, j):
                            pe.wait_ge(sem("w_low_ready"), turn * TILES_E + total("w_low_ready", RAW + n + 1))
                            pe.wait_ge(sem("hid_split"), turn * GROUPS_E + total("hid_split", j + 1))
                            wh, wl = [v[n % SPLIT][:, :].rearrange("p (k n) -> p k n", n=D) for v in (w_high, w_low)]
                            for k in range(2):
                                for half in range(2):
                                    cols = slice(512 * half, 512 * half + 512)
                                    m = split_product(acc[half][:, :], (hid_high[:, j % 2, k, :], hid_low[:, j % 2, k, :]),
                                                      (wh[:, k, cols], wl[:, k, cols]), j == 0 and k == 0)
                                    if j == k == half == 0:
                                        m.then_inc(sem("out_tok_full"), 4)
                            m.then_inc(sem("down_used"), 1)

                        for n, (kind, j) in enumerate(expert_order()):
                            if kind == "g":
                                up(n, j, "gate_full", "sil_ready")
                                if j >= 1:
                                    turn_hidden(j - 1)
                            elif kind == "u":
                                up(n, j, "up_full", "hid_ready")
                            else:
                                if j == GROUPS_E - 1:
                                    turn_hidden(j)
                                down(n, j)
                        turn_tokens(turn, P, CAPS[1])
                        scatter(turn, P)

                def expert(turn, cap, next_cap):
                        w = expert_ring(raw_slots, landed, turn)
                        etile = open_banks(turn)
                        pe.wait_ge(sem("xg_ready"), turn * 3 + 3)

                        def slab_of(n=256, kt=KT):
                            slot, here = w.take()
                            return slot[:, 0:kt * n].rearrange("p (k n) -> p k n", n=n), here

                        def up(j):
                            for full, stored, first in (("gate_full", "sil_ready", FF_TILES), ("up_full", "hid_ready", FF_TILES)):
                                slab, here = slab_of()
                                pe.wait_ge(*here)
                                b, former = etile(stored, first + j + 1)
                                pe.wait_ge(*former)
                                for m in range(2):
                                    last = by_feature(slab, slice(P * m, P * (m + 1)), xgT[:, :, 0:cap], b[:, CAP * m:CAP * m + cap],
                                                      fresh=m == 0)
                                last.then_inc(sem(full), 1)

                        def down(j):
                            slab, here = slab_of(D, 2)
                            pe.wait_ge(*here)
                            pe.wait_ge(sem("hid_ready"), turn * GROUPS_E + (FF_TILES + j + 1))
                            for k in range(2):
                                for d in range(KT):
                                    m = mm(acc[d // 3][:, CAP * (d % 3):CAP * (d % 3) + cap], slab[:, k, P * d:P * (d + 1)],
                                           hid_e[:, j % 2, CAP * k:CAP * k + cap], j == 0 and k == 0 and d % 3 == 0)
                            m.then_inc(sem("down_used"), 1)

                        up(0)
                        for j in range(1, GROUPS_E):
                            up(j)
                            down(j - 1)
                        down(GROUPS_E - 1)
                        turn_tokens(turn, cap, next_cap)
                        pe.wait_ge(sem("outT_ready"), turn * 3 + 3)
                        pe.wait_ge(sem("pickT_ready"), turn * 2 + 2)
                        pe.wait_ge(sem("xg_ready"), turn * 3 + 6)
                        for i, (rows, lo, half) in enumerate(((P, 0, 0), (P, 0, 1), (cap - P, P, 0), (cap - P, P, 1))):
                            for d in range(4 * half, 4 * half + 4):
                                m = tp(turn_banks[i][0:rows, P * (d % 4):P * (d % 4 + 1)], outT[:, d, lo:lo + rows])
                            m.then_inc(sem("out_tok_full"), 1)
                        scatter(turn, cap)

                gather(0, 0, CAPS[0])
                with pe.Fori(0, ends[0]) as turn:
                    expert_split(turn)
                with pe.Fori(ends[0], ends[1]) as turn:
                    expert(turn, CAPS[1], CAPS[2])
                with pe.Fori(ends[1], ends[2]) as turn:
                    expert(turn, CAPS[2], CAPS[2])

        @block.scalar
        def _(act):
            step = Steps(act, sem("act_step"))

            def high_dense(s):
                order = [n for phase in split_tiles() for n in phase]
                n = order[s]
                act.wait_ge(landed[n % DENSE_RAW], 16 * (n // DENSE_RAW + 1))
                if s >= DENSE_SPLIT:
                    name, count = last_use(weight_order()[order[s - DENSE_SPLIT]])
                    act.wait_ge(sem(name), total(name, count))
                act.activation(w_high[s % DENSE_SPLIT][:, 0:SLOT], slots[n % DENSE_RAW][:, 0:SLOT], ACT.Copy).then_inc(sem("dense_high_ready"), 1)

            def next_high(phase, c):
                first, last = phase_splits(phase)
                if first + c + DENSE_SPLIT <= last:
                    high_dense(first + c + DENSE_SPLIT)

            def norm(j):
                for t in range(NT):
                    if j == 0:
                        act.wait_ge(sem("x_loaded"), 16 * NT)
                    elif j < 4:
                        act.wait_ge(sem("x_added"), (None, 12, 20, 36)[j] + t + 1)
                    step(act.activation(sqd, xs[:, t, :], ACT.Square, accum_out=small[:, 32 + t:33 + t]))
                act.activation(small[:, 32:36], small[:, 32:36], ACT.Copy, scale=1.0 / D).then_inc(sem("ss_ready"), 1)
                act.wait_ge(sem("ms_ready"), j + 1)
                act.activation(small[:, 40:44], small[:, 36:40], ACT.Sqrt).then_inc(sem("rstd_ready"), 1)
                if j < 3:
                    for c in range(DENSE_SPLIT):
                        high_dense(phase_splits(j)[0] + c)
                    act.wait_ge(sem("hT_ready"), 8 * (j + 1))
                    for k in range(KT):
                        act.activation(h_high[:, k, :], hT[:, k, :], ACT.Copy).then_inc(sem("h_high_ready"), 1)

            def attention(first, done):
                def outputs(pair):
                    act.wait_ge(sem("pv_done"), 2 * done + 2 * (pair + 1))
                    act.activation(yT[:, done + pair, :], acc[pair % 2][:, :], ACT.Copy).then_inc(sem("yT_ready"), 1)

                for u in range(HEADS * NT):
                    if u >= 10 and (u - 10) % 8 == 0:
                        outputs((u - 10) // 8)
                    t = u % NT
                    n = P * (t + 1)
                    act.wait_ge(sem("max_ready"), first + u + 1)
                    if first or u >= 3:
                        act.wait_ge(sem("probsT_full"), first + u - 2)
                    b = bank["probs_ready", first + u + 1]
                    act.activation(probs[:, u % 3, 0:n], b[:, 0:n], ACT.Exp, bias=small[:, 48 + u % 4:49 + u % 4],
                                   accum_out=small[:, 52 + u % 4:53 + u % 4]).then_inc(sem("probs_ready"), 1)
                outputs(3)

            norm(0)
            for c in range(8):
                act.wait_ge(sem("qk_full"), c + 1)
                act.activation((qT if c < 4 else kT)[:, c % 4, :], bank["qk_stored", c + 1][:, :], ACT.Copy,
                               scale=HD ** -0.5 if c < 4 else 1.0).then_inc(sem("qk_stored"), 1)
                if c % 2:
                    next_high(0, c // 2)
            act.wait_ge(sem("w_dt_loaded"), 16 * KT)
            act.activation(w_dt_high[:, :, :], w_dt[:, :, :], ACT.Copy).then_inc(sem("w_dt_high"), 1)
            for c in (4, 5):
                next_high(0, c)
            for i in range(8):
                act.wait_ge(sem("z_full"), i + 1)
                act.activation(zs[:, i % 4, 256 * (i // 4):256 * (i // 4) + 256], bank["z_stored", i + 1][:, 0:256], ACT.Silu)\
                    .then_inc(sem("z_stored"), 1)
                if i % 4 == 3:
                    next_high(0, 6 + i // 4)
            act.wait_ge(sem("const_ready"), 1)
            for c in range(CONV_TILES):
                act.wait_ge(sem("conv_full"), c + 1)
                act.activation(conv_in[:, c, B_CONV - 1:], bank["conv_stored", c + 1][:, :], ACT.Copy).then_inc(sem("conv_stored"), 1)
                if c % 2:
                    next_high(0, 8 + c // 2)
            act.wait_ge(sem("small_loaded"), 64)
            act.wait_ge(sem("dt_full"), 1)
            act.activation(dt_row[0], bank["u_ready", 1][0:HEADS, :], ACT.Identity, bias=small[0:HEADS, 0:1]).then_inc(sem("u_ready"), 1)
            act.activation(small[0:HEADS, 2:3], small[0:HEADS, 1:2], ACT.Exp)
            act.wait_ge(sem("abs_ready"), 1)
            step(act.activation(dt_row[1], dt_row[1], ACT.Exp, scale=-1.0))
            act.activation(dt_row[1], dt_row[1], ACT.Ln, bias=1.0).then_inc(sem("ln_ready"), 1)
            for c in range(CONV_TILES):
                act.wait_ge(sem("conv_sum"), c + 1)
                act.activation(conv_out[:, c, :], conv_out[:, c, :], ACT.Silu).then_inc(sem("conv_ready"), 1)
            if upto >= 2:
                attention(0, 0)
                act.wait_ge(sem("dt_col_ready"), 1)
                for h in range(HEADS):
                    plain, masked = bank["decay_ready", 7 * h + 5], bank["decay_ready", 7 * h + 7]
                    if h >= 2:
                        act.wait_ge(sem("w_ready"), NT * (h - 1))
                    act.wait_ge(sem("row_full"), 2 * h + 2)
                    for j in range(NT):
                        bias = small[:, 64 + HEADS * j + h:65 + HEADS * j + h]
                        if j < NT - 1:
                            act.activation(decay[h % 2][:, j, P * (j + 1):], plain[:, P * (j + 1):], ACT.Exp, bias=bias)\
                                .then_inc(sem("decay_ready"), 1)
                        act.activation(decay[h % 2][:, j, P * j:P * (j + 1)], masked[:, P * j:P * (j + 1)], ACT.Exp, bias=bias)\
                            .then_inc(sem("decay_ready"), 1)
                act.wait_ge(sem("ssd_ms_ready"), 1)
                act.activation(small[:, 144:152], small[:, 136:144], ACT.Sqrt).then_inc(sem("ssd_rstd"), 1)

            if upto >= 3:
                norm(1)
                for f in range(FF_TILES):
                    act.wait_ge(sem("gate_full"), f + 1)
                    if f >= 2:
                        act.wait_ge(sem("hid_ready"), f - 1)
                    act.activation(sil[:, f % 2, :], bank["sil_ready", f + 1][:, :], ACT.Silu).then_inc(sem("sil_ready"), 1)
                    if f % 2:
                        next_high(1, f - 1)
                        next_high(1, f)

            if upto >= 4:
                norm(2)
                for c in range(C_TILES):
                    act.wait_ge(sem("pc_full"), total("pc_full", c + 1))
                    act.activation(pcT[:, c, 1:], bank["pc_stored", c + 1][:, :], ACT.Copy).then_inc(sem("pc_stored"), 1)
                    if c % 2:
                        next_high(2, c // 2)
                next_high(2, 7)
                act.wait_ge(sem("mixed"), 13)
                act.activation(pcT[0:64, 12, 1:], pcT[0:64, 12, 1:], ACT.Tanh).then_inc(sem("lora_in_ready"), 1)
                act.wait_ge(sem("mixed"), 14)
                act.activation(pcT[:, 13, 1:], pcT[:, 13, 1:], ACT.Sigmoid).then_inc(sem("lora_in_ready"), 1)
                for t in range(NT):
                    for i, name in enumerate(("sig", "a")):
                        act.wait_ge(sem("wa_sum"), total("wa_sum", 2 * t + i + 1))
                        act.activation(R[name], R[name], ACT.Sigmoid).then_inc(sem("sig_ready"), 1)
                    act.wait_ge(sem("lora_full"), total("lora_full", 3 * t + 3))
                    act.activation(R["g"], bank["g_ready", t + 1][:, :], ACT.Copy).then_inc(sem("g_ready"), 1)
                    act.wait_ge(sem("kk_ss"), t + 1)
                    act.activation(small[:, 176:184], small[:, 176:184], ACT.Sqrt).then_inc(sem("kk_norm"), 1)
                    for i, (name, row, sign) in enumerate((("Eex", 0, 1.0), ("Ein", 1, 1.0), ("Eni", 1, -1.0), ("Erev", 2, 1.0))):
                        act.wait_ge(sem("cum_full"), total("cum_full", 3 * t + row + 1))
                        act.activation(R[name], bank["exp_ready", 4 * t + (1, 3, 4)[row]][:, :], ACT.Exp, scale=sign).then_inc(sem("exp_ready"), 1)
                    act.wait_ge(sem("end_full"), total("end_full", t + 1))
                    act.activation(small[:, 224 + 8 * (t % 2):232 + 8 * (t % 2)], bank["end_ready", t + 1][:, 0:8], ACT.Exp)\
                        .then_inc(sem("end_ready"), 1)
                    for i in range(4):
                        act.wait_ge(sem("ft_full"), total("ft_full", 4 * t + i + 1))
                        b = bank["ft_ready", 4 * t + i + 1]
                        if i in (0, 1):
                            o = F["ar"][:, :, :, CHUNK * i:CHUNK * (i + 1)]
                            v = b[:, :].rearrange("p (a b c) -> p a b c", b=2, c=CHUNK)
                        else:
                            o, v = F["btT" if i == 2 else "ktT"], b[:, :].rearrange("p (a b) -> p a b", b=P)
                        act.activation(o, v, ACT.Copy).then_inc(sem("ft_ready"), 1)
                    for n in range(5):
                        act.wait_ge(sem("y1_full"), 5 * t + n + 1)
                        act.activation(R["Y1"], bank["y1_ready", 5 * t + n + 1][:, :], ACT.Copy).then_inc(sem("y1_ready"), 1)
                    for i, o in enumerate((R["Z1"], R["U"], F["wt"][:, :, 0:CHUNK], F["wt"][:, :, CHUNK:])):
                        act.wait_ge(sem("zu_full"), 4 * t + i + 1)
                        b = bank["z_ready", 4 * t + i + 1]
                        v = b[:, 0:256].rearrange("p (a b) -> p a b", b=CHUNK) if i >= 2 else b[:, :]
                        act.activation(o, v, ACT.Copy).then_inc(sem("z_ready"), 1)
                    for c in range(2):
                        n = 2 * t + c
                        rows = slice(CHUNK * c, CHUNK * (c + 1))
                        act.wait_ge(sem("sa_ready"), 2 * n + 2)
                        for par in range(2):
                            act.activation(R["y"][rows, :].rearrange("p (a b n) -> p a b n", b=2, n=HD)[:, :, par, :],
                                           bank["y_stored", 2 * n + par + 1][rows, 256:].rearrange("p (a n) -> p a n", n=HD), ACT.Copy)\
                                .then_inc(sem("y_stored"), 1)
                    act.wait_ge(sem("gn_ms"), t + 1)
                    act.activation(small[:, 216:224], small[:, 216:224], ACT.Sqrt).then_inc(sem("gn_rstd"), 1)
                    act.wait_ge(sem("ycT_full"), total("ycT_full", t + 1))
                    act.activation(yT[:, 0:4, P * t:P * (t + 1)], bank["ycT_ready", t + 1][:, :].rearrange("p (a b) -> p a b", b=P), ACT.Copy)\
                        .then_inc(sem("ycT_ready"), 1)

            if upto >= 5:
                for t in range(NT):
                    act.wait_ge(sem("qkvr_stored"), total("qkvr_stored", 12))
                    step(act.activation(sqd[:, 0:Q_RANK], qkvr[:, t, 0:Q_RANK], ACT.Square, accum_out=small[:, 152 + t:153 + t]))
                    step(act.activation(sqd[:, 0:KV_RANK], qkvr[:, t, Q_RANK:Q_RANK + KV_RANK], ACT.Square, accum_out=small[:, 156 + t:157 + t]))
                act.activation(small[:, 160:168], small[:, 152:160], ACT.Copy).then_inc(sem("mla_ss"), 1)
                act.wait_ge(sem("mla_ms"), 1)
                act.activation(small[:, 168:176], small[:, 160:168], ACT.Sqrt).then_inc(sem("mla_rstd"), 1)
                act.wait_ge(sem("angle_ready"), 1)
                for i in range(2):
                    act.activation(rope_cs[:, 4 * i:4 * i + 4, :], rope_cs[:, 4 * i:4 * i + 4, :], ACT.Sin).then_inc(sem("sin_ready"), 1)
                for i in range(8):
                    half, t = divmod(i, NT)
                    act.wait_ge(sem("uq_full"), total("uq_full", i + 1))
                    act.activation(q_tok[:, t, 4 * half:4 * half + 4, :], bank["q_stored", i + 1][:, 0:384].rearrange("p (h n) -> p h n", n=QD),
                                   ACT.Copy, scale=MLA_SCALE).then_inc(sem("q_stored"), 1)
                for h in range(HEADS):
                    act.wait_ge(sem("ukv_full"), total("ukv_full", h + 1))
                    act.activation(kT_d[0:HD, h, :], bank["kn_stored", h + 1][0:HD, :], ACT.Copy).then_inc(sem("kn_stored"), 1)
                for h in range(HEADS):
                    act.wait_ge(sem("qT_full"), h + 1)
                    act.activation(qT_d[:, h, :], bank["qT_ready", h + 1][0:QD, :], ACT.Copy).then_inc(sem("qT_ready"), 1)
                attention(HEADS * NT, 4)

            if upto >= 6:
                norm(3)
                act.wait_ge(sem("top_ready"), 1)
                act.activation(ex, ex, ACT.Exp).then_inc(sem("ex_ready"), 1)
                act.wait_ge(sem("turns_ready"), 1)
                ends = [act.value_load(turn_ends_i[0:1, i:i + 1], min_val=i + 1, max_val=MAX_TURNS) for i in range(len(CAPS))]

                def high(turn, ring, n):
                        raw, here = ring.take()
                        act.wait_ge(*here)
                        if ring.turn is not None:
                            name, count = expert_tile_used(n - SPLIT)
                            act.wait_ge(sem(name), turn * GROUPS_E + count)
                        act.activation(w_high[n % SPLIT][:, :], raw[:, :], ACT.Copy).then_inc(sem("w_high_ready"), 1)

                def xg_parts(turn, ahead):
                        for i in range(3):
                            cols = slice(3 * i, min(3 * i + 3, KT))
                            act.wait_ge(sem("xg_ready"), turn * 3 + (3 * ahead + i + 1))
                            act.activation(xg_high[:, cols, :], xgT[:, cols, 0:P], ACT.Copy).then_inc(sem("xg_high_ready"), 1)

                def gates_turned(turn, cap):
                        act.wait_ge(sem("pickT_full"), turn * 2 + (1 if cap > P else 2))
                        act.activation(pickT[:, 0, :], turn_banks[0][:, :], ACT.Copy).then_inc(sem("pickT_ready"), 1 if cap > P else 2)
                        if cap > P:
                            act.wait_ge(sem("pickT_full"), turn * 2 + 2)
                            act.activation(pickT[0:cap - P, 1, :], acc[3][0:cap - P, :], ACT.Copy).then_inc(sem("pickT_ready"), 1)

                def expert_split(turn):
                        ring = expert_ring(raw_slots, landed, turn)
                        ring.n = SPLIT
                        for n, (kind, j) in enumerate(expert_order()):
                            if kind == "g":
                                act.wait_ge(sem("gate_full"), turn * GROUPS_E + (FF_TILES + j + 1))
                                act.wait_ge(sem("hid_ready"), turn * GROUPS_E + (FF_TILES + j - 1))
                                act.activation(sil_e[:, j % 2, 0:256], turn_banks[2 * j % 4][:, 0:256], ACT.Silu)\
                                    .then_inc(sem("sil_ready"), 1)
                            turned = j - 1 if kind == "g" else j if j == GROUPS_E - 1 and kind == "d" else -1
                            if turned >= 0:
                                act.wait_ge(sem("hidT_full"), turn * GROUPS_E + (turned + 1))
                                if turned >= 2:
                                    act.wait_ge(sem("down_used"), turn * GROUPS_E + (10 + turned - 1))
                                act.activation(hid_high[:, turned % 2, :, :], acc[2 + turned % 2][:, 0:2 * P].rearrange("p (a b) -> p a b", b=P),
                                               ACT.Copy).then_inc(sem("hid_high_ready"), 1)
                            if n < TILES_E - 1:
                                high(turn, ring, n + SPLIT)
                        act.wait_ge(sem("down_used"), turn * GROUPS_E + (10 + GROUPS_E))
                        act.activation(out_tok[:, 0, 0:512], acc[0][:, :], ACT.Copy).then_inc(sem("outT_ready"), 3)
                        act.activation(out_tok[:, 0, 512:], acc[1][:, :], ACT.Copy).then_inc(sem("out_tok_ready"), 4)
                        gates_turned(turn, P)
                        high(turn, ring, TILES_E - 1 + SPLIT)
                        xg_parts(turn, 1)

                def expert(turn, cap):
                        for j in range(GROUPS_E):
                            act.wait_ge(sem("gate_full"), turn * GROUPS_E + (FF_TILES + j + 1))
                            act.wait_ge(sem("hid_ready"), turn * GROUPS_E + (FF_TILES + j - 1))
                            act.activation(pair_of(sil_e[:, j % 2, :], cap), pair_of(turn_banks[2 * j % 4][:, 0:2 * CAP], cap), ACT.Silu)\
                                .then_inc(sem("sil_ready"), 1)
                        act.wait_ge(sem("down_used"), turn * GROUPS_E + (10 + GROUPS_E))
                        for i in range(3):
                            n = min(3, KT - 3 * i)
                            act.activation(outT[:, 3 * i:3 * i + n, 0:cap], acc[i][:, 0:CAP * n].rearrange("p (a b) -> p a b", b=CAP)[:, :, 0:cap], ACT.Copy)\
                                .then_inc(sem("outT_ready"), 1)
                        gates_turned(turn, cap)
                        for i in range(4):
                            act.wait_ge(sem("out_tok_full"), turn * 4 + (i + 1))
                            rows = P if i < 2 else cap - P
                            act.activation(out_tok[0:rows, i // 2, 512 * (i % 2):512 * (i % 2) + 512],
                                           turn_banks[i][0:rows, :], ACT.Copy).then_inc(sem("out_tok_ready"), 1)

                ring = expert_ring(raw_slots, landed, None)
                for n in range(SPLIT):
                    high(0, ring, n)
                xg_parts(0, 0)
                with act.Fori(0, ends[0]) as turn:
                    expert_split(turn)
                with act.Fori(ends[0], ends[1]) as turn:
                    expert(turn, CAPS[1])
                with act.Fori(ends[1], ends[2]) as turn:
                    expert(turn, CAPS[2])
                act.wait_ge(sem("moe_done"), 1)
                norm(4)

        @block.vector
        def _(dve):
            step = Steps(dve, sem("dve_step"))

            def tt(o, a, b, op):
                return dve.tensor_tensor(o, a, b, op)

            def scale_by(view, shape):
                return view.to_broadcast(shape)

            def inv_mean(o, i, n, eps):
                step(dve.tensor_scalar(o, i, n, eps, ALU.mult, ALU.add))
                return dve.reciprocal(o, o)

            def low_dense(s):
                n = [n for phase in split_tiles() for n in phase][s]
                dve.wait_ge(sem("dense_high_ready"), s + 1)
                tt(w_low[s % DENSE_SPLIT][:, :], slots[n % DENSE_RAW][:, :], w_high[s % DENSE_SPLIT][:, :].bitcast(F32), ALU.subtract)\
                    .then_inc(sem("dense_low_ready"), 1)

            def next_low(phase, c):
                first, last = phase_splits(phase)
                if first + c + DENSE_SPLIT <= last:
                    low_dense(first + c + DENSE_SPLIT)

            def norm(j):
                dve.wait_ge(sem("ss_ready"), j + 1)
                inv_mean(small[:, 36:40], small[:, 32:36], 1.0, RMS_EPS).then_inc(sem("ms_ready"), 1)
                dve.wait_ge(sem("rstd_ready"), j + 1)
                if j == 4:
                    return
                for t in range(NT):
                    dve.tensor_scalar(xn[:, t, :], xs[:, t, :], small[:, 40 + t:41 + t], None, ALU.mult).then_inc(sem("xn_ready"), 1)
                if j < 3:
                    low_dense(phase_splits(j)[0])
                for t in range(NT):
                    for half in range(2):
                        dve.wait_ge(sem("xnT_full"), 8 * j + 2 * t + half + 1)
                        b = bank["hT_ready", 8 * j + 2 * t + half + 1][:, :].rearrange("p (a b) -> p a b", b=P)
                        wv = vc[:, 8 * j + 4 * half:8 * j + 4 * half + 4].unsqueeze(2).to_broadcast([P, 4, P])
                        tt(hT[:, 4 * half:4 * half + 4, P * t:P * (t + 1)], b, wv, ALU.mult).then_inc(sem("hT_ready"), 1)
                if j < 3:
                    for k in range(KT):
                        dve.wait_ge(sem("h_high_ready"), KT * j + k + 1)
                        tt(h_low[:, k, :], hT[:, k, :], h_high[:, k, :].bitcast(F32), ALU.subtract).then_inc(sem("h_low_ready"), 1)
                    low_dense(phase_splits(j)[0] + 1)

            def attention(first, done):
                for i in range(HEADS * NT + 2):
                    if i < HEADS * NT:
                        n = P * (i % NT + 1)
                        dve.wait_ge(sem("scores_full"), first + i + 1)
                        step(dve.tensor_reduce(small[:, 60 + i % 4:61 + i % 4], bank["probs_ready", first + i + 1][:, 0:n], AX, ALU.max))
                        dve.tensor_scalar(small[:, 48 + i % 4:49 + i % 4], small[:, 60 + i % 4:61 + i % 4], -1.0, None, ALU.mult).then_inc(sem("max_ready"), 1)
                    u = i - 1
                    if 0 <= u < HEADS * NT:
                        n = P * (u % NT + 1)
                        dve.wait_ge(sem("probs_ready"), first + u + 1)
                        step(dve.reciprocal(small[:, 56 + u % 4:57 + u % 4], small[:, 52 + u % 4:53 + u % 4]))
                        dve.tensor_scalar(probs[:, u % 3, 0:n], probs[:, u % 3, 0:n], small[:, 56 + u % 4:57 + u % 4], None, ALU.mult).then_inc(sem("probs_scaled"), 1)
                    u = i - 2
                    if u >= 0:
                        h, t = divmod(u, NT)
                        dve.wait_ge(sem("probsT_full"), first + u + 1)
                        if t == 0 and h >= 2:
                            dve.wait_ge(sem("pv_done"), 2 * done + h - 1)
                        dve.tensor_copy(probsT[h % 2][:, 0:t + 1, P * t:P * (t + 1)],
                                            bank["probsT_ready", first + u + 1][:, 0:P * (t + 1)].rearrange("p (a b) -> p a b", b=P)).then_inc(sem("probsT_ready"), 1)

            def add_x(full, count, t, cols, b):
                dve.wait_ge(sem(full), count)
                tt(xs[:, t, cols], xs[:, t, cols], b, ALU.add).then_inc(sem("x_added"), 1)

            def out_proj(base, full0):
                for c in range(4):
                    for t in range(NT):
                        n = 4 * c + t
                        add_x("mix_full", full0 + n + 1, t, slice(256 * c, 256 * c + 256), bank["x_added", base + n + 1][:, 0:256])

            dve.wait_ge(sem("vec_full"), 1)
            dve.tensor_copy(vc[:, :], bank["vc_ready", 1][:, 0:95]).then_inc(sem("vc_ready"), 1)
            dve.wait_ge(sem("vc_ready"), 1)
            norm(0)
            for c in range(4):
                next_low(0, c)
            dve.wait_ge(sem("w_dt_high"), 1)
            tt(w_dt_low[:, :, :], w_dt[:, :, :], w_dt_high[:, :, :].bitcast(F32), ALU.subtract).then_inc(sem("w_dt_split"), 1)
            for i in range(8):
                dve.wait_ge(sem("v_full"), i + 1)
                dve.tensor_copy(v_a[:, i % 4, 256 * (i // 4):256 * (i // 4) + 256], bank["v_stored", i + 1][:, 0:256]).then_inc(sem("v_stored"), 1)
                if i % 4 == 3:
                    next_low(0, 4 + i // 4)
            dve.wait_ge(sem("const_ready"), 1)
            dve.wait_ge(sem("small_loaded"), 64)
            for c in (6, 7, 8):
                next_low(0, c)
            for c in range(CONV_TILES):
                if c == 2:
                    next_low(0, 9)
                dve.wait_ge(sem("conv_stored"), c + 1)
                tap = lambda k: vc[:, 40 + 8 * k + c:41 + 8 * k + c]
                step(dve.tensor_scalar(conv_out[:, c, :], conv_in[:, c, 0:SEQ], tap(0), vc[:, 32 + c:33 + c], ALU.mult, ALU.add))
                for k in range(1, B_CONV):
                    i = dve.scalar_tensor_tensor(out=conv_out[:, c, :], in0=conv_in[:, c, k:k + SEQ], scalar=tap(k),
                                                 in1=conv_out[:, c, :], op0=ALU.mult, op1=ALU.add)
                    if k < B_CONV - 1:
                        step(i)
                i.then_inc(sem("conv_sum"), 1)
            dve.wait_ge(sem("u_ready"), 1)
            dve.scalar_tensor_tensor(out=dt_row[1], in0=dt_row[0], scalar=-1.0, in1=dt_row[0], op0=ALU.mult, op1=ALU.max).then_inc(sem("abs_ready"), 1)
            dve.wait_ge(sem("ln_ready"), 1)
            step(dve.scalar_tensor_tensor(out=dt_keep, in0=dt_row[0], scalar=0.0, in1=dt_row[1], op0=ALU.max, op1=ALU.add))
            if upto >= 2:
                attention(0, 0)
                step(dve.memset(ones_row, 1.0))
                dve.wait_ge(sem("pv_done"), HEADS)
                step(dve.tensor_copy(dt_row[0], dt_keep))
                step(dve.tensor_scalar(dt_row[2], dt_row[0], small[0:HEADS, 2:3], -1.0, ALU.mult, ALU.mult))
                step(dve.tensor_tensor_scan(dt_row[1], ones_row, dt_row[2], 0.0, ALU.mult, ALU.add))
                dve.tensor_scalar(dt_row[2], dt_row[1], -1.0, None, ALU.mult).then_inc(sem("cum_ready"), 1)
                for t in range(NT):
                    dve.wait_ge(sem("x_tok_full"), t + 1)
                    dve.tensor_copy(x_tok[:, t, :], bank["x_tok_ready", t + 1][:, :]).then_inc(sem("x_tok_ready"), 1)
                for i in range(8):
                    g, j = divmod(i, NT)
                    dve.wait_ge(sem("cb_full"), i + 1)
                    dve.tensor_copy(cbT[:, g, j, P * j:], bank["cb_ready", i + 1][:, P * j:]).then_inc(sem("cb_ready"), 1)
                dve.wait_ge(sem("dt_col_full"), 1)
                step(dve.tensor_copy(small[:, 64:128], bank["dt_col_ready", 1][:, 0:64]))
                dve.tensor_copy(small[:, 3:4], small[:, 64:65]).then_inc(sem("dt_col_ready"), 1)
                dtc = small[:, 96:128].rearrange("p (t h) -> p t h", h=HEADS).unsqueeze(3).to_broadcast([P, NT, HEADS, HD])
                step(tt(xdt.rearrange("p t (h n) -> p t h n", n=HD), x_tok.rearrange("p t (h n) -> p t h n", n=HD), dtc, ALU.mult))
                for h in range(HEADS + 1):
                    if h < HEADS:
                        if h >= 2:
                            dve.wait_ge(sem("ssd_full"), h - 1)
                        for j in range(NT):
                            dve.wait_ge(sem("decay_ready"), 7 * h + min(2 * j + 2, 7))
                            tt(wT[h % 2][:, j, P * j:], decay[h % 2][:, j, P * j:], cbT[:, h // 4, j, P * j:], ALU.mult).then_inc(sem("w_ready"), 1)
                    if h >= 1:
                        g = h - 1
                        dve.wait_ge(sem("ssd_full"), g + 1)
                        cols = slice(HD * g, HD * (g + 1))
                        dve.scalar_tensor_tensor(out=y_tok[:, :, cols], in0=x_tok[:, :, cols], scalar=small[:, 8 + g:9 + g],
                                                     in1=bank["y_tok_ready", g + 1][:, 0:256].rearrange("p (a b) -> p a b", b=HD),
                                                     op0=ALU.mult, op1=ALU.add).then_inc(sem("y_tok_ready"), 1)
                dve.wait_ge(sem("y_tok_ready"), HEADS)
                dve.wait_ge(sem("z_stored"), 8)
                step(tt(y_tok, y_tok, zs, ALU.mult))
                step(tt(decay[0], y_tok, y_tok, ALU.mult))
                step(dve.tensor_reduce(small[:, 128:136], decay[0].rearrange("p t (g n) -> p (t g) n", n=256), AX, ALU.add))
                inv_mean(small[:, 136:144], small[:, 128:136], 1.0 / 256, B_NORM_EPS).then_inc(sem("ssd_ms_ready"), 1)
                dve.wait_ge(sem("ssd_rstd"), 1)
                rs = small[:, 144:152].unsqueeze(2).to_broadcast([P, 8, 256])
                yv = y_tok.rearrange("p t (g n) -> p (t g) n", n=256)
                tt(yv, yv, rs, ALU.mult).then_inc(sem("yn_ready"), 1)
                for t in range(NT):
                    dve.wait_ge(sem("ynT_full"), t + 1)
                    tt(yT[:, 4:8, P * t:P * (t + 1)], bank["yT_b_ready", t + 1][:, :].rearrange("p (a b) -> p a b", b=P),
                           vc[:, 91:95].unsqueeze(2).to_broadcast([P, 4, P]), ALU.mult).then_inc(sem("yT_b_ready"), 1)
                out_proj(0, 0)

            if upto >= 3:
                norm(1)
                for f in range(FF_TILES):
                    if f % 2 == 0:
                        next_low(1, f)
                    dve.wait_ge(sem("up_full"), f + 1)
                    dve.wait_ge(sem("sil_ready"), f + 1)
                    tt(hid[:, f, :], sil[:, f % 2, :], bank["hid_ready", f + 1][:, :], ALU.mult).then_inc(sem("hid_ready"), 1)
                    if f % 2:
                        next_low(1, f)
                for half in range(2):
                    for t in range(NT):
                        add_x("down_full", 4 * half + t + 1, t, slice(512 * half, 512 * half + 512), acc[t][:, :])

            if upto >= 4:
                norm(2)
                step(dve.memset(pcT[:, :, 0:1], 0.0))
                for j in range(C_TILES):
                    dve.wait_ge(sem("pc_stored"), total("pc_stored", j + 1))
                    step(tt(mixdiff[:, j % 2, :], pcT[:, j, 0:SEQ], pcT[:, j, 1:], ALU.subtract))
                    dve.scalar_tensor_tensor(out=pcT[:, j, 1:], in0=mixdiff[:, j % 2, :], scalar=vc[:, 72 + j:73 + j],
                                                 in1=pcT[:, j, 1:], op0=ALU.mult, op1=ALU.add).then_inc(sem("mixed"), 1)
                    if j % 2:
                        next_low(2, j // 2)
                next_low(2, 7)
                for i in range(12):
                    c, t = divmod(i, NT)
                    n = 256 if c < 2 else QKVR - 512
                    dve.wait_ge(sem("qkvr_full"), total("qkvr_full", i + 1))
                    dve.tensor_copy(qkvr[:, t, 256 * c:256 * c + n], bank["qkvr_stored", i + 1][:, 0:n]).then_inc(sem("qkvr_stored"), 1)
                dve.wait_ge(sem("bc_loaded"), 16 * 7)
                by_head = lambda v: v.rearrange("p (h n) -> p h n", n=HD)
                spread = lambda v: v.unsqueeze(2).to_broadcast([P, HEADS, HD])
                dve.wait_ge(sem("mixed"), C_TILES)
                dve.memset(state[0], 0.0).then_inc(sem("state_ready"), 1)
                for t in range(NT):
                    for a, name in enumerate("rkv"):
                        dve.wait_ge(sem("rkv_full"), total("rkv_full", 3 * t + a + 1))
                        dve.tensor_copy(R[name], bank["rkv_ready", 3 * t + a + 1][:, :]).then_inc(sem("rkv_ready"), 1)
                    for i, (name, bias) in enumerate((("sig", "w0"), ("a", "a0"))):
                        dve.wait_ge(sem("lora_full"), total("lora_full", 3 * t + i + 1))
                        tt(R[name], bank["wa_sum", 2 * t + i + 1][:, :], bc[bias], ALU.add).then_inc(sem("wa_sum"), 1)
                    dve.wait_ge(sem("rkv_ready"), total("rkv_ready", 3 * t + 3))
                    step(tt(R["kk"], R["k"], bc["k_k"], ALU.mult))
                    step(tt(R["tmp"], R["kk"], R["kk"], ALU.mult))
                    dve.tensor_reduce(small[:, 176:184], by_head(R["tmp"]), AX, ALU.add).then_inc(sem("kk_ss"), 1)
                    dve.wait_ge(sem("kk_ss"), t + 1)
                    dve.wait_ge(sem("sig_ready"), 2 * t + 2)
                    step(dve.scalar_tensor_tensor(out=R["tmp"], in0=R["a"], scalar=-1.0, in1=bc["k_a"], op0=ALU.add, op1=ALU.mult))
                    step(dve.scalar_tensor_tensor(out=R["k"], in0=R["tmp"], scalar=1.0, in1=R["k"], op0=ALU.add, op1=ALU.mult))
                    step(tt(R["tmp"], R["r"], R["k"], ALU.mult))
                    step(tt(R["tmp"], R["tmp"], bc["r_k"], ALU.mult))
                    step(dve.tensor_reduce(small[:, 192:200], by_head(R["tmp"]), AX, ALU.add))
                    dve.wait_ge(sem("kk_norm"), t + 1)
                    step(dve.tensor_scalar(small[:, 184:192], small[:, 176:184], 1e-12, None, ALU.max))
                    step(dve.reciprocal(small[:, 184:192], small[:, 184:192]))
                    step(tt(by_head(R["kk"]), by_head(R["kk"]), spread(small[:, 184:192]), ALU.mult))
                    step(tt(R["b"], R["kk"], R["a"], ALU.mult))
                    dve.wait_ge(sem("exp_ready"), 4 * t + 4)
                    dve.scalar_tensor_tensor(out=R["al"], in0=R["kk"], scalar=-1.0, in1=R["Eex"], op0=ALU.mult, op1=ALU.mult).then_inc(sem("scaled_ready"), 1)
                    for o, i, e in (("rt", "r", "Ein"), ("bt", "b", "Eni"), ("kt", "k", "Eni"), ("bh", "b", "Erev"), ("kh", "k", "Erev")):
                        tt(R[o], R[i], R[e], ALU.mult).then_inc(sem("scaled_ready"), 1)
                    dve.wait_ge(sem("scaled_ready"), 6 * t + 6)
                    for i in range(6):
                        dve.wait_ge(sem("pm_full"), 6 * t + i + 1)
                        b = bank["pm_ready", 6 * t + i + 1]
                        par = i % 2
                        if i < 4:
                            mask = pair_mask[:, :, :].rearrange("p a b -> p (a b)")
                            o = F["ab" if i < 2 else "ak"][:, par::2, :]
                            tt(o, b[:, :].rearrange("p (h n) -> p h n", n=P), mask.unsqueeze(1).to_broadcast([P, 4, P]), ALU.mult).then_inc(sem("pm_ready"), 1)
                        else:
                            dve.tensor_copy(by_head(R["A"])[:, par::2, :], b[:, 0:256].rearrange("p (h n) -> p h n", n=HD)).then_inc(sem("pm_ready"), 1)
                    dve.wait_ge(sem("pm_ready"), 6 * t + 6)
                    over_heads = lambda m: m.unsqueeze(1).to_broadcast([P, HEADS, CHUNK])
                    step(tt(by_head(R["X"]), F["ab"][:, :, 0:CHUNK], over_heads(level_one[:, :]), ALU.mult))
                    step(tt(by_head(R["X"]), by_head(R["X"]), over_heads(eye64[:, :]), ALU.add))
                    step(tt(by_head(R["XT"]), by_head(R["A"]), over_heads(level_mask[:, 0, :]), ALU.mult))
                    step(tt(by_head(R["XT"]), by_head(R["XT"]), over_heads(eye64[:, :]), ALU.add))
                    tt(by_head(R["ot0"]), by_head(R["A"]), over_heads(level_mask[:, 1, :]), ALU.mult).then_inc(sem("inv_ready"), 1)
                    for n in range(5):
                        if n < 4:
                            step(tt(by_head(R[f"ot{(n + 1) % 2}"]), by_head(R["A"]), over_heads(level_mask[:, n + 2, :]), ALU.mult))
                        dve.wait_ge(sem("dx_full"), 9 * t + 2 * n + 1)
                        if n < 4:
                            dve.wait_ge(sem("dx_full"), 9 * t + 2 * n + 2)
                        tt(R["X"], R["X"], bank["dx_used", 9 * t + 2 * n + 1][:, :], ALU.add).then_inc(sem("dx_used"), 1)
                        if n < 4:
                            tt(R["XT"], R["XT"], bank["dx_used", 9 * t + 2 * n + 2][:, :], ALU.add).then_inc(sem("dx_used"), 1)
                        dve.wait_ge(sem("dx_used"), 9 * t + (2 * n + 2 if n < 4 else 9))
                    for c in range(2):
                        n = 2 * t + c
                        rows = slice(CHUNK * c, CHUNK * (c + 1))
                        dve.wait_ge(sem("end_ready"), t + 1)
                        decays = small[:, 224 + 8 * (t % 2):232 + 8 * (t % 2)].rearrange("p (a b) -> p a b", b=2)[:, :, c:c + 1].to_broadcast([P, 4, HD])
                        dve.wait_ge(sem("state_ready"), n + 1)
                        if n >= 1:
                            dve.wait_ge(sem("yc_full"), n)
                        step(tt(state[(n + 1) % 2], state[n % 2], decays, ALU.mult))
                        dve.wait_ge(sem("z_ready"), 4 * t + 2)
                        for par in range(2):
                            dve.wait_ge(sem("sa_full"), 2 * n + par + 1)
                            tt(by_head(R["SA"])[rows, par::2, :], bank["y_stored", 2 * n + par + 1][rows, 0:256]
                                   .rearrange("p (h n) -> p h n", n=HD), by_head(R["U"])[rows, par::2, :], ALU.add).then_inc(sem("sa_ready"), 1)
                        dve.wait_ge(sem("state_full"), n + 1)
                        tt(state[(n + 1) % 2], state[(n + 1) % 2],
                               bank["state_ready", n + 2][:, 0:256].rearrange("p (a b) -> p a b", b=HD), ALU.add).then_inc(sem("state_ready"), 1)
                        dve.wait_ge(sem("yc_full"), n + 1)
                        dve.wait_ge(sem("y_stored"), 2 * n + 2)
                        tt(R["y"][rows, :], R["y"][rows, :], bank["y_added", n + 1][rows, :], ALU.add).then_inc(sem("y_added"), 1)
                    dve.wait_ge(sem("y_added"), 2 * t + 2)
                    y = by_head(R["y"])
                    step(dve.tensor_reduce(small[:, 200:208], y, AX, ALU.add))
                    step(dve.tensor_scalar(small[:, 200:208], small[:, 200:208], -1.0 / HD, None, ALU.mult))
                    step(tt(y, y, spread(small[:, 200:208]), ALU.add))
                    step(tt(R["tmp"], R["y"], R["y"], ALU.mult))
                    step(dve.tensor_reduce(small[:, 208:216], by_head(R["tmp"]), AX, ALU.add))
                    inv_mean(small[:, 216:224], small[:, 208:216], 1.0 / HD, C_GN_EPS).then_inc(sem("gn_ms"), 1)
                    dve.wait_ge(sem("gn_rstd"), t + 1)
                    step(tt(y, y, spread(small[:, 216:224]), ALU.mult))
                    step(tt(R["y"], R["y"], bc["ln_w"], ALU.mult))
                    step(tt(R["y"], R["y"], bc["ln_b"], ALU.add))
                    step(tt(by_head(R["tmp"]), by_head(R["v"]), spread(small[:, 192:200]), ALU.mult))
                    step(tt(R["y"], R["y"], R["tmp"], ALU.add))
                    dve.wait_ge(sem("g_ready"), t + 1)
                    tt(R["y"], R["y"], R["g"], ALU.mult).then_inc(sem("yc_ready"), 1)

            if upto >= 5:
                dve.wait_ge(sem("mla_ss"), 1)
                step(dve.tensor_scalar(small[:, 160:164], small[:, 160:164], 1.0 / Q_RANK, RMS_EPS, ALU.mult, ALU.add))
                step(dve.tensor_scalar(small[:, 164:168], small[:, 164:168], 1.0 / KV_RANK, RMS_EPS, ALU.mult, ALU.add))
                dve.reciprocal(small[:, 160:168], small[:, 160:168]).then_inc(sem("mla_ms"), 1)
                dve.wait_ge(sem("mla_rstd"), 1)
                dve.wait_ge(sem("ycT_ready"), NT)
                for t in range(NT):
                    step(dve.tensor_scalar(qkvr[:, t, 0:Q_RANK], qkvr[:, t, 0:Q_RANK], small[:, 168 + t:169 + t], None, ALU.mult))
                    kv = qkvr[:, t, Q_RANK:Q_RANK + KV_RANK]
                    dve.tensor_scalar(kv, kv, small[:, 172 + t:173 + t], None, ALU.mult).then_inc(sem("qkvn_ready"), 1)
                for i in range(16):
                    step(dve.memset(small[:, 16 + i:17 + i], ROPE_THETA ** (-i / 16)))
                step(dve.tensor_copy(small[:, 240:244], small_i[:, 0:NT]))
                ang, turns = rope_cs[:, 0:4, :], rope_cs[:, 4:8, :]
                step(dve.tensor_copy(ang, small[:, 16:32].unsqueeze(1).to_broadcast([P, NT, 16])))
                step(tt(ang, ang, small[:, 240:244].unsqueeze(2).to_broadcast([P, NT, 16]), ALU.mult))
                step(dve.tensor_scalar(turns, ang, 1.0 / (2 * math.pi), MAGIC, ALU.mult, ALU.add))
                step(dve.tensor_scalar(turns, turns, -MAGIC, None, ALU.add))
                for part in TWO_PI:
                    step(dve.scalar_tensor_tensor(out=ang, in0=turns, scalar=-part, in1=ang, op0=ALU.mult, op1=ALU.add))
                step(dve.tensor_scalar(ang, ang, 3.1415925, -3.1415925, ALU.min, ALU.max))
                step(dve.scalar_tensor_tensor(out=turns, in0=ang, scalar=-1.0, in1=ang, op0=ALU.mult, op1=ALU.max))
                dve.tensor_scalar(turns, turns, -1.0, math.pi / 2, ALU.mult, ALU.add).then_inc(sem("angle_ready"), 1)
                for t in range(NT):
                    for i, (n, col) in enumerate(((3, 86), (2, 89))):
                        dve.wait_ge(sem("qnT_full"), 2 * t + i + 1)
                        o = (qnT if i == 0 else kvnT)[:, :, P * t:P * (t + 1)]
                        tt(o, bank["qnT_ready", 2 * t + i + 1][:, 0:P * n].rearrange("p (a b) -> p a b", b=P),
                               vc[:, col:col + n].unsqueeze(2).to_broadcast([P, n, P]), ALU.mult).then_inc(sem("qnT_ready"), 1)
                dve.wait_ge(sem("sin_ready"), 2)

                def rope(lo, hi, sin, cos, tmp):
                    step(tt(tmp[0], lo, sin, ALU.mult))
                    step(tt(tmp[1], hi, sin, ALU.mult))
                    step(tt(lo, lo, cos, ALU.mult))
                    step(tt(hi, hi, cos, ALU.mult))
                    step(tt(lo, lo, tmp[1], ALU.subtract))
                    tt(hi, hi, tmp[0], ALU.add).then_inc(sem("rope_ready"), 1)

                sin, cos = rope_cs[:, 0:4, :], rope_cs[:, 4:8, :]
                kr = qkvr[:, :, QKVR - ROPE:]
                rope(kr[:, :, 0:16], kr[:, :, 16:32], sin, cos, [rope_cs[:, 8:12, :], rope_cs[:, 12:16, :]])
                for t in range(NT):
                    dve.wait_ge(sem("ukv_full"), total("ukv_full", HEADS + t + 1))
                    dve.tensor_copy(v_d[:, t, :], bank["v_d_stored", t + 1][:, :]).then_inc(sem("v_d_stored"), 1)
                dve.wait_ge(sem("q_stored"), 8)
                tmp = [region(512 * i, NT, HEADS, 16) for i in range(2)]
                wide = [v.unsqueeze(2).to_broadcast([P, NT, HEADS, 16]) for v in (sin, cos)]
                rope(q_tok[:, :, :, HD:HD + 16], q_tok[:, :, :, HD + 16:], wide[0], wide[1], tmp)
                dve.wait_ge(sem("kpe_full"), total("kpe_full", 1))
                dve.tensor_copy(kT_d[HD:QD, :, :], bank["kpe_ready", 1][HD:QD, :].unsqueeze(1).to_broadcast([ROPE, HEADS, SEQ])).then_inc(sem("kpe_ready"), 1)
                attention(HEADS * NT, 4)
                out_proj(24, 16)

            if upto >= 6:
                norm(3)
                L, E2 = NT * N_EXPERTS, [P, NT, N_EXPERTS, N_EXPERTS]
                dve.wait_ge(sem("logit_full"), 1)
                dve.tensor_copy(logit, bank["logit_ready", 1][:, 0:L].rearrange("p (t e) -> p t e", e=N_EXPERTS)).then_inc(sem("logit_ready"), 1)
                dve.wait_ge(sem("logit_ready"), 1)
                step(dve.tensor_reduce(top, logit, AX, ALU.max))
                tt(ex, logit, top.unsqueeze(2).to_broadcast([P, NT, N_EXPERTS]), ALU.subtract).then_inc(sem("top_ready"), 1)
                other, own = logit.unsqueeze(2).to_broadcast(E2), logit.unsqueeze(3).to_broadcast(E2)
                step(tt(same, other, own, ALU.is_equal))
                step(tt(same, same, expert_lt[:, :, :].unsqueeze(1).to_broadcast(E2), ALU.mult))
                step(tt(more, other, own, ALU.is_gt))
                step(tt(more, more, same, ALU.add))
                step(dve.tensor_reduce(rank, more, AX, ALU.add))
                dve.tensor_scalar(sel, rank, TOP_K - 0.5, None, ALU.is_lt).then_inc(sem("sel_ready"), 1)
                dve.wait_ge(sem("sel_ready"), 1)
                dve.wait_ge(sem("ex_ready"), 1)
                step(tt(ex, ex, sel, ALU.mult))
                step(dve.tensor_reduce(top, ex, AX, ALU.add))
                step(dve.reciprocal(top, top))
                step(tt(gate, ex, top.unsqueeze(2).to_broadcast([P, NT, N_EXPERTS]), ALU.mult))
                dve.wait_ge(sem("place_full"), 1)
                b = bank["place_ready", 1]
                step(dve.scalar_tensor_tensor(out=place, in0=b[:, 0:L].rearrange("p (t e) -> p t e", e=N_EXPERTS), scalar=4096.0,
                                              in1=sel, op0=ALU.add, op1=ALU.mult))
                step(dve.tensor_scalar(place, place, -4096.0, None, ALU.add))
                by_round = lambda v: v.rearrange("p (r e) -> p r e", e=N_EXPERTS)
                tt(by_round(key_tmp), b[:, L:L + N_EXPERTS].unsqueeze(1).to_broadcast([P, MAX_ROUNDS, N_EXPERTS]),
                   by_round(cand[:, 1, :]), ALU.subtract).then_inc(sem("place_ready"), 1)
                dve.wait_ge(sem("place_ready"), 1)
                step(dve.tensor_scalar(key, cand[:, 2, :], 1.0 / 64, None, ALU.mult))
                for cap in CAPS[:-1]:
                    step(dve.scalar_tensor_tensor(out=key, in0=key_tmp, scalar=cap + 0.5, in1=key, op0=ALU.is_gt, op1=ALU.add))
                step(dve.tensor_scalar(key_tmp, key_tmp, 0.5, -float(len(CAPS)), ALU.is_gt, ALU.mult))
                step(tt(key, key, key_tmp, ALU.add))
                CC = [P, CANDIDATES, CANDIDATES]
                step(tt(rivals, key.unsqueeze(2).to_broadcast(CC), key.unsqueeze(1).to_broadcast(CC), ALU.is_gt))
                step(dve.tensor_reduce(pos, rivals, AX, ALU.add))
                upto_class = rivals[:, 0:len(CAPS), :]
                for i in range(len(CAPS)):
                    step(dve.tensor_scalar(rivals[:, i, :], key, i - 2.0, None, ALU.is_lt))
                step(dve.tensor_reduce(turn_ends[:, 0:3], upto_class, AX, ALU.add))
                step(dve.tensor_scalar(idle[:, 0:1], turn_ends[:, 0:1], 0.5, None, ALU.is_lt))
                step(tt(idle[:, 1:3], turn_ends[:, 1:3], turn_ends[:, 0:2], ALU.is_equal))
                for i in range(len(CAPS)):
                    step(tt(turn_ends[:, i:3], turn_ends[:, i:3], idle[:, i:i + 1].to_broadcast([P, 3 - i]), ALU.add))
                    if i < 2:
                        step(dve.tensor_scalar(key_tmp, key, i - 2.0, idle[:, i:i + 1], ALU.is_ge, ALU.mult))
                    else:
                        step(dve.tensor_scalar(key_tmp, key, 0.0, 4.0 * CANDIDATES, ALU.is_ge, ALU.mult))
                    step(tt(pos, pos, key_tmp, ALU.add))
                TC = [P, MAX_TURNS + 1, CANDIDATES]
                step(tt(at_turn[0], slot_no[:, 0:MAX_TURNS + 1].unsqueeze(2).to_broadcast(TC), pos.unsqueeze(1).to_broadcast(TC), ALU.is_equal))
                step(tt(at_turn[1], at_turn[0], cand[:, 0, :].unsqueeze(1).to_broadcast(TC), ALU.mult))
                step(dve.tensor_scalar(key_tmp, cand[:, 1, :], -IDLE, None, ALU.add))
                step(tt(at_turn[2], at_turn[0], key_tmp.unsqueeze(1).to_broadcast(TC), ALU.mult))
                step(dve.tensor_reduce(at_turn[0][:, :, 0], at_turn[1], AX, ALU.add))
                dve.tensor_copy(turn_expert_i[:, :], at_turn[0][:, :, 0]).then_inc(sem("w_low_ready"), RAW)
                step(dve.tensor_reduce(turn_off[:, :], at_turn[2], AX, ALU.add))
                dve.tensor_scalar(turn_off[:, :], turn_off[:, :], IDLE, None, ALU.add).then_inc(sem("moe_added"), 8)
                dve.wait_ge(sem("w_low_ready"), total("w_low_ready", RAW))
                dve.wait_ge(sem("moe_added"), 8)
                dve.tensor_copy(turn_ends_i[:, :], turn_ends[:, :]).then_inc(sem("turns_ready"), 1)
                dve.wait_ge(sem("turns_ready"), 1)
                ends = [dve.value_load(turn_ends_i[0:1, i:i + 1], min_val=i + 1, max_val=MAX_TURNS) for i in range(len(CAPS))]

                def place_slots(turn, ahead, cap):
                        e = dve.value_load(turn_expert_i[0:1, bass.ds(turn + ahead, 1)] if ahead else turn_expert_i[0:1, 0:1],
                                           min_val=0, max_val=N_EXPERTS - 1)
                        dve.tensor_scalar(own_place, place[:, :, bass.ds(e, 1)].rearrange("p t a -> p (t a)"),
                                          turn_off[:, bass.ds(turn + ahead, 1)] if ahead else turn_off[:, 0:1], None,
                                          ALU.subtract).then_inc(sem("own_place_ready"), 1)
                        dve.wait_ge(sem("own_place_ready"), turn + (ahead + 1))
                        for t in range(NT):
                            i = dve.tensor_scalar(pick[:, t, 0:cap], slot_no[:, 0:cap], own_place[:, t:t + 1], None, ALU.is_equal)
                        i.then_inc(sem("pick_ready"), 1)
                        dve.wait_ge(sem("pick_ready"), turn + (ahead + 1))

                def gathered(turn, ahead, cap):
                        for i in range(3):
                            n = min(3, KT - 3 * i)
                            dve.wait_ge(sem("xg_full"), turn * 3 + (3 * ahead + i + 1))
                            tt(xgT[:, 3 * i:3 * i + n, 0:cap], turn_banks[1 + i][:, 0:CAP * n].rearrange("p (a b) -> p a b", b=CAP)[:, :, 0:cap],
                                   vc[:, 24 + 3 * i:24 + 3 * i + n].unsqueeze(2).to_broadcast([P, n, cap]), ALU.mult).then_inc(sem("xg_ready"), 1)

                def gates(turn, cap, next_cap):
                        e = dve.value_load(turn_expert_i[0:1, bass.ds(turn, 1)], min_val=0, max_val=N_EXPERTS - 1)
                        for t in range(NT):
                            i = dve.tensor_scalar(pick_g[:, t, 0:cap], slot_no[:, 0:cap], own_place[:, t:t + 1], gate[:, t, bass.ds(e, 1)],
                                                          ALU.is_equal, ALU.mult)
                        i.then_inc(sem("pick_g_ready"), 1)
                        dve.wait_ge(sem("pick_g_ready"), turn + 1)
                        dve.wait_ge(sem("xg_full"), turn * 3 + 3)
                        place_slots(turn, 1, next_cap)

                def xg_parts(turn, ahead):
                        for i in range(3):
                            cols = slice(3 * i, min(3 * i + 3, KT))
                            dve.wait_ge(sem("xg_high_ready"), turn * 3 + total("xg_high_ready", 3 * ahead + i + 1))
                            tt(xg_low[:, cols, :], xgT[:, cols, 0:P], xg_high[:, cols, :].bitcast(F32), ALU.subtract).then_inc(sem("xg_split"), 1)

                def scattered(turn):
                        for i in range(8):
                            t, half = divmod(i, 2)
                            dve.wait_ge(sem("scatter_full"), turn * 8 + i + 1)
                            cols = slice(512 * half, 512 * half + 512)
                            tt(xs[:, t, cols], xs[:, t, cols], turn_banks[i % 4][:, :], ALU.add).then_inc(sem("moe_added"), 1)
                        dve.wait_ge(sem("moe_added"), turn * 8 + 16)

                def low(turn, n):
                        dve.wait_ge(sem("w_high_ready"), turn * TILES_E + total("w_high_ready", n + 1))
                        tt(w_low[n % SPLIT][:, :], raw_slots[n % RAW][:, :], w_high[n % SPLIT][:, :].bitcast(F32), ALU.subtract)\
                            .then_inc(sem("w_low_ready"), 1)

                def expert_split(turn):
                        gates(turn, P, CAPS[1])
                        for n, (kind, j) in enumerate(expert_order()):
                            turned = j - 1 if kind == "g" else j if j == GROUPS_E - 1 and kind == "d" else -1
                            if turned >= 0:
                                dve.wait_ge(sem("hid_high_ready"), turn * GROUPS_E + total("hid_high_ready", turned + 1))
                                tt(hid_low[:, turned % 2, :, :], acc[2 + turned % 2][:, 0:2 * P].rearrange("p (a b) -> p a b", b=P),
                                   hid_high[:, turned % 2, :, :].bitcast(F32), ALU.subtract).then_inc(sem("hid_split"), 1)
                            if kind == "u":
                                dve.wait_ge(sem("up_full"), turn * GROUPS_E + (FF_TILES + j + 1))
                                dve.wait_ge(sem("sil_ready"), turn * GROUPS_E + (FF_TILES + j + 1))
                                if j >= 2:
                                    dve.wait_ge(sem("hidT_full"), turn * GROUPS_E + (j - 1))
                                tt(hid_tok[:, j % 2, :], sil_e[:, j % 2, 0:256], turn_banks[(1 + 2 * j) % 4][:, 0:256], ALU.mult)\
                                    .then_inc(sem("hid_ready"), 1)
                            if n < TILES_E - 1:
                                low(turn, n + SPLIT)
                        gathered(turn, 1, CAPS[1])
                        low(turn, TILES_E - 1 + SPLIT)
                        xg_parts(turn, 1)
                        scattered(turn)

                def expert(turn, cap, next_cap):
                        gates(turn, cap, next_cap)
                        for j in range(GROUPS_E):
                            dve.wait_ge(sem("up_full"), turn * GROUPS_E + (FF_TILES + j + 1))
                            dve.wait_ge(sem("sil_ready"), turn * GROUPS_E + (FF_TILES + j + 1))
                            dve.wait_ge(sem("down_used"), turn * GROUPS_E + (10 + j - 1))
                            tt(pair_of(hid_e[:, j % 2, :], cap), pair_of(sil_e[:, j % 2, :], cap),
                               pair_of(turn_banks[(1 + 2 * j) % 4][:, 0:2 * CAP], cap), ALU.mult).then_inc(sem("hid_ready"), 1)
                        gathered(turn, 1, next_cap)
                        scattered(turn)

                place_slots(0, 0, CAPS[0])
                for n in range(SPLIT):
                    low(0, n)
                gathered(0, 0, CAPS[0])
                xg_parts(0, 0)
                with dve.Fori(0, ends[0]) as turn:
                    expert_split(turn)
                dve.tensor_copy(idle[:, 0:1], idle[:, 1:2]).then_inc(sem("splits_over"), 1)
                with dve.Fori(ends[0], ends[1]) as turn:
                    expert(turn, CAPS[1], CAPS[2])
                with dve.Fori(ends[1], ends[2]) as turn:
                    expert(turn, CAPS[2], CAPS[2])
                dve.tensor_copy(small[:, 7:8], turn_ends[:, 0:1]).then_inc(sem("moe_done"), 1)
                norm(4)
                dve.wait_ge(sem("final_loaded"), 16)
                for t in range(NT):
                    dve.scalar_tensor_tensor(out=y_out[:, t, :], in0=xs[:, t, :], scalar=small[:, 40 + t:41 + t], in1=final_w,
                                                 op0=ALU.mult, op1=ALU.mult).then_inc(sem("y_ready"), 1)


_OUT = (1, SEQ, D)


def kernel(**inputs):
    import numpy as np
    import concourse.bacc as bacc
    from concourse.bass_utils import run_bass_kernel_spmd

    nc = bacc.Bacc("TRN2", target_bir_lowering=False, num_devices=1)
    arrays, args = {}, {}
    for name, value in inputs.items():
        a = np.ascontiguousarray(value)
        arrays[f"in_{name}_dram"] = a
        args[name] = nc.dram_tensor(f"in_{name}_dram", a.shape, mybir.dt.from_np(a.dtype), kind="ExternalInput").ap()
    args["out"] = nc.dram_tensor("out_0_dram", _OUT, F32, kind="ExternalOutput").ap()
    hybrid_trunk(nc, **args)
    r = run_bass_kernel_spmd(nc, [arrays], core_ids=[0])
    return r.results[0]["out_0_dram"]
```

```python
import math
from contextlib import ExitStack

import concourse.bass as bass
from concourse import mybir

F32 = mybir.dt.float32
F32R = mybir.dt.float32r
I32 = mybir.dt.int32
ALU = mybir.AluOpType
ACT = mybir.ActivationFunctionType
AX = mybir.AxisListType.X

P = 128
SEQ, D = 512, 1024
NT = SEQ // P
KT = D // P
CHUNK = 64
RMS_EPS = 1e-6
HEADS, HD = 8, 64
REL_CLIP = 256
A_COLS = 3 * HEADS * HD
B_WIDTH, B_STATE, B_GROUPS, B_CONV = 512, 128, 2, 4
B_CONV_CH = B_WIDTH + 2 * B_GROUPS * B_STATE
CONV_TILES = B_CONV_CH // P
DT_COL = A_COLS + B_WIDTH + B_CONV_CH
B_NORM_EPS = 1e-5
FF = 2816
FF_TILES = FF // P
C_WIDTH = 512
C_IN = 3 * C_WIDTH + 64 + 64 + 128
C_TILES = C_IN // P
C_GN_EPS = 64e-5
Q_RANK, KV_RANK, ROPE = 384, 256, 32
QKVR = Q_RANK + KV_RANK + ROPE
QD = HD + ROPE
MLA_SCALE = QD ** -0.5
ROPE_THETA = 10000.0
N_EXPERTS, TOP_K, FF_E = 8, 2, 3584
FE_TILES = FF_E // P
GROUPS_E = FE_TILES // 2
CAPS = (P, 144, 168)
CAP = CAPS[-1]
CAP2 = CAP - P
MAX_ROUNDS = -(-SEQ // CAP)
CANDIDATES = MAX_ROUNDS * N_EXPERTS
MAX_TURNS = (TOP_K * SEQ + N_EXPERTS * (CAP - 1)) // CAP + len(CAPS) - 1
IDLE = 8192.0
TILES_E = 3 * GROUPS_E
MASKED = -1e30
DECAY_RATE = -math.exp(-0.5)
SLOTS = 7
DENSE_RAW, DENSE_SPLIT = 3, 2
RAW, SPLIT = 6, 3
SPLIT_PHASES = (("e_in",), ("e_out",), ("ff_g", "ff_u", "ff_d"), ("o_in",), ("o_out",))
E_IN, E_OUT, FFN, O_IN, O_OUT = range(5)
NORM_PHASE = {0: E_IN, 1: FFN, 2: O_IN}
EVEN_PARTS, FF_PARTS, ODD_PARTS, EXPERT_PARTS = 1, 9, 9 + FF_TILES, 17 + FF_TILES
SLOT = 2048
MAGIC = 1.5 * 2.0 ** 23
TWO_PI = (6.28125, 0.00193500518798828125, 3.0199159819e-07)


class Banks:

    def __init__(self, banks, start):
        self.banks, self.n, self.read = banks, 0, [start] * len(banks)

    def open(self, signal, count):
        i = self.n % len(self.banks)
        former, self.read[i] = self.read[i], (signal, count)
        self.n += 1
        return self.banks[i], former


class Steps:

    def __init__(self, eng, sem):
        self.eng, self.sem, self.n, self.turn, self.size = eng, sem, 0, None, 0

    def __call__(self, instruction):
        self.n += 1
        instruction.then_inc(self.sem, 1)
        value = self.n if self.turn is None else self.turn * self.size + self.n
        self.eng.wait_ge(self.sem, value)


COUNTS_ON = {
    "pc_full": ("conv_full", 8), "pc_stored": ("conv_stored", 8), "qkvr_full": ("v_full", 8), "qkvr_stored": ("v_stored", 8),
    "ycT_full": ("ynT_full", 4), "rkv_full": ("x_tok_full", 4), "lora_full": ("cb_full", 8), "cum_full": ("row_full", 16),
    "end_full": ("dt_col_full", 1), "ft_full": ("ssd_full", 8), "uq_full": ("z_full", 8), "ukv_full": ("qk_full", 8),
    "w_high_ready": ("dense_high_ready", 64), "w_low_ready": ("dense_low_ready", 64), "xg_high_ready": ("h_high_ready", 24),
    "xg_split": ("h_low_ready", 24), "hid_high_ready": ("part_high", EXPERT_PARTS), "hid_split": ("part_low", EXPERT_PARTS),
    "kpe_full": ("dt_full", 1), "rkv_ready": ("x_tok_ready", 4), "wa_sum": ("cb_ready", 8),
}


def total(name, count):
    return count + COUNTS_ON.get(name, (name, 0))[1]


def weight_order():
    w = [("e_in", c) for c in range(12)] + [("e_out", c) for c in range(4)]
    for c in range(FF_TILES // 2):
        w += [("ff_g", c), ("ff_u", c)]
    w += [("ff_d", half, c) for half in range(2) for c in range(6)]
    w += [("o_in", c) for c in range(10)]
    w += [("uq", 0), ("uq", 1), ("ukv", 0)]
    w += [("o_out", c) for c in range(4)]
    return w


def split_tiles():
    return [[n for n, item in enumerate(weight_order()) if item[0] in kinds] for kinds in SPLIT_PHASES]


def splits_before(n):
    return sum(m < n for phase in split_tiles() for m in phase)


def phase_splits(phase):
    first = sum(len(tiles) for tiles in split_tiles()[:phase])
    return first, first + len(split_tiles()[phase]) - 1


def expert_order():
    w = [("g", 0), ("u", 0)]
    for j in range(1, GROUPS_E):
        w += [("g", j), ("u", j), ("d", j - 1)]
    return w + [("d", GROUPS_E - 1)]


def last_use(item):
    kind, c = item[0], item[-1]
    if kind == "e_in":
        name, per, first = [("qk_full", 2, 0), ("v_full", 4, 4), ("z_full", 4, 6), ("conv_full", 2, 8)][
            0 if c < 4 else 1 if c < 6 else 2 if c < 8 else 3]
        return name, per * (c - first + 1)
    if kind == "o_in":
        return ("pc_full", 2 * (c + 1)) if c < 7 else ("qkvr_full", 4 * (c - 6))
    if kind in ("e_out", "o_out"):
        return "mix_full", 4 * (c + 1) + (16 if kind == "o_out" else 0)
    if kind in ("ff_g", "ff_u"):
        return ("gate_full" if kind == "ff_g" else "up_full"), 2 * (c + 1)
    if kind == "ff_d":
        return ("down_used", 5 * item[1] + c + 1) if c < 5 else ("down_full", 4 * (item[1] + 1))
    return {"uq": ("uq_full", 4 * (c + 1)), "ukv": ("ukv_full", 12)}[kind]


def expert_tile_used(n):
    kind, j = expert_order()[n]
    name, done = {"g": ("gate_full", FF_TILES), "u": ("up_full", FF_TILES), "d": ("down_used", 10)}[kind]
    return name, done + j + 1 - (0 if n >= 0 else GROUPS_E)


class Ring:

    def __init__(self, slots, landed, before=None, turn=None, size=0):
        self.slots, self.landed, self.before = slots, landed, before or [0] * len(slots)
        self.n, self.turn, self.size = 0, turn, size
        assert size % len(slots) == 0

    def load(self, eng, view, source):
        slot = self.n % len(self.slots)
        eng.dma_start(view(self.slots[slot]), source).then_inc(self.landed[slot], 16)
        self.n += 1

    def take(self):
        slot = self.n % len(self.slots)
        value = 16 * (self.before[slot] + self.n // len(self.slots) + 1)
        if self.turn is not None:
            value = self.turn * (16 * self.size // len(self.slots)) + value
        self.n += 1
        return self.slots[slot], (self.landed[slot], value)


def expert_ring(slots, landed, turn):
    n = len(weight_order())
    return Ring(slots, landed[:RAW], [len(range(i, n, DENSE_RAW)) if i < DENSE_RAW else 0 for i in range(RAW)], turn, TILES_E)


def hybrid_trunk(nc, x, positions, e_norm_mix, e_w_in, a_rel_bias, b_conv_w, b_conv_b, b_dt_bias,
                 b_a_log, b_d_skip, b_norm_w, e_w_out, e_norm_ffn, ff_w_gate, ff_w_up, ff_w_down,
                 o_norm_mix, o_w_in, c_mu, c_w0, c_w2, c_a0, c_a2, c_g2, c_k_k, c_k_a, c_r_k,
                 c_ln_w, c_ln_b, d_q_norm, d_w_uq, d_kv_norm, d_w_ukv, o_w_out, o_norm_ffn,
                 moe_router, moe_w_gate, moe_w_up, moe_w_down, final_norm, out, upto=99):
    ctx = ExitStack()
    with ctx:
        def sb(name, shape, dt=F32):
            return ctx.enter_context(nc.sbuf_tensor(name, shape, dt))

        assert sum(len(tiles) for tiles in split_tiles()) == COUNTS_ON["w_low_ready"][1]
        sems, bank = {}, {}

        def sem(name):
            name = COUNTS_ON.get(name, (name,))[0]
            if name not in sems:
                sems[name] = ctx.enter_context(nc.semaphore(name))
            return sems[name]

        slots, slot_at = [], []
        for i in range(SLOTS):
            slots.append(sb(f"slot{i}", [P, SLOT]))
            slot_at.append(nc.sbuf_base - 4 * SLOT)
        xs = sb("xs", [P, NT, D])
        ident = sb("ident", [P, P])
        flip = sb("flip", [P, P])
        chunk_mask = sb("chunk_mask", [P, P])
        causal_mask = sb("causal_mask", [P, P])
        cum_incl = sb("cum_incl", [P, P])
        cum_excl = sb("cum_excl", [P, P])
        cum_rev = sb("cum_rev", [P, P])
        chunk_sum = sb("chunk_sum", [P, 2])
        before = sb("before", [P, P])
        ones = sb("ones", [P, P])
        pair_mask = sb("pair_mask", [P, 2, CHUNK])
        level_mask = sb("level_mask", [P, 6, CHUNK])
        level_one = sb("level_one", [P, CHUNK])
        eye64 = sb("eye64", [P, CHUNK])
        slot_no = sb("slot_no", [P, CAP])
        vec_rows = sb("vec_rows", [P, P])
        vc = sb("vc", [P, 95])
        w_dt = sb("w_dt", [P, KT, HEADS])
        w_dt_high, w_dt_low = sb("w_dt_high", [P, KT, HEADS], F32R), sb("w_dt_low", [P, KT, HEADS], F32R)
        w_router = sb("w_router", [P, KT, N_EXPERTS])
        lora = sb("lora", [P, 2, C_WIDTH])
        small = sb("small", [P, 256])
        small_i = sb("small_i", [P, 16], I32)
        expert_lt = sb("expert_lt", [P, N_EXPERTS, N_EXPERTS])
        cand = sb("cand", [P, 3, CANDIDATES])
        turn_off = sb("turn_off", [P, MAX_TURNS + 1])
        turn_ends = sb("turn_ends", [P, 3])
        idle = sb("idle", [P, 3])
        turn_expert_i = sb("turn_expert_i", [P, MAX_TURNS + 1], I32)
        turn_ends_i = sb("turn_ends_i", [P, 3], I32)

        ARENA = 30600
        arena = sb("arena", [P, ARENA])
        arena_at = nc.sbuf_base - 4 * ARENA

        def rounded(name, at, *shape):
            return nc.alloc_sbuf_tensor_at(name, [P, *shape], F32R, offset=at)

        def region(at, *shape, rows=P):
            n = math.prod(shape)
            assert at + n <= ARENA, (at, shape)
            v = arena[0:rows, at:at + n]
            if len(shape) == 2:
                v = v.rearrange("p (a b) -> p a b", b=shape[1])
            if len(shape) == 3:
                v = v.rearrange("p (a b c) -> p a b c", b=shape[1], c=shape[2])
            return v

        head_row = lora[0:HEADS, :, :].rearrange("p a b -> p (a b)").rearrange("p (a b) -> p a b", b=P)
        hT = region(0, KT, SEQ)
        xn = region(4096, NT, D)
        yT = region(4096, KT, SEQ)
        qT, kT = region(8192, 4, SEQ), region(10240, 4, SEQ)
        v_a, zs = region(12288, NT, C_WIDTH), region(14336, NT, B_WIDTH)
        bias_w = region(16384, HEADS, SEQ)
        conv_in = region(20480, CONV_TILES, SEQ + B_CONV - 1)
        conv_out = region(24600, CONV_TILES, SEQ)
        probs = region(28696, 3, SEQ)
        probsT = [region(2048 * i, NT, SEQ) for i in range(2)]
        bias_ext = region(24600, 640, rows=HEADS)
        x_tok, xdt = region(8192, NT, B_WIDTH), region(10240, NT, B_WIDTH)
        y_tok, cbT = region(12288, NT, B_WIDTH), region(16384, B_GROUPS, NT, SEQ)
        decay = [region(20480 + 2048 * i, NT, SEQ) for i in range(2)]
        wT = [region(24600 + 2048 * i, NT, SEQ) for i in range(2)]
        dt_row = [region(28696 + 512 * i, SEQ, rows=HEADS) for i in range(3)]
        sqd = region(0, D)
        y_squares = region(2048, NT, 256)
        squares = [region(28696 if j in (1, 3) else 0, D) for j in range(5)]
        hid = region(8192, FF_TILES, SEQ)
        sil = region(19456, 2, SEQ)
        BC = 27000
        bc = {n: region(BC + 512 * i, C_WIDTH) for i, n in enumerate(["w0", "a0", "k_k", "k_a", "r_k", "ln_w", "ln_b"])}
        pcT = region(8192, C_TILES, SEQ + 1)
        qkvr = region(15376, NT, QKVR)
        rw = 18064
        mixdiff = region(rw, 2, SEQ)
        free_rows = list(range(0, 4096, 512)) + list(range(6144, 8192, 512)) + list(range(rw, BC - 511, 512))
        R, F = {}, {}
        F["ar"] = arena[:, 0:1024].rearrange("p (a b c) -> p a b c", b=2, c=P)
        F["ab"] = arena[:, 1024:2048].rearrange("p (a b) -> p a b", b=P)
        F["ak"] = arena[:, 2048:3072].rearrange("p (a b) -> p a b", b=P)
        names = ["r", "k", "sig", "a", "kk", "b", "Eex", "Ein", "Eni", "Erev", "rt", "bt", "kt", "tmp",
                 "al0", "al1", "bh0", "bh1", "kh0", "kh1", "v0", "v1", "g0", "g1",
                 "X", "XT", "Y1", "ot0", "ot1", "Z1", "U", "SA", "y", "A", "wt", "btT", "ktT", "state", "mla"]
        rows_of_512 = [region(at, C_WIDTH) for at in free_rows[6:]]
        rows_of_512 += [slots[i][:, C_WIDTH * j:C_WIDTH * (j + 1)] for i in range(DENSE_RAW, SLOTS) for j in range(SLOT // C_WIDTH)]
        for i, name in enumerate(names):
            R[name] = rows_of_512[i]

        for name in ("btT", "ktT"):
            F[name] = R[name].rearrange("p (a b) -> p a b", b=P)
        F["wt"] = R["wt"].rearrange("p (a b) -> p a b", b=P)
        bonus = [small[:, 192:200], small[:, 240:248]]
        state = [R["state"][:, 256 * i:256 * (i + 1)].rearrange("p (a b) -> p a b", b=HD) for i in range(2)]

        q_tok = region(8192, NT, HEADS, QD)
        qT_d = region(18064, HEADS, SEQ, rows=QD)
        kT_d = region(22160, HEADS, SEQ, rows=QD)
        v_d = region(11264, NT, C_WIDTH)
        qnT, kvnT = region(26256, 3, SEQ), region(13312, 2, SEQ)
        rope_cs = region(14336, 16, 16)
        E0 = 8192
        pick = region(E0, NT, CAP)
        pick_g = region(E0 + 672, NT, CAP)
        pickT = region(E0 + 1344, 2, SEQ)
        xgT = region(E0 + 2368, KT, CAP)
        sil_e = region(E0 + 3712, 2, 2 * CAP)
        hid_e = region(E0 + 4384, 2, 2 * CAP)
        outT = region(E0 + 5056, KT, CAP)
        out_tok = region(E0 + 6400, 2, D)
        final_w = region(E0 + 8448, D)
        y_out = region(E0 + 9472, NT, D)
        M0 = E0 + 13568
        logit, ex, gate, place, rank, sel = [region(M0 + 32 * i, NT, N_EXPERTS) for i in range(6)]
        same, more = [region(M0 + 256 * (1 + i), NT, N_EXPERTS * N_EXPERTS).rearrange("p t (e j) -> p t e j", j=N_EXPERTS)
                      for i in range(2)]
        top = region(M0 + 1024, NT)
        own_place = region(M0 + 1028, NT)
        key, pos, key_tmp = [region(M0 + 1040 + 32 * i, CANDIDATES) for i in range(3)]
        rivals = region(M0 + 1200, CANDIDATES, CANDIDATES)
        at_turn = [region(M0 + 2300 + 544 * i, MAX_TURNS + 1, CANDIDATES) for i in range(3)]
        w_high = [rounded(f"w_high{i}", at, SLOT) for i, at in enumerate((slot_at[3], slot_at[4], arena_at))]
        w_low = [rounded(f"w_low{i}", at, SLOT) for i, at in enumerate((slot_at[5], slot_at[6], arena_at + 4 * SLOT))]
        raw_slots = slots[:3] + [region(E0 + 9472 + SLOT * i, SLOT) for i in range(2)] + [region(M0 + 1200, SLOT)]
        S0 = 25600
        assert M0 + 1200 + SLOT <= S0 and len(raw_slots) == RAW
        xg_high, xg_low = rounded("xg_high", arena_at + 4 * S0, KT, P), rounded("xg_low", arena_at + 4 * (S0 + 1024), KT, P)
        hid_tok = region(S0 + 2048, 2, 2 * P)
        hid_high = rounded("hid_high", arena_at + 4 * (S0 + 2560), 2, 2, P)
        hid_low = rounded("hid_low", arena_at + 4 * (S0 + 3072), 2, 2, P)
        h_high, h_low = rounded("h_high", arena_at + 4 * 4096, KT, SEQ), rounded("h_low", arena_at, KT, SEQ)
        y_low = rounded("y_low", arena_at + 4 * 4096, KT, SEQ)
        y_high_even = rounded("y_high_even", arena_at, KT, SEQ)
        odd_rows = [8192 + SEQ * k for k in range(6)] + [15376 + SEQ * k for k in range(2)]
        y_high_odd = [rounded(f"y_high_odd{k}", arena_at + 4 * at, SEQ) for k, at in enumerate(odd_rows)]
        ff_low = rounded("ff_low", arena_at + 4 * 8192, FF_TILES, SEQ)
        ff_rows = [20480 + SEQ * f for f in range(12)] + [SEQ * f for f in range(FF_TILES - 12)]
        ff_high = [rounded(f"ff_high{f}", arena_at + 4 * at, SEQ) for f, at in enumerate(ff_rows)]
        ones_row, dt_keep = region(6144, SEQ, rows=HEADS), region(6656, SEQ, rows=HEADS)

        banks = [ctx.enter_context(nc.psum_tensor(f"bank{i}", [P, 512], F32)) for i in range(8)]
        turn_banks, acc = banks[0:4], banks[4:8]

        ext_d = nc.dram_tensor("bias_ext_d", [HEADS, 640], F32)

        def cols8(dram, lo, n):
            return dram[:, lo:lo + n].rearrange("(k p) n -> p k n", p=P)

        def pair_of(view, cap):
            return view.rearrange("p (a b) -> p a b", b=CAP)[:, :, 0:cap]

        landed = [sem(f"landed{i}") for i in range(SLOTS)]

        block = ctx.enter_context(nc.Block())

        @block.sync
        def _(sp):
            w = Ring(slots[:DENSE_RAW], landed[:DENSE_RAW])
            xv = x[0].rearrange("(t p) d -> p t d", p=P)
            for t in range(NT):
                sp.dma_start(xs[:, t, :], xv[:, t, :]).then_inc(sem("x_loaded"), 16)
            row = 0
            for dram, n in ((e_norm_mix, 8), (e_norm_ffn, 8), (o_norm_mix, 8), (o_norm_ffn, 8), (b_conv_b, 8)):
                sp.dma_start(vec_rows[row:row + n, :], dram[0].rearrange("(k p) -> k p", p=P)).then_inc(sem("vec_loaded"), 16)
                row += n
            for tap in range(B_CONV):
                sp.dma_start(vec_rows[row:row + 8, :], b_conv_w[0, tap].rearrange("(k p) -> k p", p=P)).then_inc(sem("vec_loaded"), 16)
                row += 8
            for dram, n in ((c_mu, 14), (d_q_norm, 3), (d_kv_norm, 2), (b_norm_w, 4)):
                sp.dma_start(vec_rows[row:row + n, :], dram[0].rearrange("(k p) -> k p", p=P)).then_inc(sem("vec_loaded"), 16)
                row += n
            assert row == 95

            def load(kind, *c):
                if kind in ("e_in", "o_in", "e_out", "o_out", "ff_g", "ff_u"):
                    dram = {"e_in": e_w_in, "o_in": o_w_in, "e_out": e_w_out, "o_out": o_w_out,
                            "ff_g": ff_w_gate, "ff_u": ff_w_up}[kind]
                    n = min(256, dram.shape[2] - 256 * c[0])
                    w.load(sp, lambda s: s[:, 0:KT * n].rearrange("p (k n) -> p k n", n=n),
                           cols8(dram[0], 256 * c[0], n))
                elif kind == "ff_d":
                    half, j = c
                    n = min(4, FF_TILES - 4 * j)
                    w.load(sp, lambda s: s[:, 0:n * 512].rearrange("p (k n) -> p k n", n=512),
                           ff_w_down[0, 4 * j * P:(4 * j + n) * P, 512 * half:512 * half + 512]
                           .rearrange("(k p) n -> p k n", p=P))
                elif kind == "uq":
                    w.load(sp, lambda s: s[:, 0:3 * 384].rearrange("p (k n) -> p k n", n=384),
                           cols8(d_w_uq[0], 384 * c[0], 384))
                elif kind == "ukv":
                    w.load(sp, lambda s: s[:, :].rearrange("p (k n) -> p k n", n=1024),
                           cols8(d_w_ukv[0], 0, 1024))

            order = weight_order()
            last_item = {1: ("e_in", 11), 2: ("e_out", 3), 3: ("ff_d", 1, 5), 4: ("o_in", 9)}.get(upto)
            for n, item in enumerate(order):
                if item == ("ff_d", 0, 0):
                    sp.wait_ge(sem("mix_full"), 16)
                    sp.dma_start(lora[0:64, 0, :], c_w2[0]).then_inc(sem("lora_loaded"), 16)
                    sp.dma_start(lora[64:128, 0, :], c_a2[0]).then_inc(sem("lora_loaded"), 16)
                    sp.dma_start(lora[:, 1, :], c_g2[0]).then_inc(sem("lora_loaded"), 16)
                    for i, dram in enumerate((c_w0, c_a0, c_k_k, c_k_a, None, c_ln_w, c_ln_b)):
                        src = dram[0:1, :] if dram is not None else c_r_k[0:1].rearrange("a h d -> a (h d)")
                        sp.dma_start(region(BC + 512 * i, C_WIDTH), src.to_broadcast([P, C_WIDTH])).then_inc(sem("bc_loaded"), 16)
                if n >= DENSE_RAW:
                    former = n - DENSE_RAW
                    if splits_before(former + 1) > splits_before(former):
                        sp.wait_ge(sem("dense_low_ready"), splits_before(former + 1))
                    else:
                        name, count = last_use(order[former])
                        sp.wait_ge(sem(name), total(name, count))
                load(*item)
                if item == last_item:
                    break
            if upto >= 6:
                sp.wait_ge(sem("mix_full"), 32)
                sp.dma_start(final_w, final_norm.rearrange("(a n) -> a n", a=1).to_broadcast([P, D])).then_inc(sem("final_loaded"), 16)
                sp.wait_ge(sem("turns_ready"), 1)
                ends = [sp.value_load(turn_ends_i[0:1, i:i + 1], min_val=i + 1, max_val=MAX_TURNS) for i in range(len(CAPS))]

                def expert(turn, split):
                    e = sp.value_load(turn_expert_i[0:1, bass.ds(turn, 1)], min_val=0, max_val=N_EXPERTS - 1)
                    ring = expert_ring(raw_slots, landed, turn)
                    for n, (kind, j) in enumerate(expert_order()):
                        if split:
                            sp.wait_ge(sem("w_low_ready"), turn * TILES_E + total("w_low_ready", n + 1))
                        else:
                            if n == RAW:
                                sp.wait_ge(sem("splits_over"), 1)
                            name, count = expert_tile_used(n - RAW)
                            sp.wait_ge(sem(name), turn * GROUPS_E + count)
                        if kind in ("g", "u"):
                            dram = moe_w_gate if kind == "g" else moe_w_up
                            ring.load(sp, lambda s: s[:, :].rearrange("p (k n) -> p k n", n=256),
                                      dram[0, bass.ds(e, 1), :, 256 * j:256 * j + 256].rearrange("a (k p) n -> p (a k) n", p=P))
                        else:
                            ring.load(sp, lambda s: s[:, :].rearrange("p (k n) -> p k n", n=D),
                                      moe_w_down[0, bass.ds(e, 1), 256 * j:256 * j + 256, :].rearrange("a (k p) n -> p (a k) n", p=P))

                with sp.Fori(0, ends[0]) as turn:
                    expert(turn, True)
                with sp.Fori(ends[0], ends[2]) as turn:
                    expert(turn, False)
                sp.wait_ge(sem("y_ready"), NT)
                sp.dma_start(out[0].rearrange("(t p) d -> p t d", p=P), y_out).then_inc(sem("stored"), 16)
                sp.wait_ge(sem("stored"), 16)

        @block.gpsimd
        def _(pool):
            link = Steps(pool, sem("pool_step"))

            def select(view, op, fill, base, pattern, mult):
                link(pool.affine_select(out=view, in_=view, compare_op=op, fill=fill, base=base,
                                        pattern=pattern, channel_multiplier=mult))

            link(pool.memset(ident[:, :], 0.0))
            pool.affine_select(out=ident[:, :], in_=ident[:, :], compare_op=ALU.not_equal, fill=1.0, base=0,
                               pattern=[[-1, P]], channel_multiplier=1).then_inc(sem("ident_ready"), 1)
            for k in range(KT):
                pool.dma_start(w_dt[:, k, :], e_w_in[0, k * P:(k + 1) * P, DT_COL:DT_COL + HEADS]).then_inc(sem("w_dt_loaded"), 16)
            pool.dma_start(w_router[:, :, :], moe_router[0].rearrange("(k p) e -> p k e", p=P)).then_inc(sem("router_loaded"), 16)
            pool.dma_start(small[0:HEADS, 0:1], b_dt_bias[0].rearrange("(h a) -> h a", a=1)).then_inc(sem("small_loaded"), 16)
            pool.dma_start(small[0:HEADS, 1:2], b_a_log[0].rearrange("(h a) -> h a", a=1)).then_inc(sem("small_loaded"), 16)
            pool.dma_start(small[:, 8:16], b_d_skip[0:1, :].to_broadcast([P, HEADS])).then_inc(sem("small_loaded"), 16)
            pool.dma_start(small_i[:, 0:NT], positions[0].rearrange("(t p) -> p t", p=P),
                           allow_slow_non_contiguous=True).then_inc(sem("small_loaded"), 16)

            pool.dma_start(bias_ext[:, 0:384], a_rel_bias[0, :, 129:513]).then_inc(sem("rel_loaded"), 16)
            pool.wait_ge(sem("rel_loaded"), 16)
            link(pool.tensor_copy(bias_ext[:, 384:640], bias_ext[:, 383:384].to_broadcast([HEADS, 256])))
            pool.dma_start(ext_d[:, :], bias_ext).then_inc(sem("rel_stored"), 16)
            pool.wait_ge(sem("rel_stored"), 16)
            for h in range(HEADS):
                src = bass.AP(ext_d, 640 * h, [[1, P], [1, SEQ]])
                pool.dma_start(bias_w[:, h, :], src).then_inc(sem("bias_loaded"), 16)

            link(pool.memset(flip[:, :], 0.0))
            select(flip[:, :], ALU.not_equal, 1.0, -(P - 1), [[1, P]], 1)
            link(pool.memset(chunk_mask[:, :], 0.0))
            link(pool.memset(chunk_mask[0:CHUNK, CHUNK:P], MASKED))
            link(pool.memset(causal_mask[:, :], 0.0))
            select(causal_mask[:, :], ALU.is_ge, MASKED, 0, [[1, P]], -1)
            link(pool.memset(ones[:, :], 1.0))
            link(pool.memset(before[:, :], 1.0))
            select(before[:, :], ALU.is_gt, 0.0, 0, [[1, P]], -1)
            for m, op, sign in ((cum_incl, ALU.is_ge, 1), (cum_excl, ALU.is_gt, 1), (cum_rev, ALU.is_gt, -1)):
                link(pool.memset(m[:, :], DECAY_RATE))
                select(m[:, :], op, 0.0, 0, [[sign, P]], -sign)
                if sign > 0:
                    link(pool.memset(m[0:CHUNK, CHUNK:P], 0.0))
                else:
                    link(pool.memset(m[CHUNK:P, 0:CHUNK], 0.0))
            link(pool.memset(chunk_sum[:, :], 0.0))
            for c in range(2):
                link(pool.memset(chunk_sum[CHUNK * c:CHUNK * (c + 1), c:c + 1], DECAY_RATE))
            link(pool.memset(pair_mask[:, :, :], 1.0))
            link(pool.memset(level_mask[:, :, :], 1.0))
            link(pool.memset(level_one[:, :], 1.0))
            link(pool.memset(eye64[:, :], 0.0))
            for c in range(2):
                rows = slice(CHUNK * c, CHUNK * (c + 1))
                select(pair_mask[rows, 0, :], ALU.is_gt, 0.0, 0, [[1, CHUNK]], -1)
                select(pair_mask[rows, 1, :], ALU.is_ge, 0.0, 0, [[1, CHUNK]], -1)
                select(eye64[rows, :], ALU.not_equal, 1.0, 0, [[-1, CHUNK]], 1)
                v = level_one[rows, :].rearrange("p (b c) -> p b c", c=2)
                select(v, ALU.is_equal, 0.0, 0, [[-2, CHUNK // 2], [0, 2]], 1)
                link(pool.memset(v[:, :, 0:1], 0.0))
                for n in range(6):
                    s = 1 << n
                    v = level_mask[rows, n, :].rearrange("p (b c) -> p b c", c=2 * s)
                    link(pool.memset(v[:, :, s:2 * s], 0.0))
                    select(v, ALU.is_ge, 0.0, -s, [[-2 * s, CHUNK // (2 * s)], [0, 2 * s]], 1)
                    select(v, ALU.is_ge, 0.0, 2 * s - 1, [[2 * s, CHUNK // (2 * s)], [0, 2 * s]], -1)
            link(pool.iota(slot_no[:, :], [[1, CAP]], base=0, channel_multiplier=0, allow_small_or_imprecise_dtypes=True))
            iota = dict(base=0, channel_multiplier=0, allow_small_or_imprecise_dtypes=True)
            link(pool.iota(cand[:, 0, :].rearrange("p (r e) -> p r e", e=N_EXPERTS), [[0, MAX_ROUNDS], [1, N_EXPERTS]], **iota))
            link(pool.iota(cand[:, 1, :].rearrange("p (r e) -> p r e", e=N_EXPERTS), [[CAP, MAX_ROUNDS], [0, N_EXPERTS]], **iota))
            link(pool.iota(cand[:, 2, :], [[1, CANDIDATES]], **iota))
            link(pool.memset(expert_lt[:, :, :], 1.0))
            select(expert_lt[:, :, :], ALU.is_gt, 0.0, 0, [[1, N_EXPERTS], [-1, N_EXPERTS]], 0)
            link(pool.memset(head_row[:, :, :], 0.0))
            select(head_row[:, :, :], ALU.not_equal, 1.0, 0, [[-1, HEADS], [0, P]], 1)
            pool.memset(conv_in[:, :, 0:B_CONV - 1], 0.0).then_inc(sem("const_ready"), 1)


        @block.tensor
        def _(pe):
            w = Ring(slots[:DENSE_RAW], landed[:DENSE_RAW])
            turn_bank = Banks(turn_banks, (sem("ident_ready"), 1))

            def tile(name, count):
                bank[name, count], former = turn_bank.open(sem(name), total(name, count))
                return bank[name, count], former

            def mm(o, lhsT, rhs, start):
                return pe.matmul(o, lhsT, rhs, start=start, stop=True, skip_group_check=True)

            def tp(o, i, rows=P):
                return pe.transpose(o, i, ident[0:rows, 0:rows])

            def norm(j):
                for t in range(NT):
                    pe.wait_ge(sem("xn_ready"), NT * j + t + 1)
                    for half in range(2):
                        b, former = tile("hT_ready", 8 * j + 2 * t + half + 1)
                        pe.wait_ge(*former)
                        for k in range(4):
                            m = tp(b[:, P * k:P * (k + 1)], xn[:, t, P * (4 * half + k):P * (4 * half + k + 1)])
                        m.then_inc(sem("xnT_full"), 1)
                pe.wait_ge(sem("hT_ready"), 8 * (j + 1))

            def by_feature(slab, cols, rhs, o, kt=KT, fresh=True):
                for k in range(kt):
                    m = mm(o, slab[:, k, cols], rhs[:, k, :], fresh and k == 0)
                return m

            def by_token(lhs, t, slab, o, kt=KT):
                for k in range(kt):
                    m = mm(o, lhs[:, k, P * t:P * (t + 1)], slab[:, k, :], k == 0)
                return m

            def split_product(o, left, right, start):
                mm(o, left[0], right[0], start)
                mm(o, left[0], right[1], False)
                return mm(o, left[1], right[0], False)

            def split_slab(n=256, kt=KT):
                s = splits_before(w.n)
                w.n += 1
                parts = [v[s % DENSE_SPLIT][:, 0:kt * n].rearrange("p (k n) -> p k n", n=n) for v in (w_high, w_low)]
                return parts, (sem("dense_low_ready"), s + 1)

            def by_feature_split(parts, cols, o, phase=None):
                for k in range(KT):
                    if phase is not None:
                        pe.wait_ge(sem("h_low_ready"), KT * phase + k + 1)
                    m = split_product(o, [v[:, k, cols] for v in parts], (h_high[:, k, :], h_low[:, k, :]), k == 0)
                return m

            def by_token_split(parts, t, o):
                for k in range(KT):
                    m = split_product(o, [v[:, k, P * t:P * (t + 1)] for v in (h_high, h_low)], [v[:, k, :] for v in parts], k == 0)
                return m

            def out_proj(base, high, waits):
                for c in range(4):
                    parts, here = split_slab()
                    pe.wait_ge(*here)
                    for t in range(NT):
                        if c == 0:
                            pe.wait_ge(sem("part_low"), waits[t])
                        b, former = tile("x_added", base + 4 * c + t + 1)
                        pe.wait_ge(*former)
                        for k in range(KT):
                            now = slice(P * t, P * (t + 1))
                            m = split_product(b[:, 0:256], (high[k][:, now], y_low[:, k, now]), [v[:, k, :] for v in parts], k == 0)
                        m.then_inc(sem("mix_full"), 1)

            def slab_of(n=256, kt=KT):
                slot, here = w.take()
                return slot[:, 0:kt * n].rearrange("p (k n) -> p k n", n=n), here

            def attention(first, score, value, done):
                for i in range(HEADS * NT + 3):
                    if i < HEADS * NT:
                        b, former = tile("probs_ready", first + i + 1)
                        pe.wait_ge(*former)
                        score(b, i // NT, i % NT).then_inc(sem("scores_full"), 1)
                    u = i - 3
                    if u >= 0 and u % NT == NT - 1:
                        h = u // NT
                        pe.wait_ge(sem("probsT_ready"), first + u + 1)
                        pair = h // 2
                        if h % 2 == 0 and pair >= 2:
                            pe.wait_ge(sem("yT_ready"), done + pair - 1)
                        rows = slice(64 * (h % 2), 64 * (h % 2) + 64)
                        for k in range(NT):
                            m = mm(acc[pair % 2][rows, P * k:], value(h, k), probsT[h % 2][:, k, P * k:], k == 0)
                        m.then_inc(sem("pv_done"), 1)
                    u = i - 2
                    if 0 <= u < HEADS * NT:
                        pe.wait_ge(sem("probs_scaled"), first + u + 1)
                        b, former = tile("probsT_ready", first + u + 1)
                        pe.wait_ge(*former)
                        for k in range(u % NT + 1):
                            m = tp(b[:, P * k:P * (k + 1)], probs[:, u % 3, P * k:P * (k + 1)])
                        m.then_inc(sem("probsT_full"), 1)

            pe.wait_ge(sem("ident_ready"), 1)
            pe.wait_ge(sem("vec_loaded"), 16 * 13)
            b, former = tile("vc_ready", 1)
            pe.wait_ge(*former)
            tp(b[:, 0:95], vec_rows[0:95, :], 95).then_inc(sem("vec_full"), 1)

            norm(0)
            for c in range(12):
                parts, here = split_slab()
                pe.wait_ge(*here)
                if c < 4 or c >= 8:
                    full, stored = ("qk_full", "qk_stored") if c < 4 else ("conv_full", "conv_stored")
                    for m in range(2):
                        b, former = tile(stored, 2 * (c % 8) + m + 1)
                        pe.wait_ge(*former)
                        by_feature_split(parts, slice(P * m, P * (m + 1)), b[:, :], 0 if c == m == 0 else None).then_inc(sem(full), 1)
                else:
                    full, stored = ("v_full", "v_stored") if c < 6 else ("z_full", "z_stored")
                    for t in range(NT):
                        b, former = tile(stored, 4 * (c % 2) + t + 1)
                        pe.wait_ge(*former)
                        by_token_split(parts, t, b[:, 0:256]).then_inc(sem(full), 1)
            pe.wait_ge(sem("part_low"), 1)
            b, former = tile("u_ready", 1)
            pe.wait_ge(*former)
            by_feature_split((w_dt_high, w_dt_low), slice(0, HEADS), b[0:HEADS, :]).then_inc(sem("dt_full"), 1)

            if upto >= 2:
                pe.wait_ge(sem("const_ready"), 1)
                pe.wait_ge(sem("bias_loaded"), 16 * HEADS)
                pe.wait_ge(sem("qk_stored"), 8)
                pe.wait_ge(sem("v_stored"), 8)

                def score_a(b, h, t):
                    rows = slice(64 * (h % 2), 64 * (h % 2) + 64)
                    mm(b[:, 0:P * (t + 1)], qT[rows, h // 2, P * t:P * (t + 1)], kT[rows, h // 2, 0:P * (t + 1)], True)
                    for k in range(t + 1):
                        mm(b[:, P * k:P * (k + 1)], bias_w[:, h, P * (t - k):P * (t - k + 1)], flip[:, :], False)
                    return mm(b[:, P * t:P * (t + 1)], ident[:, :], chunk_mask[:, :], False)

                attention(0, score_a, lambda h, k: v_a[:, k, HD * h:HD * (h + 1)], 0)

                pe.wait_ge(sem("conv_ready"), CONV_TILES)
                for t in range(NT):
                    b, former = tile("x_tok_ready", t + 1)
                    pe.wait_ge(*former)
                    for c in range(4):
                        m = tp(b[:, P * c:P * (c + 1)], conv_out[:, c, P * t:P * (t + 1)])
                    m.then_inc(sem("x_tok_full"), 1)
                for g in range(B_GROUPS):
                    for j in range(NT):
                        b, former = tile("cb_ready", NT * g + j + 1)
                        pe.wait_ge(*former)
                        mm(b[:, P * j:], conv_out[:, 4 + g, P * j:P * (j + 1)], conv_out[:, 6 + g, P * j:], True)\
                            .then_inc(sem("cb_full"), 1)
                pe.wait_ge(sem("cum_ready"), 1)
                b, former = tile("dt_col_ready", 1)
                pe.wait_ge(*former)
                for j in range(NT):
                    tp(b[:, HEADS * j:HEADS * (j + 1)], dt_row[2][:, P * j:P * (j + 1)], HEADS)
                    m = tp(b[:, 32 + HEADS * j:32 + HEADS * (j + 1)], dt_row[0][:, P * j:P * (j + 1)], HEADS)
                m.then_inc(sem("dt_col_full"), 1)
                for h in range(HEADS + 1):
                    if h < HEADS:
                        for masked in range(2):
                            b, former = tile("decay_ready", 7 * h + (7 if masked else 5))
                            pe.wait_ge(*former)
                            m = mm(b[:, :], head_row[:, h, :], dt_row[1], True)
                            if masked:
                                for j in range(NT):
                                    m = mm(b[:, P * j:P * (j + 1)], ident[:, :], causal_mask[:, :], False)
                            m.then_inc(sem("row_full"), 1)
                    if h >= 1:
                        g = h - 1
                        pe.wait_ge(sem("w_ready"), NT * (g + 1))
                        b, former = tile("y_tok_ready", g + 1)
                        pe.wait_ge(*former)
                        for l in range(NT):
                            for j in range(l + 1):
                                m = mm(b[:, HD * l:HD * (l + 1)], wT[g % 2][:, j, P * l:P * (l + 1)],
                                       xdt[:, j, HD * g:HD * (g + 1)], l == 0)
                        m.then_inc(sem("ssd_full"), 1)
                for t in range(NT):
                    pe.wait_ge(sem("yn_ready"), t + 1)
                    b, former = tile("yT_b_ready", t + 1)
                    pe.wait_ge(*former)
                    for c in range(4):
                        m = tp(b[:, P * c:P * (c + 1)], y_tok[:, t, P * c:P * (c + 1)])
                    m.then_inc(sem("ynT_full"), 1)
                pe.wait_ge(sem("yT_ready"), 4)
                pe.wait_ge(sem("yT_b_ready"), 4)
                out_proj(0, [y_high_even[:, k, :] for k in range(KT)], [EVEN_PARTS + 4 + t + 1 for t in range(NT)])

            if upto >= 3:
                norm(1)
                for c in range(FF_TILES // 2):
                    for full, stored in (("gate_full", "sil_ready"), ("up_full", "hid_ready")):
                        parts, here = split_slab()
                        pe.wait_ge(*here)
                        for m in range(2):
                            b, former = tile(stored, 2 * c + m + 1)
                            pe.wait_ge(*former)
                            by_feature_split(parts, slice(P * m, P * (m + 1)), b[:, :],
                                             1 if c == m == 0 and full == "gate_full" else None).then_inc(sem(full), 1)
                for half in range(2):
                    for c in range(6):
                        n = min(4, FF_TILES - 4 * c)
                        parts, here = split_slab(512, n)
                        pe.wait_ge(*here)
                        for k in range(n):
                            f = 4 * c + k
                            if half == 0:
                                pe.wait_ge(sem("part_low"), FF_PARTS + f + 1)
                            for t in range(NT):
                                if half and f == 0:
                                    pe.wait_ge(sem("x_added"), 16 + t + 1)
                                now = slice(P * t, P * (t + 1))
                                m = split_product(acc[t][:, :], (ff_high[f][:, now], ff_low[:, f, now]), [v[:, k, :] for v in parts], f == 0)
                                if f == FF_TILES - 1:
                                    m.then_inc(sem("down_full"), 1)
                        if c < 5:
                            m.then_inc(sem("down_used"), 1)

            if upto >= 4:
                norm(2)
                for c in range(7):
                    parts, here = split_slab()
                    pe.wait_ge(*here)
                    for m in range(2):
                        b, former = tile("pc_stored", 2 * c + m + 1)
                        pe.wait_ge(*former)
                        by_feature_split(parts, slice(P * m, P * (m + 1)), b[:, :], 2 if c == m == 0 else None).then_inc(sem("pc_full"), 1)
                for c in range(3):
                    n = 256 if c < 2 else QKVR - 512
                    parts, here = split_slab(n)
                    pe.wait_ge(*here)
                    for t in range(NT):
                        b, former = tile("qkvr_stored", 4 * c + t + 1)
                        pe.wait_ge(*former)
                        by_token_split(parts, t, b[:, 0:n]).then_inc(sem("qkvr_full"), 1)

                pe.wait_ge(sem("lora_loaded"), 48)
                quad = lambda c: slice(64 * c, 64 * c + 64)
                def prepare(t, piece):
                    now = slice(1 + P * t, 1 + P * (t + 1))
                    if piece == 0:
                        pe.wait_ge(sem("mixed"), C_TILES)
                        for a in range(3):
                            b, former = tile("rkv_ready", 3 * t + a + 1)
                            pe.wait_ge(*former)
                            for k in range(4):
                                m = tp(b[:, P * k:P * (k + 1)], pcT[:, 4 * a + k, now])
                            m.then_inc(sem("rkv_full"), 1)
                    if piece == 1:
                        pe.wait_ge(sem("lora_in_ready"), 2)
                        for a in range(2):
                            b, former = tile("wa_sum", 2 * t + a + 1)
                            pe.wait_ge(*former)
                            mm(b[:, :], pcT[quad(a), 12, now], lora[quad(a), 0, :], True).then_inc(sem("lora_full"), 1)
                        b, former = tile("g_ready", t + 1)
                        pe.wait_ge(*former)
                        mm(b[:, :], pcT[:, 13, now], lora[:, 1, :], True).then_inc(sem("lora_full"), 1)
                    if piece == 2:
                        pe.wait_ge(sem("sig_ready"), 2 * t + 1)
                        for i, tri in enumerate((cum_excl, cum_incl, cum_rev)):
                            b, former = tile("exp_ready", 4 * t + (1, 3, 4)[i])
                            pe.wait_ge(*former)
                            mm(b[:, :], tri[:, :], R["sig"], True).then_inc(sem("cum_full"), 1)
                        b, former = tile("end_ready", t + 1)
                        pe.wait_ge(*former)
                        for k in range(4):
                            m = mm(b[:, 2 * k:2 * k + 2], R["sig"][:, P * k:P * (k + 1)], chunk_sum[:, :], k == 0)
                        m.then_inc(sem("end_full"), 1)

                def outputs_by_feature(t):
                    pe.wait_ge(sem("yc_ready"), t + 1)
                    b, former = tile("ycT_ready", t + 1)
                    pe.wait_ge(*former)
                    for k in range(4):
                        m = tp(b[:, P * k:P * (k + 1)], R["y"][:, P * k:P * (k + 1)])
                    m.then_inc(sem("ycT_full"), 1)

                for piece in range(3):
                    prepare(0, piece)
                for t in range(NT):
                    for i, name in enumerate((f"al{t % 2}", "rt", "bt", "kt")):
                        pe.wait_ge(sem("scaled_ready"), 6 * t + i + 1)
                        b, former = tile("ft_ready", 4 * t + i + 1)
                        pe.wait_ge(*former)
                        for k in range(4):
                            m = tp(b[:, P * k:P * (k + 1)], R[name][:, P * k:P * (k + 1)])
                        m.then_inc(sem("ft_full"), 1)
                    pe.wait_ge(sem("ft_ready"), 4 * (t + 1))
                    for i, lhs in enumerate(("btT", "ktT")):
                        for par in range(2):
                            b, former = tile("pm_ready", 6 * t + 2 * i + par + 1)
                            pe.wait_ge(*former)
                            for pair in range(4):
                                for c in range(2):
                                    m = mm(b[quad(c), P * pair:P * (pair + 1)], F[lhs][quad(par), pair, quad(c)],
                                           F["ar"][quad(par), pair, c, :], pair == 0)
                            m.then_inc(sem("pm_full"), 1)
                    for par in range(2):
                        b, former = tile("pm_ready", 6 * t + 5 + par)
                        pe.wait_ge(*former)
                        for pair in range(4):
                            for c in range(2):
                                m = mm(b[quad(c), HD * pair:HD * (pair + 1)], F["ar"][quad(par), pair, c, 0:CHUNK],
                                       F["btT"][quad(par), pair, quad(c)], pair == 0)
                        m.then_inc(sem("pm_full"), 1)

                    def each(b, lhs, rhs, half=None, first=True):
                        for h in range(HEADS) if half is None else range(4 * half, 4 * half + 4):
                            for c in range(2):
                                m = mm(b[quad(c), HD * h:HD * (h + 1)], lhs(h, c), rhs(h, c), h == (4 * half if half else 0) and first)
                        return m

                    def at(name):
                        return lambda h, c: R[name][quad(c), HD * h:HD * (h + 1)]

                    if t >= 1:
                        outputs_by_feature(t - 1)
                    for n in range(5):
                        if n == 0:
                            pe.wait_ge(sem("inv_ready"), t + 1)
                        else:
                            pe.wait_ge(sem("dx_used"), 9 * t + 2 * n - 1)
                        for half in range(2):
                            if t or n:
                                pe.wait_ge(sem("y1_ready"), 10 * t + 2 * n + half - 1)
                            each(acc[half], at(f"ot{n % 2}"), at("X"), half).then_inc(sem("y1_full"), 1)
                        if n > 0:
                            pe.wait_ge(sem("dx_used"), 9 * t + 2 * n)
                        b, former = tile("dx_used", 9 * t + 2 * n + 1)
                        pe.wait_ge(*former)
                        for half in range(2):
                            pe.wait_ge(sem("y1_ready"), 10 * t + 2 * n + half + 1)
                            m = each(b, at("XT"), at("Y1"), half, half == 0)
                        m.then_inc(sem("dx_full"), 1)
                        if n < 4:
                            b, former = tile("dx_used", 9 * t + 2 * n + 2)
                            pe.wait_ge(*former)
                            each(b, at("Y1"), at("XT")).then_inc(sem("dx_full"), 1)
                        if t + 1 < NT and n < 3:
                            prepare(t + 1, n)
                    b, former = tile("z_ready", 4 * t + 1)
                    pe.wait_ge(*former)
                    each(b, lambda h, c: F["ak"][quad(c), h, 0:CHUNK], at(f"v{t % 2}")).then_inc(sem("zu_full"), 1)
                    pe.wait_ge(sem("dx_used"), 9 * t + 9)
                    pe.wait_ge(sem("z_ready"), 4 * t + 1)
                    b, former = tile("z_ready", 4 * t + 2)
                    pe.wait_ge(*former)
                    each(b, at("X"), at("Z1")).then_inc(sem("zu_full"), 1)
                    for c in range(2):
                        b, former = tile("z_ready", 4 * t + 3 + c)
                        pe.wait_ge(*former)
                        for h in range(HEADS):
                            m = mm(b[quad(h % 2), CHUNK * (h // 2):CHUNK * (h // 2 + 1)], at(f"al{t % 2}")(h, c), at("X")(h, c), h < 2)
                        m.then_inc(sem("zu_full"), 1)
                    pe.wait_ge(sem("z_ready"), 4 * t + 4)
                    pe.wait_ge(sem("scaled_ready"), 6 * t + 6)
                    for c in range(2):
                        n = 2 * t + c
                        S = state[n % 2]
                        pe.wait_ge(sem("state_ready"), n + 1)
                        for par in range(2):
                            b, former = tile("y_stored", 2 * n + par + 1)
                            pe.wait_ge(*former)
                            for pair in range(4):
                                mm(b[quad(c), HD * pair:HD * (pair + 1)], F["wt"][quad(par), pair, quad(c)],
                                   S[quad(par), pair, :], pair == 0)
                            for pair in range(4):
                                m = mm(b[quad(c), 256 + HD * pair:256 + HD * (pair + 1)], F["ar"][quad(par), pair, c, CHUNK:],
                                       S[quad(par), pair, :], False)
                            m.then_inc(sem("sa_full"), 1)
                        by, former = tile("y_added", n + 1)
                        pe.wait_ge(*former)
                        bs, former = tile("state_ready", n + 2)
                        pe.wait_ge(*former)
                        for h in range(HEADS):
                            mm(bs[quad(h % 2), HD * (h // 2):HD * (h // 2 + 1)], at(f"kh{t % 2}")(h, c), at(f"v{t % 2}")(h, c), h < 2)
                        for h in range(HEADS):
                            mm(by[quad(c), HD * h:HD * (h + 1)], F["ak"][quad(c), h, CHUNK:], at(f"v{t % 2}")(h, c), h == 0)
                        pe.wait_ge(sem("sa_ready"), 2 * n + 2)
                        for h in range(HEADS):
                            m = mm(bs[quad(h % 2), HD * (h // 2):HD * (h // 2 + 1)], at(f"bh{t % 2}")(h, c), at("SA")(h, c), False)
                        m.then_inc(sem("state_full"), 1)
                        for h in range(HEADS):
                            m = mm(by[quad(c), HD * h:HD * (h + 1)], F["ab"][quad(c), h, CHUNK:], at("SA")(h, c), False)
                        m.then_inc(sem("yc_full"), 1)
                outputs_by_feature(NT - 1)

            if upto >= 5:
                for t in range(NT):
                    pe.wait_ge(sem("qkvn_ready"), t + 1)
                    for i, (lo, n) in enumerate(((0, 3), (Q_RANK, 2))):
                        b, former = tile("qnT_ready", 2 * t + i + 1)
                        pe.wait_ge(*former)
                        for k in range(n):
                            m = tp(b[:, P * k:P * (k + 1)], qkvr[:, t, lo + P * k:lo + P * (k + 1)])
                        m.then_inc(sem("qnT_full"), 1)
                pe.wait_ge(sem("qnT_ready"), 8)
                for half in range(2):
                    slab, here = slab_of(384, 3)
                    pe.wait_ge(*here)
                    for t in range(NT):
                        b, former = tile("q_stored", 4 * half + t + 1)
                        pe.wait_ge(*former)
                        by_token(qnT, t, slab, b[:, 0:384], 3).then_inc(sem("uq_full"), 1)
                slab, here = slab_of(1024, 2)
                pe.wait_ge(*here)
                for h in range(HEADS):
                    b, former = tile("kn_stored", h + 1)
                    pe.wait_ge(*former)
                    by_feature(slab, slice(P * h, P * h + HD), kvnT, b[0:HD, :], 2).then_inc(sem("ukv_full"), 1)
                vals = slab.rearrange("p k (h n) -> p k h n", n=P)[:, :, :, HD:P]
                for t in range(NT):
                    b, former = tile("v_d_stored", t + 1)
                    pe.wait_ge(*former)
                    by_token(kvnT, t, vals, b[:, :].rearrange("p (h n) -> p h n", n=HD), 2).then_inc(sem("ukv_full"), 1)
                pe.wait_ge(sem("rope_ready"), 2)
                b, former = tile("kpe_ready", 1)
                pe.wait_ge(*former)
                for t in range(NT):
                    m = tp(b[0:QD, P * t:P * (t + 1)], qkvr[:, t, QKVR - QD:QKVR])
                m.then_inc(sem("kpe_full"), 1)
                for h in range(HEADS):
                    b, former = tile("qT_ready", h + 1)
                    pe.wait_ge(*former)
                    for t in range(NT):
                        m = tp(b[0:QD, P * t:P * (t + 1)], q_tok[:, t, h, :])
                    m.then_inc(sem("qT_full"), 1)
                pe.wait_ge(sem("qT_ready"), HEADS)
                pe.wait_ge(sem("kpe_ready"), 1)
                pe.wait_ge(sem("kn_stored"), HEADS)
                pe.wait_ge(sem("v_d_stored"), NT)

                def score_d(b, h, t):
                    mm(b[:, 0:P * (t + 1)], qT_d[:, h, P * t:P * (t + 1)], kT_d[:, h, 0:P * (t + 1)], True)
                    return mm(b[:, P * t:P * (t + 1)], ident[:, :], chunk_mask[:, :], False)

                attention(HEADS * NT, score_d, lambda h, k: v_d[:, k, HD * h:HD * (h + 1)], 4)
                pe.wait_ge(sem("yT_ready"), 8)
                pe.wait_ge(sem("ycT_ready"), NT)
                out_proj(24, [v[:, :] for v in y_high_odd], [ODD_PARTS + KT] * NT)

            if upto >= 6:
                norm(3)
                pe.wait_ge(sem("router_loaded"), 16)
                b, former = tile("logit_ready", 1)
                pe.wait_ge(*former)
                for t in range(NT):
                    for k in range(KT):
                        m = mm(b[:, 8 * t:8 * t + 8], hT[:, k, P * t:P * (t + 1)], w_router[:, k, :], t == 0 and k == 0)
                m.then_inc(sem("logit_full"), 1)
                pe.wait_ge(sem("sel_ready"), 1)
                b, former = tile("place_ready", 1)
                pe.wait_ge(*former)
                for t in range(NT + 1):
                    for s in range(min(t + 1, NT)):
                        m = mm(b[:, 8 * t:8 * t + 8], (before if s == t else ones)[:, :], sel[:, s, :], t == 0)
                m.then_inc(sem("place_full"), 1)
                pe.wait_ge(sem("place_ready"), 1)
                pe.wait_ge(sem("turns_ready"), 1)
                ends = [pe.value_load(turn_ends_i[0:1, i:i + 1], min_val=i + 1, max_val=MAX_TURNS) for i in range(len(CAPS))]

                def gather(turn, ahead, cap):
                        pe.wait_ge(sem("pick_ready"), turn + (ahead + 1))
                        for i in range(3):
                            b = turn_banks[1 + i]
                            for d in range(3 * i, min(3 * i + 3, KT)):
                                for t in range(NT):
                                    m = mm(b[:, CAP * (d % 3):CAP * (d % 3) + cap], xn[:, t, P * d:P * (d + 1)], pick[:, t, 0:cap],
                                           d % 3 == 0 and t == 0)
                            m.then_inc(sem("xg_full"), 1)

                def turn_gates(turn, cap):
                        pe.wait_ge(sem("pick_g_ready"), turn + 1)
                        for t in range(NT):
                            m = tp(turn_banks[0][:, P * t:P * (t + 1)], pick_g[:, t, 0:P])
                        m.then_inc(sem("pickT_full"), 1 if cap > P else 2)
                        if cap > P:
                            for t in range(NT):
                                m = tp(acc[3][0:cap - P, P * t:P * (t + 1)], pick_g[:, t, P:cap])
                            m.then_inc(sem("pickT_full"), 1)

                def scatter(turn, cap):
                        pe.wait_ge(sem("pickT_ready"), turn * 2 + 2)
                        pe.wait_ge(sem("outT_ready"), turn * 3 + 3)
                        pe.wait_ge(sem("out_tok_ready"), turn * 4 + 4)
                        pe.wait_ge(sem("xg_ready"), turn * 3 + 6)
                        for i in range(2 * NT):
                            t, half = divmod(i, 2)
                            if i >= 4:
                                pe.wait_ge(sem("moe_added"), turn * 8 + (8 + i - 3))
                            b = turn_banks[i % 4]
                            cols = slice(512 * half, 512 * half + 512)
                            m = mm(b[:, :], pickT[:, 0, P * t:P * (t + 1)], out_tok[:, 0, cols], True)
                            if cap > P:
                                m = mm(b[:, :], pickT[0:cap - P, 1, P * t:P * (t + 1)], out_tok[0:cap - P, 1, cols], False)
                            m.then_inc(sem("scatter_full"), 1)

                def turn_tokens(turn, cap, next_cap):
                        pe.wait_ge(sem("sil_ready"), turn * GROUPS_E + (FF_TILES + GROUPS_E))
                        pe.wait_ge(sem("hid_ready"), turn * GROUPS_E + (FF_TILES + GROUPS_E))
                        turn_gates(turn, cap)
                        gather(turn, 1, next_cap)

                def open_banks(turn):
                        ebank = Banks(turn_banks, None)
                        ebank.read = [(sem("moe_added"), turn * 8 + (5 + i)) for i in range(4)]

                        def etile(name, count):
                            return ebank.open(sem(name), turn * GROUPS_E + count)

                        return etile

                def expert_split(turn):
                        etile = open_banks(turn)
                        pe.wait_ge(sem("xg_split"), turn * 3 + total("xg_split", 3))

                        def up(n, j, full, stored):
                            b, former = etile(stored, FF_TILES + j + 1)
                            pe.wait_ge(sem("w_low_ready"), turn * TILES_E + total("w_low_ready", RAW + n + 1))
                            pe.wait_ge(*former)
                            wh, wl = [v[n % SPLIT][:, :].rearrange("p (k n) -> p k n", n=256) for v in (w_high, w_low)]
                            for k in range(KT):
                                m = split_product(b[:, 0:256], (xg_high[:, k, :], xg_low[:, k, :]), (wh[:, k, :], wl[:, k, :]), k == 0)
                            m.then_inc(sem(full), 1)

                        def turn_hidden(j):
                            pe.wait_ge(sem("hid_ready"), turn * GROUPS_E + (FF_TILES + j + 1))
                            for k in range(2):
                                m = tp(acc[2 + j % 2][:, P * k:P * (k + 1)], hid_tok[:, j % 2, P * k:P * (k + 1)])
                            m.then_inc(sem("hidT_full"), 1)

                        def down(n, j):
                            pe.wait_ge(sem("w_low_ready"), turn * TILES_E + total("w_low_ready", RAW + n + 1))
                            pe.wait_ge(sem("hid_split"), turn * GROUPS_E + total("hid_split", j + 1))
                            wh, wl = [v[n % SPLIT][:, :].rearrange("p (k n) -> p k n", n=D) for v in (w_high, w_low)]
                            for k in range(2):
                                for half in range(2):
                                    cols = slice(512 * half, 512 * half + 512)
                                    m = split_product(acc[half][:, :], (hid_high[:, j % 2, k, :], hid_low[:, j % 2, k, :]),
                                                      (wh[:, k, cols], wl[:, k, cols]), j == 0 and k == 0)
                                    if j == k == half == 0:
                                        m.then_inc(sem("out_tok_full"), 4)
                            m.then_inc(sem("down_used"), 1)

                        for n, (kind, j) in enumerate(expert_order()):
                            if kind == "g":
                                up(n, j, "gate_full", "sil_ready")
                                if j >= 1:
                                    turn_hidden(j - 1)
                            elif kind == "u":
                                up(n, j, "up_full", "hid_ready")
                            else:
                                if j == GROUPS_E - 1:
                                    turn_hidden(j)
                                down(n, j)
                        turn_tokens(turn, P, CAPS[1])
                        scatter(turn, P)

                def expert(turn, cap, next_cap):
                        w = expert_ring(raw_slots, landed, turn)
                        etile = open_banks(turn)
                        pe.wait_ge(sem("xg_ready"), turn * 3 + 3)

                        def slab_of(n=256, kt=KT):
                            slot, here = w.take()
                            return slot[:, 0:kt * n].rearrange("p (k n) -> p k n", n=n), here

                        def up(j):
                            for full, stored, first in (("gate_full", "sil_ready", FF_TILES), ("up_full", "hid_ready", FF_TILES)):
                                slab, here = slab_of()
                                pe.wait_ge(*here)
                                b, former = etile(stored, first + j + 1)
                                pe.wait_ge(*former)
                                for m in range(2):
                                    last = by_feature(slab, slice(P * m, P * (m + 1)), xgT[:, :, 0:cap], b[:, CAP * m:CAP * m + cap],
                                                      fresh=m == 0)
                                last.then_inc(sem(full), 1)

                        def down(j):
                            slab, here = slab_of(D, 2)
                            pe.wait_ge(*here)
                            pe.wait_ge(sem("hid_ready"), turn * GROUPS_E + (FF_TILES + j + 1))
                            for k in range(2):
                                for d in range(KT):
                                    m = mm(acc[d // 3][:, CAP * (d % 3):CAP * (d % 3) + cap], slab[:, k, P * d:P * (d + 1)],
                                           hid_e[:, j % 2, CAP * k:CAP * k + cap], j == 0 and k == 0 and d % 3 == 0)
                            m.then_inc(sem("down_used"), 1)

                        up(0)
                        for j in range(1, GROUPS_E):
                            up(j)
                            down(j - 1)
                        down(GROUPS_E - 1)
                        turn_tokens(turn, cap, next_cap)
                        pe.wait_ge(sem("outT_ready"), turn * 3 + 3)
                        pe.wait_ge(sem("pickT_ready"), turn * 2 + 2)
                        pe.wait_ge(sem("xg_ready"), turn * 3 + 6)
                        for i, (rows, lo, half) in enumerate(((P, 0, 0), (P, 0, 1), (cap - P, P, 0), (cap - P, P, 1))):
                            for d in range(4 * half, 4 * half + 4):
                                m = tp(turn_banks[i][0:rows, P * (d % 4):P * (d % 4 + 1)], outT[:, d, lo:lo + rows])
                            m.then_inc(sem("out_tok_full"), 1)
                        scatter(turn, cap)

                gather(0, 0, CAPS[0])
                with pe.Fori(0, ends[0]) as turn:
                    expert_split(turn)
                with pe.Fori(ends[0], ends[1]) as turn:
                    expert(turn, CAPS[1], CAPS[2])
                with pe.Fori(ends[1], ends[2]) as turn:
                    expert(turn, CAPS[2], CAPS[2])

        @block.scalar
        def _(act):
            step = Steps(act, sem("act_step"))

            def high_dense(s):
                order = [n for phase in split_tiles() for n in phase]
                n = order[s]
                act.wait_ge(landed[n % DENSE_RAW], 16 * (n // DENSE_RAW + 1))
                if s >= DENSE_SPLIT:
                    name, count = last_use(weight_order()[order[s - DENSE_SPLIT]])
                    act.wait_ge(sem(name), total(name, count))
                act.activation(w_high[s % DENSE_SPLIT][:, 0:SLOT], slots[n % DENSE_RAW][:, 0:SLOT], ACT.Copy).then_inc(sem("dense_high_ready"), 1)

            def next_high(phase, c):
                first, last = phase_splits(phase)
                if first + c + DENSE_SPLIT <= last:
                    high_dense(first + c + DENSE_SPLIT)

            def norm(j):
                first = 768 if j in (1, 3) else 512
                for part in range(2):
                    cols = slice(0, first) if part == 0 else slice(first, D)
                    for t in range(NT):
                        if j == 0:
                            act.wait_ge(sem("x_loaded"), 16 * NT)
                        elif j < 4:
                            act.wait_ge(sem("x_added"), (None, (8, 12), (16, 20), (32, 36))[j][part] + t + 1)
                        i = act.activation(squares[j][:, cols], xs[:, t, cols], ACT.Square, accum_out=small[:, (248, 32)[part] + t:(249, 33)[part] + t])
                        if part == 1 and t == NT - 1:
                            i.then_inc(sem("ss_ready"), 1)
                        else:
                            step(i)
                act.wait_ge(sem("ms_ready"), j + 1)
                act.activation(small[:, 40:44], small[:, 36:40], ACT.Sqrt).then_inc(sem("rstd_ready"), 1)
                if j < 3:
                    for c in range(DENSE_SPLIT):
                        high_dense(phase_splits(NORM_PHASE[j])[0] + c)
                    act.wait_ge(sem("hT_ready"), 8 * (j + 1))
                    for k in range(KT):
                        act.activation(h_high[:, k, :], hT[:, k, :], ACT.Copy).then_inc(sem("h_high_ready"), 1)

            def high_odd(k):
                act.activation(y_high_odd[k][:, :], yT[:, k, :], ACT.Copy).then_inc(sem("part_high"), 1)

            def out_proj(phase, full0):
                for c in range(4 - DENSE_SPLIT):
                    next_high(phase, c)

            def attention(first, done):
                def outputs(pair):
                    act.wait_ge(sem("pv_done"), 2 * done + 2 * (pair + 1))
                    act.activation(yT[:, done + pair, :], acc[pair % 2][:, :], ACT.Copy).then_inc(sem("yT_ready"), 1)
                    if done:
                        act.wait_ge(sem("yT_ready"), done + pair + 1)
                        high_odd(done + pair)

                for i in range(HEADS * NT + 2):
                    if i >= 11 and (i - 11) % 8 == 0:
                        outputs((i - 11) // 8)
                    if i < HEADS * NT:
                        n = P * (i % NT + 1)
                        act.wait_ge(sem("max_ready"), first + i + 1)
                        if first or i >= 3:
                            act.wait_ge(sem("probsT_full"), first + i - 2)
                        b = bank["probs_ready", first + i + 1]
                        act.activation(probs[:, i % 3, 0:n], b[:, 0:n], ACT.Exp, bias=small[:, 48 + i % 4:49 + i % 4],
                                       accum_out=small[:, 52 + i % 4:53 + i % 4]).then_inc(sem("probs_ready"), 1)
                    u = i - 2
                    if u >= 0:
                        h, t = divmod(u, NT)
                        act.wait_ge(sem("probsT_full"), first + u + 1)
                        if t == 0 and h >= 2:
                            act.wait_ge(sem("pv_done"), 2 * done + h - 1)
                        act.activation(probsT[h % 2][:, 0:t + 1, P * t:P * (t + 1)],
                                       bank["probsT_ready", first + u + 1][:, 0:P * (t + 1)].rearrange("p (a b) -> p a b", b=P),
                                       ACT.Copy).then_inc(sem("probsT_ready"), 1)
                outputs(3)

            norm(0)
            for c in range(8):
                act.wait_ge(sem("qk_full"), c + 1)
                act.activation((qT if c < 4 else kT)[:, c % 4, :], bank["qk_stored", c + 1][:, :], ACT.Copy,
                               scale=HD ** -0.5 if c < 4 else 1.0).then_inc(sem("qk_stored"), 1)
                if c % 2:
                    next_high(E_IN, c // 2)
            act.wait_ge(sem("w_dt_loaded"), 16 * KT)
            act.activation(w_dt_high[:, :, :], w_dt[:, :, :], ACT.Copy).then_inc(sem("part_high"), 1)
            for c in (4, 5):
                next_high(E_IN, c)
            for i in range(8):
                act.wait_ge(sem("z_full"), i + 1)
                act.activation(zs[:, i % 4, 256 * (i // 4):256 * (i // 4) + 256], bank["z_stored", i + 1][:, 0:256], ACT.Silu)\
                    .then_inc(sem("z_stored"), 1)
                if i % 4 == 3:
                    next_high(E_IN, 6 + i // 4)
            act.wait_ge(sem("const_ready"), 1)

            def conv_silu(c):
                act.wait_ge(sem("conv_sum"), c + 1)
                act.activation(conv_out[:, c, :], conv_out[:, c, :], ACT.Silu).then_inc(sem("conv_ready"), 1)

            for c in range(CONV_TILES):
                act.wait_ge(sem("conv_full"), c + 1)
                act.activation(conv_in[:, c, B_CONV - 1:], bank["conv_stored", c + 1][:, :], ACT.Copy).then_inc(sem("conv_stored"), 1)
                if c % 2:
                    next_high(E_IN, 8 + c // 2)
                if c >= 3:
                    conv_silu(c - 3)
            for c in range(CONV_TILES - 3, CONV_TILES):
                conv_silu(c)
            act.wait_ge(sem("small_loaded"), 64)
            act.wait_ge(sem("dt_full"), 1)
            act.activation(dt_row[0], bank["u_ready", 1][0:HEADS, :], ACT.Identity, bias=small[0:HEADS, 0:1]).then_inc(sem("u_ready"), 1)
            act.activation(small[0:HEADS, 2:3], small[0:HEADS, 1:2], ACT.Exp)
            act.wait_ge(sem("abs_ready"), 1)
            step(act.activation(dt_row[1], dt_row[1], ACT.Exp, scale=-1.0))
            act.activation(dt_row[1], dt_row[1], ACT.Ln, bias=1.0).then_inc(sem("ln_ready"), 1)
            if upto >= 2:
                attention(0, 0)
                for c in range(DENSE_SPLIT):
                    high_dense(phase_splits(E_OUT)[0] + c)
                act.wait_ge(sem("yT_ready"), 4)
                for k in range(4):
                    act.activation(y_high_even[:, k, :], yT[:, k, :], ACT.Copy).then_inc(sem("part_high"), 1)
                act.wait_ge(sem("dt_col_ready"), 1)
                for h in range(HEADS):
                    plain, masked = bank["decay_ready", 7 * h + 5], bank["decay_ready", 7 * h + 7]
                    if h >= 2:
                        act.wait_ge(sem("w_ready"), NT * (h - 1))
                    act.wait_ge(sem("row_full"), 2 * h + 2)
                    for j in range(NT):
                        bias = small[:, 64 + HEADS * j + h:65 + HEADS * j + h]
                        if j < NT - 1:
                            act.activation(decay[h % 2][:, j, P * (j + 1):], plain[:, P * (j + 1):], ACT.Exp, bias=bias)\
                                .then_inc(sem("decay_ready"), 1)
                        act.activation(decay[h % 2][:, j, P * j:P * (j + 1)], masked[:, P * j:P * (j + 1)], ACT.Exp, bias=bias)\
                            .then_inc(sem("decay_ready"), 1)
                act.wait_ge(sem("ssd_ms_ready"), 1)
                act.activation(small[:, 144:152], small[:, 136:144], ACT.Sqrt).then_inc(sem("ssd_rstd"), 1)
                for t in range(NT):
                    now = slice(P * t, P * (t + 1))
                    act.wait_ge(sem("yT_b_ready"), t + 1)
                    act.activation(y_high_even[:, 4:8, now], yT[:, 4:8, now], ACT.Copy).then_inc(sem("part_high"), 1)
                out_proj(E_OUT, 0)

            if upto >= 3:
                norm(1)
                for f in range(FF_TILES):
                    act.wait_ge(sem("gate_full"), f + 1)
                    if f >= 2:
                        act.wait_ge(sem("hid_ready"), f - 1)
                    act.activation(sil[:, f % 2, :], bank["sil_ready", f + 1][:, :], ACT.Silu).then_inc(sem("sil_ready"), 1)
                    if f % 2:
                        next_high(FFN, f - 1)
                        next_high(FFN, f)
                        for g in (f - 3, f - 2):
                            if 0 <= g < 12:
                                act.wait_ge(sem("hid_ready"), g + 1)
                                act.activation(ff_high[g][:, :], hid[:, g, :], ACT.Copy).then_inc(sem("part_high"), 1)
                act.wait_ge(sem("up_full"), FF_TILES)
                act.wait_ge(sem("hid_ready"), FF_TILES)
                for g in range(12, FF_TILES):
                    act.activation(ff_high[g][:, :], hid[:, g, :], ACT.Copy).then_inc(sem("part_high"), 1)
                for c in range(12):
                    next_high(FFN, FF_TILES + c)

            if upto >= 4:
                norm(2)
                for c in range(C_TILES):
                    act.wait_ge(sem("pc_full"), total("pc_full", c + 1))
                    act.activation(pcT[:, c, 1:], bank["pc_stored", c + 1][:, :], ACT.Copy).then_inc(sem("pc_stored"), 1)
                    if c % 2:
                        next_high(O_IN, c // 2)
                next_high(O_IN, 7)
                act.wait_ge(sem("mixed"), 13)
                act.activation(pcT[0:64, 12, 1:], pcT[0:64, 12, 1:], ACT.Tanh).then_inc(sem("lora_in_ready"), 1)
                act.wait_ge(sem("mixed"), 14)
                act.activation(pcT[:, 13, 1:], pcT[:, 13, 1:], ACT.Sigmoid).then_inc(sem("lora_in_ready"), 1)
                def prepare(t, piece):
                    if piece == 1:
                        for i, name in enumerate(("sig", "a")):
                            act.wait_ge(sem("wa_sum"), total("wa_sum", 2 * t + i + 1))
                            act.activation(R[name], R[name], ACT.Sigmoid).then_inc(sem("sig_ready"), 1)
                        act.wait_ge(sem("lora_full"), total("lora_full", 3 * t + 3))
                        act.activation(R[f"g{t % 2}"], bank["g_ready", t + 1][:, :], ACT.Copy).then_inc(sem("g_ready"), 1)
                        act.wait_ge(sem("kk_ss"), t + 1)
                        act.activation(small[:, 176:184], small[:, 176:184], ACT.Sqrt).then_inc(sem("kk_norm"), 1)
                    if piece == 2:
                        for i, (name, row, sign) in enumerate((("Eex", 0, 1.0), ("Ein", 1, 1.0), ("Eni", 1, -1.0), ("Erev", 2, 1.0))):
                            act.wait_ge(sem("cum_full"), total("cum_full", 3 * t + row + 1))
                            act.activation(R[name], bank["exp_ready", 4 * t + (1, 3, 4)[row]][:, :], ACT.Exp, scale=sign).then_inc(sem("exp_ready"), 1)
                        act.wait_ge(sem("end_full"), total("end_full", t + 1))
                        act.activation(small[:, 224 + 8 * (t % 2):232 + 8 * (t % 2)], bank["end_ready", t + 1][:, 0:8], ACT.Exp)\
                            .then_inc(sem("end_ready"), 1)

                def outputs_by_feature(t):
                    act.wait_ge(sem("ycT_full"), total("ycT_full", t + 1))
                    act.activation(yT[:, 0:4, P * t:P * (t + 1)], bank["ycT_ready", t + 1][:, :].rearrange("p (a b) -> p a b", b=P), ACT.Copy)\
                        .then_inc(sem("ycT_ready"), 1)

                for piece in range(3):
                    prepare(0, piece)
                for t in range(NT):
                    for i in range(4):
                        act.wait_ge(sem("ft_full"), total("ft_full", 4 * t + i + 1))
                        b = bank["ft_ready", 4 * t + i + 1]
                        if i in (0, 1):
                            o = F["ar"][:, :, :, CHUNK * i:CHUNK * (i + 1)]
                            v = b[:, :].rearrange("p (a b c) -> p a b c", b=2, c=CHUNK)
                        else:
                            o, v = F["btT" if i == 2 else "ktT"], b[:, :].rearrange("p (a b) -> p a b", b=P)
                        act.activation(o, v, ACT.Copy).then_inc(sem("ft_ready"), 1)
                    if t >= 1:
                        outputs_by_feature(t - 1)
                    for n in range(5):
                        for half in range(2):
                            cols = slice(256 * half, 256 * half + 256)
                            act.wait_ge(sem("y1_full"), 10 * t + 2 * n + half + 1)
                            act.activation(R["Y1"][:, cols], acc[half][:, cols], ACT.Copy).then_inc(sem("y1_ready"), 1)
                        if t + 1 < NT and n < 3:
                            prepare(t + 1, n)
                        if n == 3:
                            act.wait_ge(sem("qkvr_stored"), total("qkvr_stored", 12))
                            step(act.activation(R["mla"][:, 0:Q_RANK], qkvr[:, t, 0:Q_RANK], ACT.Square, accum_out=small[:, 152 + t:153 + t]))
                            step(act.activation(R["mla"][:, 0:KV_RANK], qkvr[:, t, Q_RANK:Q_RANK + KV_RANK], ACT.Square,
                                                accum_out=small[:, 156 + t:157 + t]))
                    if t == NT - 1:
                        act.activation(small[:, 160:168], small[:, 152:160], ACT.Copy).then_inc(sem("mla_ss"), 1)
                        act.wait_ge(sem("mla_ms"), 1)
                        act.activation(small[:, 168:176], small[:, 160:168], ACT.Sqrt).then_inc(sem("mla_rstd"), 1)
                    for i, o in enumerate((R["Z1"], R["U"], F["wt"][:, :, 0:CHUNK], F["wt"][:, :, CHUNK:])):
                        act.wait_ge(sem("zu_full"), 4 * t + i + 1)
                        b = bank["z_ready", 4 * t + i + 1]
                        v = b[:, 0:256].rearrange("p (a b) -> p a b", b=CHUNK) if i >= 2 else b[:, :]
                        act.activation(o, v, ACT.Copy).then_inc(sem("z_ready"), 1)
                    for c in range(2):
                        n = 2 * t + c
                        rows = slice(CHUNK * c, CHUNK * (c + 1))
                        act.wait_ge(sem("sa_ready"), 2 * n + 2)
                        for par in range(2):
                            act.activation(R["y"][rows, :].rearrange("p (a b n) -> p a b n", b=2, n=HD)[:, :, par, :],
                                           bank["y_stored", 2 * n + par + 1][rows, 256:].rearrange("p (a n) -> p a n", n=HD), ACT.Copy)\
                                .then_inc(sem("y_stored"), 1)
                    act.wait_ge(sem("gn_ms"), t + 1)
                    act.activation(small[:, 216:224], small[:, 216:224], ACT.Sqrt).then_inc(sem("gn_rstd"), 1)
                outputs_by_feature(NT - 1)

            if upto >= 5:
                act.wait_ge(sem("angle_ready"), 1)
                for i in range(2):
                    act.activation(rope_cs[:, 4 * i:4 * i + 4, :], rope_cs[:, 4 * i:4 * i + 4, :], ACT.Sin).then_inc(sem("sin_ready"), 1)
                for i in range(8):
                    half, t = divmod(i, NT)
                    act.wait_ge(sem("uq_full"), total("uq_full", i + 1))
                    act.activation(q_tok[:, t, 4 * half:4 * half + 4, :], bank["q_stored", i + 1][:, 0:384].rearrange("p (h n) -> p h n", n=QD),
                                   ACT.Copy, scale=MLA_SCALE).then_inc(sem("q_stored"), 1)
                for h in range(HEADS):
                    act.wait_ge(sem("ukv_full"), total("ukv_full", h + 1))
                    act.activation(kT_d[0:HD, h, :], bank["kn_stored", h + 1][0:HD, :], ACT.Copy).then_inc(sem("kn_stored"), 1)
                for h in range(HEADS):
                    act.wait_ge(sem("qT_full"), h + 1)
                    act.activation(qT_d[:, h, :], bank["qT_ready", h + 1][0:QD, :], ACT.Copy).then_inc(sem("qT_ready"), 1)
                act.wait_ge(sem("ycT_ready"), total("ycT_ready", NT))
                for k in range(4):
                    high_odd(k)
                for c in range(DENSE_SPLIT):
                    high_dense(phase_splits(O_OUT)[0] + c)
                attention(HEADS * NT, 4)
                out_proj(O_OUT, 16)

            if upto >= 6:
                norm(3)
                act.wait_ge(sem("top_ready"), 1)
                act.activation(ex, ex, ACT.Exp).then_inc(sem("ex_ready"), 1)
                act.wait_ge(sem("turns_ready"), 1)
                ends = [act.value_load(turn_ends_i[0:1, i:i + 1], min_val=i + 1, max_val=MAX_TURNS) for i in range(len(CAPS))]

                def high(turn, ring, n):
                        raw, here = ring.take()
                        act.wait_ge(*here)
                        if ring.turn is not None:
                            name, count = expert_tile_used(n - SPLIT)
                            act.wait_ge(sem(name), turn * GROUPS_E + count)
                        act.activation(w_high[n % SPLIT][:, :], raw[:, :], ACT.Copy).then_inc(sem("w_high_ready"), 1)

                def xg_parts(turn, ahead):
                        for i in range(3):
                            cols = slice(3 * i, min(3 * i + 3, KT))
                            act.wait_ge(sem("xg_ready"), turn * 3 + (3 * ahead + i + 1))
                            act.activation(xg_high[:, cols, :], xgT[:, cols, 0:P], ACT.Copy).then_inc(sem("xg_high_ready"), 1)

                def gates_turned(turn, cap):
                        act.wait_ge(sem("pickT_full"), turn * 2 + (1 if cap > P else 2))
                        act.activation(pickT[:, 0, :], turn_banks[0][:, :], ACT.Copy).then_inc(sem("pickT_ready"), 1 if cap > P else 2)
                        if cap > P:
                            act.wait_ge(sem("pickT_full"), turn * 2 + 2)
                            act.activation(pickT[0:cap - P, 1, :], acc[3][0:cap - P, :], ACT.Copy).then_inc(sem("pickT_ready"), 1)

                def expert_split(turn):
                        ring = expert_ring(raw_slots, landed, turn)
                        ring.n = SPLIT
                        for n, (kind, j) in enumerate(expert_order()):
                            if kind == "g":
                                act.wait_ge(sem("gate_full"), turn * GROUPS_E + (FF_TILES + j + 1))
                                act.wait_ge(sem("hid_ready"), turn * GROUPS_E + (FF_TILES + j - 1))
                                act.activation(sil_e[:, j % 2, 0:256], turn_banks[2 * j % 4][:, 0:256], ACT.Silu)\
                                    .then_inc(sem("sil_ready"), 1)
                            turned = j - 1 if kind == "g" else j if j == GROUPS_E - 1 and kind == "d" else -1
                            if turned >= 0:
                                act.wait_ge(sem("hidT_full"), turn * GROUPS_E + (turned + 1))
                                if turned >= 2:
                                    act.wait_ge(sem("down_used"), turn * GROUPS_E + (10 + turned - 1))
                                act.activation(hid_high[:, turned % 2, :, :], acc[2 + turned % 2][:, 0:2 * P].rearrange("p (a b) -> p a b", b=P),
                                               ACT.Copy).then_inc(sem("hid_high_ready"), 1)
                            if n < TILES_E - 1:
                                high(turn, ring, n + SPLIT)
                        act.wait_ge(sem("down_used"), turn * GROUPS_E + (10 + GROUPS_E))
                        act.activation(out_tok[:, 0, 0:512], acc[0][:, :], ACT.Copy).then_inc(sem("outT_ready"), 3)
                        act.activation(out_tok[:, 0, 512:], acc[1][:, :], ACT.Copy).then_inc(sem("out_tok_ready"), 4)
                        gates_turned(turn, P)
                        high(turn, ring, TILES_E - 1 + SPLIT)
                        xg_parts(turn, 1)

                def expert(turn, cap):
                        for j in range(GROUPS_E):
                            act.wait_ge(sem("gate_full"), turn * GROUPS_E + (FF_TILES + j + 1))
                            act.wait_ge(sem("hid_ready"), turn * GROUPS_E + (FF_TILES + j - 1))
                            act.activation(pair_of(sil_e[:, j % 2, :], cap), pair_of(turn_banks[2 * j % 4][:, 0:2 * CAP], cap), ACT.Silu)\
                                .then_inc(sem("sil_ready"), 1)
                        act.wait_ge(sem("down_used"), turn * GROUPS_E + (10 + GROUPS_E))
                        for i in range(3):
                            n = min(3, KT - 3 * i)
                            act.activation(outT[:, 3 * i:3 * i + n, 0:cap], acc[i][:, 0:CAP * n].rearrange("p (a b) -> p a b", b=CAP)[:, :, 0:cap], ACT.Copy)\
                                .then_inc(sem("outT_ready"), 1)
                        gates_turned(turn, cap)
                        for i in range(4):
                            act.wait_ge(sem("out_tok_full"), turn * 4 + (i + 1))
                            rows = P if i < 2 else cap - P
                            act.activation(out_tok[0:rows, i // 2, 512 * (i % 2):512 * (i % 2) + 512],
                                           turn_banks[i][0:rows, :], ACT.Copy).then_inc(sem("out_tok_ready"), 1)

                ring = expert_ring(raw_slots, landed, None)
                for n in range(SPLIT):
                    high(0, ring, n)
                xg_parts(0, 0)
                with act.Fori(0, ends[0]) as turn:
                    expert_split(turn)
                with act.Fori(ends[0], ends[1]) as turn:
                    expert(turn, CAPS[1])
                with act.Fori(ends[1], ends[2]) as turn:
                    expert(turn, CAPS[2])
                act.wait_ge(sem("moe_done"), 1)
                norm(4)

        @block.vector
        def _(dve):
            step = Steps(dve, sem("dve_step"))

            def tt(o, a, b, op):
                return dve.tensor_tensor(o, a, b, op)

            def inv_mean(o, i, n, eps):
                step(dve.tensor_scalar(o, i, n, eps, ALU.mult, ALU.add))
                return dve.reciprocal(o, o)

            def low_dense(s):
                n = [n for phase in split_tiles() for n in phase][s]
                dve.wait_ge(sem("dense_high_ready"), s + 1)
                tt(w_low[s % DENSE_SPLIT][:, :], slots[n % DENSE_RAW][:, :], w_high[s % DENSE_SPLIT][:, :].bitcast(F32), ALU.subtract)\
                    .then_inc(sem("dense_low_ready"), 1)

            def next_low(phase, c):
                first, last = phase_splits(phase)
                if first + c + DENSE_SPLIT <= last:
                    low_dense(first + c + DENSE_SPLIT)

            def norm(j):
                dve.wait_ge(sem("ss_ready"), j + 1)
                step(tt(small[:, 32:36], small[:, 32:36], small[:, 248:252], ALU.add))
                inv_mean(small[:, 36:40], small[:, 32:36], 1.0 / D, RMS_EPS).then_inc(sem("ms_ready"), 1)
                dve.wait_ge(sem("rstd_ready"), j + 1)
                if j == 4:
                    return
                for t in range(NT):
                    dve.tensor_scalar(xn[:, t, :], xs[:, t, :], small[:, 40 + t:41 + t], None, ALU.mult).then_inc(sem("xn_ready"), 1)
                if j < 3:
                    low_dense(phase_splits(NORM_PHASE[j])[0])
                for t in range(NT):
                    for half in range(2):
                        dve.wait_ge(sem("xnT_full"), 8 * j + 2 * t + half + 1)
                        b = bank["hT_ready", 8 * j + 2 * t + half + 1][:, :].rearrange("p (a b) -> p a b", b=P)
                        wv = vc[:, 8 * j + 4 * half:8 * j + 4 * half + 4].unsqueeze(2).to_broadcast([P, 4, P])
                        tt(hT[:, 4 * half:4 * half + 4, P * t:P * (t + 1)], b, wv, ALU.mult).then_inc(sem("hT_ready"), 1)
                if j < 3:
                    for k in range(KT):
                        dve.wait_ge(sem("h_high_ready"), KT * j + k + 1)
                        tt(h_low[:, k, :], hT[:, k, :], h_high[:, k, :].bitcast(F32), ALU.subtract).then_inc(sem("h_low_ready"), 1)
                    low_dense(phase_splits(NORM_PHASE[j])[0] + 1)

            def attention(first, done):
                for i in range(HEADS * NT + 2):
                    if done and i >= 14 and (i - 14) % 8 == 0:
                        low_odd(done + (i - 14) // 8)
                    if i < HEADS * NT:
                        n = P * (i % NT + 1)
                        dve.wait_ge(sem("scores_full"), first + i + 1)
                        dve.tensor_reduce(small[:, 48 + i % 4:49 + i % 4], bank["probs_ready", first + i + 1][:, 0:n], AX, ALU.max,
                                          negate=True).then_inc(sem("max_ready"), 1)
                    u = i - 1
                    if 0 <= u < HEADS * NT:
                        n = P * (u % NT + 1)
                        dve.wait_ge(sem("probs_ready"), first + u + 1)
                        step(dve.reciprocal(small[:, 56 + u % 4:57 + u % 4], small[:, 52 + u % 4:53 + u % 4]))
                        dve.tensor_scalar(probs[:, u % 3, 0:n], probs[:, u % 3, 0:n], small[:, 56 + u % 4:57 + u % 4], None, ALU.mult).then_inc(sem("probs_scaled"), 1)

            def add_x(full, count, t, cols, b):
                dve.wait_ge(sem(full), count)
                tt(xs[:, t, cols], xs[:, t, cols], b, ALU.add).then_inc(sem("x_added"), 1)

            def low_odd(k):
                dve.wait_ge(sem("part_high"), ODD_PARTS + k + 1)
                tt(y_low[:, k, :], yT[:, k, :], y_high_odd[k][:, :].bitcast(F32), ALU.subtract).then_inc(sem("part_low"), 1)

            def low_ff(g):
                dve.wait_ge(sem("part_high"), FF_PARTS + g + 1)
                tt(ff_low[:, g, :], hid[:, g, :], ff_high[g][:, :].bitcast(F32), ALU.subtract).then_inc(sem("part_low"), 1)

            def out_proj(phase, base, full0):
                for c in range(4):
                    if c >= 1:
                        next_low(phase, c - 1)
                    for t in range(NT):
                        n = 4 * c + t
                        add_x("mix_full", full0 + n + 1, t, slice(256 * c, 256 * c + 256), bank["x_added", base + n + 1][:, 0:256])

            dve.wait_ge(sem("vec_full"), 1)
            dve.tensor_copy(vc[:, :], bank["vc_ready", 1][:, 0:95]).then_inc(sem("vc_ready"), 1)
            dve.wait_ge(sem("vc_ready"), 1)
            norm(0)
            for c in range(4):
                next_low(E_IN, c)
            dve.wait_ge(sem("part_high"), 1)
            tt(w_dt_low[:, :, :], w_dt[:, :, :], w_dt_high[:, :, :].bitcast(F32), ALU.subtract).then_inc(sem("part_low"), 1)
            for i in range(8):
                dve.wait_ge(sem("v_full"), i + 1)
                dve.tensor_copy(v_a[:, i % 4, 256 * (i // 4):256 * (i // 4) + 256], bank["v_stored", i + 1][:, 0:256]).then_inc(sem("v_stored"), 1)
                if i % 4 == 3:
                    next_low(E_IN, 4 + i // 4)
            dve.wait_ge(sem("const_ready"), 1)
            dve.wait_ge(sem("small_loaded"), 64)
            for c in (6, 7, 8):
                next_low(E_IN, c)
            for c in range(CONV_TILES):
                if c == 2:
                    next_low(E_IN, 9)
                dve.wait_ge(sem("conv_stored"), c + 1)
                tap = lambda k: vc[:, 40 + 8 * k + c:41 + 8 * k + c]
                step(dve.tensor_scalar(conv_out[:, c, :], conv_in[:, c, 0:SEQ], tap(0), vc[:, 32 + c:33 + c], ALU.mult, ALU.add))
                for k in range(1, B_CONV):
                    i = dve.scalar_tensor_tensor(out=conv_out[:, c, :], in0=conv_in[:, c, k:k + SEQ], scalar=tap(k),
                                                 in1=conv_out[:, c, :], op0=ALU.mult, op1=ALU.add)
                    if k < B_CONV - 1:
                        step(i)
                i.then_inc(sem("conv_sum"), 1)
            dve.wait_ge(sem("u_ready"), 1)
            dve.scalar_tensor_tensor(out=dt_row[1], in0=dt_row[0], scalar=-1.0, in1=dt_row[0], op0=ALU.mult, op1=ALU.max).then_inc(sem("abs_ready"), 1)
            dve.wait_ge(sem("ln_ready"), 1)
            step(dve.scalar_tensor_tensor(out=dt_keep, in0=dt_row[0], scalar=0.0, in1=dt_row[1], op0=ALU.max, op1=ALU.add))
            if upto >= 2:
                attention(0, 0)
                step(dve.memset(ones_row, 1.0))
                dve.wait_ge(sem("pv_done"), HEADS)
                step(dve.tensor_copy(dt_row[0], dt_keep))
                step(dve.tensor_scalar(dt_row[2], dt_row[0], small[0:HEADS, 2:3], -1.0, ALU.mult, ALU.mult))
                step(dve.tensor_tensor_scan(dt_row[1], ones_row, dt_row[2], 0.0, ALU.mult, ALU.add))
                dve.tensor_scalar(dt_row[2], dt_row[1], -1.0, None, ALU.mult).then_inc(sem("cum_ready"), 1)
                for t in range(NT):
                    dve.wait_ge(sem("x_tok_full"), t + 1)
                    dve.tensor_copy(x_tok[:, t, :], bank["x_tok_ready", t + 1][:, :]).then_inc(sem("x_tok_ready"), 1)
                for i in range(8):
                    g, j = divmod(i, NT)
                    dve.wait_ge(sem("cb_full"), i + 1)
                    dve.tensor_copy(cbT[:, g, j, P * j:], bank["cb_ready", i + 1][:, P * j:]).then_inc(sem("cb_ready"), 1)
                dve.wait_ge(sem("dt_col_full"), 1)
                step(dve.tensor_copy(small[:, 64:128], bank["dt_col_ready", 1][:, 0:64]))
                dve.tensor_copy(small[:, 3:4], small[:, 64:65]).then_inc(sem("dt_col_ready"), 1)
                dtc = small[:, 96:128].rearrange("p (t h) -> p t h", h=HEADS).unsqueeze(3).to_broadcast([P, NT, HEADS, HD])
                step(tt(xdt.rearrange("p t (h n) -> p t h n", n=HD), x_tok.rearrange("p t (h n) -> p t h n", n=HD), dtc, ALU.mult))
                def gate_squares(g):
                    cols = slice(256 * g, 256 * g + 256)
                    dve.wait_ge(sem("y_tok_ready"), HEADS // B_GROUPS * (g + 1))
                    dve.wait_ge(sem("z_stored"), 8)
                    step(tt(y_tok[:, :, cols], y_tok[:, :, cols], zs[:, :, cols], ALU.mult))
                    step(tt(y_squares, y_tok[:, :, cols], y_tok[:, :, cols], ALU.mult))
                    step(dve.tensor_reduce(small[:, 128:136].rearrange("p (t g) -> p t g", g=2)[:, :, g], y_squares, AX, ALU.add))

                for h in range(HEADS + 1):
                    if h == 7:
                        gate_squares(0)
                    if h in (5, 6):
                        low_dense(phase_splits(E_OUT)[0] + h - 5)
                    if 1 <= h < 5:
                        k = h - 1
                        dve.wait_ge(sem("part_high"), EVEN_PARTS + k + 1)
                        tt(y_low[:, k, :], yT[:, k, :], y_high_even[:, k, :].bitcast(F32), ALU.subtract).then_inc(sem("part_low"), 1)
                    if h < HEADS:
                        if h >= 2:
                            dve.wait_ge(sem("ssd_full"), h - 1)
                        for j in range(NT):
                            dve.wait_ge(sem("decay_ready"), 7 * h + min(2 * j + 2, 7))
                            tt(wT[h % 2][:, j, P * j:], decay[h % 2][:, j, P * j:], cbT[:, h // 4, j, P * j:], ALU.mult).then_inc(sem("w_ready"), 1)
                    if h >= 1:
                        g = h - 1
                        dve.wait_ge(sem("ssd_full"), g + 1)
                        cols = slice(HD * g, HD * (g + 1))
                        dve.scalar_tensor_tensor(out=y_tok[:, :, cols], in0=x_tok[:, :, cols], scalar=small[:, 8 + g:9 + g],
                                                     in1=bank["y_tok_ready", g + 1][:, 0:256].rearrange("p (a b) -> p a b", b=HD),
                                                     op0=ALU.mult, op1=ALU.add).then_inc(sem("y_tok_ready"), 1)
                gate_squares(1)
                inv_mean(small[:, 136:144], small[:, 128:136], 1.0 / 256, B_NORM_EPS).then_inc(sem("ssd_ms_ready"), 1)
                dve.wait_ge(sem("ssd_rstd"), 1)
                rs = small[:, 144:152].unsqueeze(2).to_broadcast([P, 8, 256])
                for t in range(NT):
                    yv = y_tok[:, t, :].rearrange("p (g n) -> p g n", n=256)
                    tt(yv, yv, rs[:, 2 * t:2 * t + 2, :], ALU.mult).then_inc(sem("yn_ready"), 1)
                for t in range(NT):
                    dve.wait_ge(sem("ynT_full"), t + 1)
                    tt(yT[:, 4:8, P * t:P * (t + 1)], bank["yT_b_ready", t + 1][:, :].rearrange("p (a b) -> p a b", b=P),
                           vc[:, 91:95].unsqueeze(2).to_broadcast([P, 4, P]), ALU.mult).then_inc(sem("yT_b_ready"), 1)
                for t in range(NT):
                    now = slice(P * t, P * (t + 1))
                    dve.wait_ge(sem("part_high"), EVEN_PARTS + 4 + t + 1)
                    tt(y_low[:, 4:8, now], yT[:, 4:8, now], y_high_even[:, 4:8, now].bitcast(F32), ALU.subtract).then_inc(sem("part_low"), 1)
                out_proj(E_OUT, 0, 0)

            if upto >= 3:
                norm(1)
                for f in range(FF_TILES):
                    if f % 2 == 0:
                        next_low(FFN, f)
                    dve.wait_ge(sem("up_full"), f + 1)
                    dve.wait_ge(sem("sil_ready"), f + 1)
                    tt(hid[:, f, :], sil[:, f % 2, :], bank["hid_ready", f + 1][:, :], ALU.mult).then_inc(sem("hid_ready"), 1)
                    if f % 2:
                        next_low(FFN, f)
                        for g in (f - 3, f - 2):
                            if 0 <= g < 12:
                                low_ff(g)
                for g in range(12, FF_TILES):
                    low_ff(g)
                for half in range(2):
                    for c in range(5):
                        next_low(FFN, FF_TILES + 6 * half + c)
                    for t in range(NT):
                        add_x("down_full", 4 * half + t + 1, t, slice(512 * half, 512 * half + 512), acc[t][:, :])
                    next_low(FFN, FF_TILES + 6 * half + 5)

            if upto >= 4:
                norm(2)
                step(dve.memset(pcT[:, :, 0:1], 0.0))
                for j in range(C_TILES):
                    dve.wait_ge(sem("pc_stored"), total("pc_stored", j + 1))
                    step(tt(mixdiff[:, j % 2, :], pcT[:, j, 0:SEQ], pcT[:, j, 1:], ALU.subtract))
                    dve.scalar_tensor_tensor(out=pcT[:, j, 1:], in0=mixdiff[:, j % 2, :], scalar=vc[:, 72 + j:73 + j],
                                                 in1=pcT[:, j, 1:], op0=ALU.mult, op1=ALU.add).then_inc(sem("mixed"), 1)
                    if j % 2:
                        next_low(O_IN, j // 2)
                next_low(O_IN, 7)
                for i in range(12):
                    c, t = divmod(i, NT)
                    n = 256 if c < 2 else QKVR - 512
                    dve.wait_ge(sem("qkvr_full"), total("qkvr_full", i + 1))
                    dve.tensor_copy(qkvr[:, t, 256 * c:256 * c + n], bank["qkvr_stored", i + 1][:, 0:n]).then_inc(sem("qkvr_stored"), 1)
                dve.wait_ge(sem("bc_loaded"), 16 * 7)
                by_head = lambda v: v.rearrange("p (h n) -> p h n", n=HD)
                spread = lambda v: v.unsqueeze(2).to_broadcast([P, HEADS, HD])
                dve.wait_ge(sem("mixed"), C_TILES)
                dve.memset(state[0], 0.0).then_inc(sem("state_ready"), 1)
                def rope_angles():
                    for i in range(16):
                        step(dve.memset(small[:, 16 + i:17 + i], ROPE_THETA ** (-i / 16)))
                    step(dve.tensor_copy(small[:, 252:256], small_i[:, 0:NT]))
                    ang, turns = rope_cs[:, 0:4, :], rope_cs[:, 4:8, :]
                    step(dve.tensor_copy(ang, small[:, 16:32].unsqueeze(1).to_broadcast([P, NT, 16])))
                    step(tt(ang, ang, small[:, 252:256].unsqueeze(2).to_broadcast([P, NT, 16]), ALU.mult))
                    step(dve.tensor_scalar(turns, ang, 1.0 / (2 * math.pi), MAGIC, ALU.mult, ALU.add))
                    step(dve.tensor_scalar(turns, turns, -MAGIC, None, ALU.add))
                    for part in TWO_PI:
                        step(dve.scalar_tensor_tensor(out=ang, in0=turns, scalar=-part, in1=ang, op0=ALU.mult, op1=ALU.add))
                    step(dve.tensor_scalar(ang, ang, 3.1415925, -3.1415925, ALU.min, ALU.max))
                    step(dve.scalar_tensor_tensor(out=turns, in0=ang, scalar=-1.0, in1=ang, op0=ALU.mult, op1=ALU.max))
                    dve.tensor_scalar(turns, turns, -1.0, math.pi / 2, ALU.mult, ALU.add).then_inc(sem("angle_ready"), 1)

                def latent_norms():
                    dve.wait_ge(sem("mla_ss"), 1)
                    step(dve.tensor_scalar(small[:, 160:164], small[:, 160:164], 1.0 / Q_RANK, RMS_EPS, ALU.mult, ALU.add))
                    step(dve.tensor_scalar(small[:, 164:168], small[:, 164:168], 1.0 / KV_RANK, RMS_EPS, ALU.mult, ALU.add))
                    dve.reciprocal(small[:, 160:168], small[:, 160:168]).then_inc(sem("mla_ms"), 1)
                    dve.wait_ge(sem("mla_rstd"), 1)
                    for t in range(NT):
                        step(dve.tensor_scalar(qkvr[:, t, 0:Q_RANK], qkvr[:, t, 0:Q_RANK], small[:, 168 + t:169 + t], None, ALU.mult))
                        kv = qkvr[:, t, Q_RANK:Q_RANK + KV_RANK]
                        dve.tensor_scalar(kv, kv, small[:, 172 + t:173 + t], None, ALU.mult).then_inc(sem("qkvn_ready"), 1)

                def prepare(t, piece):
                    if piece == 0:
                        for a, name in enumerate(("r", "k", f"v{t % 2}")):
                            dve.wait_ge(sem("rkv_full"), total("rkv_full", 3 * t + a + 1))
                            dve.tensor_copy(R[name], bank["rkv_ready", 3 * t + a + 1][:, :]).then_inc(sem("rkv_ready"), 1)
                    if piece == 1:
                        for i, (name, bias) in enumerate((("sig", "w0"), ("a", "a0"))):
                            dve.wait_ge(sem("lora_full"), total("lora_full", 3 * t + i + 1))
                            tt(R[name], bank["wa_sum", 2 * t + i + 1][:, :], bc[bias], ALU.add).then_inc(sem("wa_sum"), 1)
                        dve.wait_ge(sem("rkv_ready"), total("rkv_ready", 3 * t + 3))
                        step(tt(R["kk"], R["k"], bc["k_k"], ALU.mult))
                        step(tt(R["tmp"], R["kk"], R["kk"], ALU.mult))
                        dve.tensor_reduce(small[:, 176:184], by_head(R["tmp"]), AX, ALU.add).then_inc(sem("kk_ss"), 1)
                        dve.wait_ge(sem("kk_ss"), t + 1)
                        dve.wait_ge(sem("sig_ready"), 2 * t + 2)
                        step(dve.scalar_tensor_tensor(out=R["tmp"], in0=R["a"], scalar=-1.0, in1=bc["k_a"], op0=ALU.add, op1=ALU.mult))
                        step(dve.scalar_tensor_tensor(out=R["k"], in0=R["tmp"], scalar=1.0, in1=R["k"], op0=ALU.add, op1=ALU.mult))
                        step(tt(R["tmp"], R["r"], R["k"], ALU.mult))
                        step(tt(R["tmp"], R["tmp"], bc["r_k"], ALU.mult))
                        step(dve.tensor_reduce(bonus[t % 2], by_head(R["tmp"]), AX, ALU.add))
                    if piece == 2:
                        dve.wait_ge(sem("kk_norm"), t + 1)
                        step(dve.tensor_scalar(small[:, 184:192], small[:, 176:184], 1e-12, None, ALU.max))
                        step(dve.reciprocal(small[:, 184:192], small[:, 184:192]))
                        step(tt(by_head(R["kk"]), by_head(R["kk"]), spread(small[:, 184:192]), ALU.mult))
                        step(tt(R["b"], R["kk"], R["a"], ALU.mult))
                        dve.wait_ge(sem("exp_ready"), 4 * t + 4)
                        dve.scalar_tensor_tensor(out=R[f"al{t % 2}"], in0=R["kk"], scalar=-1.0, in1=R["Eex"], op0=ALU.mult, op1=ALU.mult).then_inc(sem("scaled_ready"), 1)
                        for o, i, e in (("rt", "r", "Ein"), ("bt", "b", "Eni"), ("kt", "k", "Eni"), (f"bh{t % 2}", "b", "Erev"), (f"kh{t % 2}", "k", "Erev")):
                            tt(R[o], R[i], R[e], ALU.mult).then_inc(sem("scaled_ready"), 1)
                        dve.wait_ge(sem("scaled_ready"), 6 * t + 6)

                for piece in range(3):
                    prepare(0, piece)
                for t in range(NT):
                    for i in range(6):
                        dve.wait_ge(sem("pm_full"), 6 * t + i + 1)
                        b = bank["pm_ready", 6 * t + i + 1]
                        par = i % 2
                        if i < 4:
                            mask = pair_mask[:, :, :].rearrange("p a b -> p (a b)")
                            o = F["ab" if i < 2 else "ak"][:, par::2, :]
                            tt(o, b[:, :].rearrange("p (h n) -> p h n", n=P), mask.unsqueeze(1).to_broadcast([P, 4, P]), ALU.mult).then_inc(sem("pm_ready"), 1)
                        else:
                            dve.tensor_copy(by_head(R["A"])[:, par::2, :], b[:, 0:256].rearrange("p (h n) -> p h n", n=HD)).then_inc(sem("pm_ready"), 1)
                    dve.wait_ge(sem("pm_ready"), 6 * t + 6)
                    over_heads = lambda m: m.unsqueeze(1).to_broadcast([P, HEADS, CHUNK])
                    step(tt(by_head(R["X"]), F["ab"][:, :, 0:CHUNK], over_heads(level_one[:, :]), ALU.mult))
                    step(tt(by_head(R["X"]), by_head(R["X"]), over_heads(eye64[:, :]), ALU.add))
                    step(tt(by_head(R["XT"]), by_head(R["A"]), over_heads(level_mask[:, 0, :]), ALU.mult))
                    step(tt(by_head(R["XT"]), by_head(R["XT"]), over_heads(eye64[:, :]), ALU.add))
                    tt(by_head(R["ot0"]), by_head(R["A"]), over_heads(level_mask[:, 1, :]), ALU.mult).then_inc(sem("inv_ready"), 1)
                    for n in range(5):
                        if n < 4:
                            step(tt(by_head(R[f"ot{(n + 1) % 2}"]), by_head(R["A"]), over_heads(level_mask[:, n + 2, :]), ALU.mult))
                        dve.wait_ge(sem("dx_full"), 9 * t + 2 * n + 1)
                        tt(R["X"], R["X"], bank["dx_used", 9 * t + 2 * n + 1][:, :], ALU.add).then_inc(sem("dx_used"), 1)
                        if n < 4:
                            dve.wait_ge(sem("dx_full"), 9 * t + 2 * n + 2)
                            tt(R["XT"], R["XT"], bank["dx_used", 9 * t + 2 * n + 2][:, :], ALU.add).then_inc(sem("dx_used"), 1)
                        dve.wait_ge(sem("dx_used"), 9 * t + (2 * n + 2 if n < 4 else 9))
                        if t + 1 < NT and n < 3:
                            prepare(t + 1, n)
                        if t == NT - 1 and n == 0:
                            rope_angles()
                    if t == NT - 1:
                        latent_norms()
                    for c in range(2):
                        n = 2 * t + c
                        rows = slice(CHUNK * c, CHUNK * (c + 1))
                        dve.wait_ge(sem("end_ready"), t + 1)
                        decays = small[:, 224 + 8 * (t % 2):232 + 8 * (t % 2)].rearrange("p (a b) -> p a b", b=2)[:, :, c:c + 1].to_broadcast([P, 4, HD])
                        dve.wait_ge(sem("state_ready"), n + 1)
                        if n >= 1:
                            dve.wait_ge(sem("yc_full"), n)
                        step(tt(state[(n + 1) % 2], state[n % 2], decays, ALU.mult))
                        dve.wait_ge(sem("z_ready"), 4 * t + 2)
                        for par in range(2):
                            dve.wait_ge(sem("sa_full"), 2 * n + par + 1)
                            tt(by_head(R["SA"])[rows, par::2, :], bank["y_stored", 2 * n + par + 1][rows, 0:256]
                                   .rearrange("p (h n) -> p h n", n=HD), by_head(R["U"])[rows, par::2, :], ALU.add).then_inc(sem("sa_ready"), 1)
                        dve.wait_ge(sem("state_full"), n + 1)
                        tt(state[(n + 1) % 2], state[(n + 1) % 2],
                               bank["state_ready", n + 2][:, 0:256].rearrange("p (a b) -> p a b", b=HD), ALU.add).then_inc(sem("state_ready"), 1)
                        dve.wait_ge(sem("yc_full"), n + 1)
                        dve.wait_ge(sem("y_stored"), 2 * n + 2)
                        tt(R["y"][rows, :], R["y"][rows, :], bank["y_added", n + 1][rows, :], ALU.add).then_inc(sem("y_added"), 1)
                    dve.wait_ge(sem("y_added"), 2 * t + 2)
                    y = by_head(R["y"])
                    step(dve.tensor_reduce(small[:, 200:208], y, AX, ALU.add))
                    step(dve.tensor_scalar(small[:, 200:208], small[:, 200:208], -1.0 / HD, None, ALU.mult))
                    step(tt(y, y, spread(small[:, 200:208]), ALU.add))
                    step(tt(R["tmp"], R["y"], R["y"], ALU.mult))
                    step(dve.tensor_reduce(small[:, 208:216], by_head(R["tmp"]), AX, ALU.add))
                    inv_mean(small[:, 216:224], small[:, 208:216], 1.0 / HD, C_GN_EPS).then_inc(sem("gn_ms"), 1)
                    dve.wait_ge(sem("gn_rstd"), t + 1)
                    step(tt(y, y, spread(small[:, 216:224]), ALU.mult))
                    step(tt(R["y"], R["y"], bc["ln_w"], ALU.mult))
                    step(tt(R["y"], R["y"], bc["ln_b"], ALU.add))
                    step(tt(by_head(R["tmp"]), by_head(R[f"v{t % 2}"]), spread(bonus[t % 2]), ALU.mult))
                    step(tt(R["y"], R["y"], R["tmp"], ALU.add))
                    dve.wait_ge(sem("g_ready"), t + 1)
                    tt(R["y"], R["y"], R[f"g{t % 2}"], ALU.mult).then_inc(sem("yc_ready"), 1)

            if upto >= 5:
                dve.wait_ge(sem("ycT_ready"), total("ycT_ready", NT))
                for t in range(NT):
                    for i, (n, col) in enumerate(((3, 86), (2, 89))):
                        dve.wait_ge(sem("qnT_full"), 2 * t + i + 1)
                        o = (qnT if i == 0 else kvnT)[:, :, P * t:P * (t + 1)]
                        tt(o, bank["qnT_ready", 2 * t + i + 1][:, 0:P * n].rearrange("p (a b) -> p a b", b=P),
                               vc[:, col:col + n].unsqueeze(2).to_broadcast([P, n, P]), ALU.mult).then_inc(sem("qnT_ready"), 1)
                dve.wait_ge(sem("sin_ready"), 2)

                def rope(lo, hi, sin, cos, tmp):
                    step(tt(tmp[0], lo, sin, ALU.mult))
                    step(tt(tmp[1], hi, sin, ALU.mult))
                    step(tt(lo, lo, cos, ALU.mult))
                    step(tt(hi, hi, cos, ALU.mult))
                    step(tt(lo, lo, tmp[1], ALU.subtract))
                    tt(hi, hi, tmp[0], ALU.add).then_inc(sem("rope_ready"), 1)

                sin, cos = rope_cs[:, 0:4, :], rope_cs[:, 4:8, :]
                kr = qkvr[:, :, QKVR - ROPE:]
                rope(kr[:, :, 0:16], kr[:, :, 16:32], sin, cos, [rope_cs[:, 8:12, :], rope_cs[:, 12:16, :]])
                for t in range(NT):
                    dve.wait_ge(sem("ukv_full"), total("ukv_full", HEADS + t + 1))
                    dve.tensor_copy(v_d[:, t, :], bank["v_d_stored", t + 1][:, :]).then_inc(sem("v_d_stored"), 1)
                dve.wait_ge(sem("q_stored"), 8)
                tmp = [region(512 * i, NT, HEADS, 16) for i in range(2)]
                wide = [v.unsqueeze(2).to_broadcast([P, NT, HEADS, 16]) for v in (sin, cos)]
                rope(q_tok[:, :, :, HD:HD + 16], q_tok[:, :, :, HD + 16:], wide[0], wide[1], tmp)
                dve.wait_ge(sem("kpe_full"), total("kpe_full", 1))
                dve.tensor_copy(kT_d[HD:QD, :, :], bank["kpe_ready", 1][HD:QD, :].unsqueeze(1).to_broadcast([ROPE, HEADS, SEQ])).then_inc(sem("kpe_ready"), 1)
                for k in range(4):
                    low_odd(k)
                for c in range(DENSE_SPLIT):
                    low_dense(phase_splits(O_OUT)[0] + c)
                attention(HEADS * NT, 4)
                low_odd(KT - 1)
                out_proj(O_OUT, 24, 16)

            if upto >= 6:
                norm(3)
                L, E2 = NT * N_EXPERTS, [P, NT, N_EXPERTS, N_EXPERTS]
                dve.wait_ge(sem("logit_full"), 1)
                dve.tensor_copy(logit, bank["logit_ready", 1][:, 0:L].rearrange("p (t e) -> p t e", e=N_EXPERTS)).then_inc(sem("logit_ready"), 1)
                dve.wait_ge(sem("logit_ready"), 1)
                step(dve.tensor_reduce(top, logit, AX, ALU.max))
                tt(ex, logit, top.unsqueeze(2).to_broadcast([P, NT, N_EXPERTS]), ALU.subtract).then_inc(sem("top_ready"), 1)
                other, own = logit.unsqueeze(2).to_broadcast(E2), logit.unsqueeze(3).to_broadcast(E2)
                step(tt(same, other, own, ALU.is_equal))
                step(tt(same, same, expert_lt[:, :, :].unsqueeze(1).to_broadcast(E2), ALU.mult))
                step(tt(more, other, own, ALU.is_gt))
                step(tt(more, more, same, ALU.add))
                step(dve.tensor_reduce(rank, more, AX, ALU.add))
                dve.tensor_scalar(sel, rank, TOP_K - 0.5, None, ALU.is_lt).then_inc(sem("sel_ready"), 1)
                dve.wait_ge(sem("sel_ready"), 1)
                dve.wait_ge(sem("ex_ready"), 1)
                step(tt(ex, ex, sel, ALU.mult))
                step(dve.tensor_reduce(top, ex, AX, ALU.add))
                step(dve.reciprocal(top, top))
                step(tt(gate, ex, top.unsqueeze(2).to_broadcast([P, NT, N_EXPERTS]), ALU.mult))
                dve.wait_ge(sem("place_full"), 1)
                b = bank["place_ready", 1]
                step(dve.scalar_tensor_tensor(out=place, in0=b[:, 0:L].rearrange("p (t e) -> p t e", e=N_EXPERTS), scalar=4096.0,
                                              in1=sel, op0=ALU.add, op1=ALU.mult))
                step(dve.tensor_scalar(place, place, -4096.0, None, ALU.add))
                by_round = lambda v: v.rearrange("p (r e) -> p r e", e=N_EXPERTS)
                tt(by_round(key_tmp), b[:, L:L + N_EXPERTS].unsqueeze(1).to_broadcast([P, MAX_ROUNDS, N_EXPERTS]),
                   by_round(cand[:, 1, :]), ALU.subtract).then_inc(sem("place_ready"), 1)
                dve.wait_ge(sem("place_ready"), 1)
                step(dve.tensor_scalar(key, cand[:, 2, :], 1.0 / 64, None, ALU.mult))
                for cap in CAPS[:-1]:
                    step(dve.scalar_tensor_tensor(out=key, in0=key_tmp, scalar=cap + 0.5, in1=key, op0=ALU.is_gt, op1=ALU.add))
                step(dve.tensor_scalar(key_tmp, key_tmp, 0.5, -float(len(CAPS)), ALU.is_gt, ALU.mult))
                step(tt(key, key, key_tmp, ALU.add))
                CC = [P, CANDIDATES, CANDIDATES]
                step(tt(rivals, key.unsqueeze(2).to_broadcast(CC), key.unsqueeze(1).to_broadcast(CC), ALU.is_gt))
                step(dve.tensor_reduce(pos, rivals, AX, ALU.add))
                upto_class = rivals[:, 0:len(CAPS), :]
                for i in range(len(CAPS)):
                    step(dve.tensor_scalar(rivals[:, i, :], key, i - 2.0, None, ALU.is_lt))
                step(dve.tensor_reduce(turn_ends[:, 0:3], upto_class, AX, ALU.add))
                step(dve.tensor_scalar(idle[:, 0:1], turn_ends[:, 0:1], 0.5, None, ALU.is_lt))
                step(tt(idle[:, 1:3], turn_ends[:, 1:3], turn_ends[:, 0:2], ALU.is_equal))
                for i in range(len(CAPS)):
                    step(tt(turn_ends[:, i:3], turn_ends[:, i:3], idle[:, i:i + 1].to_broadcast([P, 3 - i]), ALU.add))
                    if i < 2:
                        step(dve.tensor_scalar(key_tmp, key, i - 2.0, idle[:, i:i + 1], ALU.is_ge, ALU.mult))
                    else:
                        step(dve.tensor_scalar(key_tmp, key, 0.0, 4.0 * CANDIDATES, ALU.is_ge, ALU.mult))
                    step(tt(pos, pos, key_tmp, ALU.add))
                TC = [P, MAX_TURNS + 1, CANDIDATES]
                step(tt(at_turn[0], slot_no[:, 0:MAX_TURNS + 1].unsqueeze(2).to_broadcast(TC), pos.unsqueeze(1).to_broadcast(TC), ALU.is_equal))
                step(tt(at_turn[1], at_turn[0], cand[:, 0, :].unsqueeze(1).to_broadcast(TC), ALU.mult))
                step(dve.tensor_scalar(key_tmp, cand[:, 1, :], -IDLE, None, ALU.add))
                step(tt(at_turn[2], at_turn[0], key_tmp.unsqueeze(1).to_broadcast(TC), ALU.mult))
                step(dve.tensor_reduce(at_turn[0][:, :, 0], at_turn[1], AX, ALU.add))
                dve.tensor_copy(turn_expert_i[:, :], at_turn[0][:, :, 0]).then_inc(sem("w_low_ready"), RAW)
                step(dve.tensor_reduce(turn_off[:, :], at_turn[2], AX, ALU.add))
                dve.tensor_scalar(turn_off[:, :], turn_off[:, :], IDLE, None, ALU.add).then_inc(sem("moe_added"), 8)
                dve.wait_ge(sem("w_low_ready"), total("w_low_ready", RAW))
                dve.wait_ge(sem("moe_added"), 8)
                dve.tensor_copy(turn_ends_i[:, :], turn_ends[:, :]).then_inc(sem("turns_ready"), 1)
                dve.wait_ge(sem("turns_ready"), 1)
                ends = [dve.value_load(turn_ends_i[0:1, i:i + 1], min_val=i + 1, max_val=MAX_TURNS) for i in range(len(CAPS))]

                def place_slots(turn, ahead, cap):
                        e = dve.value_load(turn_expert_i[0:1, bass.ds(turn + ahead, 1)] if ahead else turn_expert_i[0:1, 0:1],
                                           min_val=0, max_val=N_EXPERTS - 1)
                        dve.tensor_scalar(own_place, place[:, :, bass.ds(e, 1)].rearrange("p t a -> p (t a)"),
                                          turn_off[:, bass.ds(turn + ahead, 1)] if ahead else turn_off[:, 0:1], None,
                                          ALU.subtract).then_inc(sem("own_place_ready"), 1)
                        dve.wait_ge(sem("own_place_ready"), turn + (ahead + 1))
                        for t in range(NT):
                            i = dve.tensor_scalar(pick[:, t, 0:cap], slot_no[:, 0:cap], own_place[:, t:t + 1], None, ALU.is_equal)
                        i.then_inc(sem("pick_ready"), 1)
                        dve.wait_ge(sem("pick_ready"), turn + (ahead + 1))

                def gathered(turn, ahead, cap):
                        for i in range(3):
                            n = min(3, KT - 3 * i)
                            dve.wait_ge(sem("xg_full"), turn * 3 + (3 * ahead + i + 1))
                            tt(xgT[:, 3 * i:3 * i + n, 0:cap], turn_banks[1 + i][:, 0:CAP * n].rearrange("p (a b) -> p a b", b=CAP)[:, :, 0:cap],
                                   vc[:, 24 + 3 * i:24 + 3 * i + n].unsqueeze(2).to_broadcast([P, n, cap]), ALU.mult).then_inc(sem("xg_ready"), 1)

                def gates(turn, cap, next_cap):
                        e = dve.value_load(turn_expert_i[0:1, bass.ds(turn, 1)], min_val=0, max_val=N_EXPERTS - 1)
                        for t in range(NT):
                            i = dve.tensor_scalar(pick_g[:, t, 0:cap], slot_no[:, 0:cap], own_place[:, t:t + 1], gate[:, t, bass.ds(e, 1)],
                                                          ALU.is_equal, ALU.mult)
                        i.then_inc(sem("pick_g_ready"), 1)
                        dve.wait_ge(sem("pick_g_ready"), turn + 1)
                        dve.wait_ge(sem("xg_full"), turn * 3 + 3)
                        place_slots(turn, 1, next_cap)

                def xg_parts(turn, ahead):
                        for i in range(3):
                            cols = slice(3 * i, min(3 * i + 3, KT))
                            dve.wait_ge(sem("xg_high_ready"), turn * 3 + total("xg_high_ready", 3 * ahead + i + 1))
                            tt(xg_low[:, cols, :], xgT[:, cols, 0:P], xg_high[:, cols, :].bitcast(F32), ALU.subtract).then_inc(sem("xg_split"), 1)

                def scattered(turn):
                        for i in range(8):
                            t, half = divmod(i, 2)
                            dve.wait_ge(sem("scatter_full"), turn * 8 + i + 1)
                            cols = slice(512 * half, 512 * half + 512)
                            tt(xs[:, t, cols], xs[:, t, cols], turn_banks[i % 4][:, :], ALU.add).then_inc(sem("moe_added"), 1)
                        dve.wait_ge(sem("moe_added"), turn * 8 + 16)

                def low(turn, n):
                        dve.wait_ge(sem("w_high_ready"), turn * TILES_E + total("w_high_ready", n + 1))
                        tt(w_low[n % SPLIT][:, :], raw_slots[n % RAW][:, :], w_high[n % SPLIT][:, :].bitcast(F32), ALU.subtract)\
                            .then_inc(sem("w_low_ready"), 1)

                def expert_split(turn):
                        gates(turn, P, CAPS[1])
                        for n, (kind, j) in enumerate(expert_order()):
                            turned = j - 1 if kind == "g" else j if j == GROUPS_E - 1 and kind == "d" else -1
                            if turned >= 0:
                                dve.wait_ge(sem("hid_high_ready"), turn * GROUPS_E + total("hid_high_ready", turned + 1))
                                tt(hid_low[:, turned % 2, :, :], acc[2 + turned % 2][:, 0:2 * P].rearrange("p (a b) -> p a b", b=P),
                                   hid_high[:, turned % 2, :, :].bitcast(F32), ALU.subtract).then_inc(sem("hid_split"), 1)
                            if kind == "u":
                                dve.wait_ge(sem("up_full"), turn * GROUPS_E + (FF_TILES + j + 1))
                                dve.wait_ge(sem("sil_ready"), turn * GROUPS_E + (FF_TILES + j + 1))
                                if j >= 2:
                                    dve.wait_ge(sem("hidT_full"), turn * GROUPS_E + (j - 1))
                                tt(hid_tok[:, j % 2, :], sil_e[:, j % 2, 0:256], turn_banks[(1 + 2 * j) % 4][:, 0:256], ALU.mult)\
                                    .then_inc(sem("hid_ready"), 1)
                            if n < TILES_E - 1:
                                low(turn, n + SPLIT)
                        gathered(turn, 1, CAPS[1])
                        low(turn, TILES_E - 1 + SPLIT)
                        xg_parts(turn, 1)
                        scattered(turn)

                def expert(turn, cap, next_cap):
                        gates(turn, cap, next_cap)
                        for j in range(GROUPS_E):
                            dve.wait_ge(sem("up_full"), turn * GROUPS_E + (FF_TILES + j + 1))
                            dve.wait_ge(sem("sil_ready"), turn * GROUPS_E + (FF_TILES + j + 1))
                            dve.wait_ge(sem("down_used"), turn * GROUPS_E + (10 + j - 1))
                            tt(pair_of(hid_e[:, j % 2, :], cap), pair_of(sil_e[:, j % 2, :], cap),
                               pair_of(turn_banks[(1 + 2 * j) % 4][:, 0:2 * CAP], cap), ALU.mult).then_inc(sem("hid_ready"), 1)
                        gathered(turn, 1, next_cap)
                        scattered(turn)

                place_slots(0, 0, CAPS[0])
                for n in range(SPLIT):
                    low(0, n)
                gathered(0, 0, CAPS[0])
                xg_parts(0, 0)
                with dve.Fori(0, ends[0]) as turn:
                    expert_split(turn)
                dve.tensor_copy(idle[:, 0:1], idle[:, 1:2]).then_inc(sem("splits_over"), 1)
                with dve.Fori(ends[0], ends[1]) as turn:
                    expert(turn, CAPS[1], CAPS[2])
                with dve.Fori(ends[1], ends[2]) as turn:
                    expert(turn, CAPS[2], CAPS[2])
                dve.tensor_copy(small[:, 7:8], turn_ends[:, 0:1]).then_inc(sem("moe_done"), 1)
                norm(4)
                dve.wait_ge(sem("final_loaded"), 16)
                for t in range(NT):
                    dve.scalar_tensor_tensor(out=y_out[:, t, :], in0=xs[:, t, :], scalar=small[:, 40 + t:41 + t], in1=final_w,
                                                 op0=ALU.mult, op1=ALU.mult).then_inc(sem("y_ready"), 1)


_OUT = (1, SEQ, D)


def kernel(**inputs):
    import numpy as np
    import concourse.bacc as bacc
    from concourse.bass_utils import run_bass_kernel_spmd

    nc = bacc.Bacc("TRN2", target_bir_lowering=False, num_devices=1)
    arrays, args = {}, {}
    for name, value in inputs.items():
        a = np.ascontiguousarray(value)
        arrays[f"in_{name}_dram"] = a
        args[name] = nc.dram_tensor(f"in_{name}_dram", a.shape, mybir.dt.from_np(a.dtype), kind="ExternalInput").ap()
    args["out"] = nc.dram_tensor("out_0_dram", _OUT, F32, kind="ExternalOutput").ap()
    hybrid_trunk(nc, **args)
    r = run_bass_kernel_spmd(nc, [arrays], core_ids=[0])
    return r.results[0]["out_0_dram"]
```
